# Optimizing a Trainium2 kernel written in Bass

```python
import math
import jax, jax.numpy as jnp
from jax import lax
import numpy as np

D_MODEL = 1024
BATCH = 1
SEQ = 256
DEPTH = 1

GRID_W = 64
CTX_LEN = 256
RMS_EPS = 1e-6
SHORT_CONV = 3
D_HYENA = 512
HYENA_ORDER = 2
HYENA_EMB_BANDS = 16
HYENA_EMB_DIM = 1 + 2 * HYENA_EMB_BANDS
HYENA_FILTER_HIDDEN = 64
HYENA_DECAY_TARGET = 1e-2
HYENA_MIN_DECAY = math.log(HYENA_DECAY_TARGET) / 1.5
HYENA_MAX_DECAY = math.log(HYENA_DECAY_TARGET) / 0.3
MLSTM_HEADS = 4
MLSTM_HEAD_DIM = 128
D_MLSTM = MLSTM_HEADS * MLSTM_HEAD_DIM
MLSTM_CHUNK = 128
N_BRANCHES = 2
HY_COLS = (HYENA_ORDER + 1) * D_HYENA
ML_COLS = 4 * D_MLSTM
GATE_COLS = 4 * MLSTM_HEADS
MERGE_COLS = N_BRANCHES * D_MODEL
ML_START = HY_COLS
GATE_START = ML_START + ML_COLS
MERGE_START = GATE_START + GATE_COLS
D_IN_PROJ = MERGE_START + MERGE_COLS
N_EXPERTS = 16
EC_CAPACITY_FACTOR = 2
D_FF_EXPERT = 2 * D_MODEL


def rmsnorm(x, g):
    x32 = x.astype(jnp.float32)
    y = x32 * lax.rsqrt(jnp.mean(x32 * x32, axis=-1, keepdims=True) + RMS_EPS)
    return y.astype(x.dtype) * g

def modulate(h, shift, scale):
    return h * (1.0 + scale[:, None, :]) + shift[:, None, :]

def short_conv(u, w, rows, row_len):
    B, L, C = u.shape
    K = w.shape[0]
    ur = u.reshape(B, rows, row_len, C)
    up = jnp.pad(ur, ((0, 0), (0, 0), (K // 2, K // 2), (0, 0)))
    y = sum(up[:, :, j:j + row_len] * w[j] for j in range(K))
    return y.reshape(B, L, C)

def hyena_filters(L, w1, b1, w2, b2, w3):
    f32 = lambda a: a.astype(jnp.float32)
    t = jnp.linspace(0.0, 1.0, L, dtype=jnp.float32)[:, None]
    bands = jnp.linspace(1e-4, HYENA_EMB_BANDS - 1, HYENA_EMB_BANDS, dtype=jnp.float32)[None, :]
    ang = (2.0 * math.pi / L) * jnp.arange(L, dtype=jnp.float32)[:, None] * bands
    z = jnp.concatenate([t, jnp.cos(ang), jnp.sin(ang)], axis=-1)
    h = jnp.sin(z @ f32(w1) + f32(b1))
    h = jnp.sin(h @ f32(w2) + f32(b2))
    h = (h @ f32(w3)).reshape(L, HYENA_ORDER, 2, D_HYENA)
    deltas = jnp.abs(jnp.linspace(HYENA_MIN_DECAY, HYENA_MAX_DECAY, D_HYENA, dtype=jnp.float32))
    return h * jnp.exp(-t * deltas)[:, None, None, :]

def bidir_long_conv(u, h, skip):
    B, L, C = u.shape
    k = jnp.concatenate([h[:, 0], jnp.zeros((1, C), h.dtype), h[:0:-1, 1]], axis=0)
    U = jnp.fft.rfft(u.astype(jnp.float32), n=2 * L, axis=1)
    Kf = jnp.fft.rfft(k, n=2 * L, axis=0)
    y = jnp.fft.irfft(U * Kf[None], n=2 * L, axis=1)[:, :L]
    return (y + u.astype(jnp.float32) * skip.astype(jnp.float32)).astype(u.dtype)

def hyena_branch(hy_p, conv_w, f_w1, f_b1, f_w2, f_b2, f_w3, skip, rows, row_len):
    L = hy_p.shape[1]
    parts = jnp.split(short_conv(hy_p, conv_w, rows, row_len), HYENA_ORDER + 1, axis=-1)
    filt = hyena_filters(L, f_w1, f_b1, f_w2, f_b2, f_w3)
    z = parts[0]
    for o in range(HYENA_ORDER):
        z = parts[o + 1] * bidir_long_conv(z, filt[:, o], skip[o])
    return z

def mlstm_chunk_scan(q, k, v, log_i, log_f, state0):
    G, H, L, dh = q.shape
    nc = L // MLSTM_CHUNK

    def chunks(a):
        return jnp.moveaxis(a.reshape(G, H, nc, MLSTM_CHUNK, *a.shape[3:]), 2, 0)

    tril = jnp.tril(jnp.ones((MLSTM_CHUNK, MLSTM_CHUNK), dtype=bool))

    def step(carry, inp):
        C, n, m = carry
        qc, kc, vc, li, lf = inp
        b = jnp.cumsum(lf, axis=-1)
        logw = jnp.where(tril, b[..., :, None] - b[..., None, :] + li[..., None, :], -jnp.inf)
        m_inter = b + m[..., None]
        m_t = jnp.maximum(m_inter, logw.max(-1))
        a_intra = jnp.exp(logw - m_t[..., None]) * jnp.einsum('ghtd,ghsd->ghts', qc, kc)
        a_inter = jnp.exp(m_inter - m_t)
        num = jnp.einsum('ghts,ghse->ghte', a_intra, vc) + a_inter[..., None] * jnp.einsum('ghtd,ghde->ghte', qc, C)
        den = a_intra.sum(-1) + a_inter * jnp.einsum('ghtd,ghd->ght', qc, n)
        h = num / jnp.maximum(jnp.abs(den), jnp.exp(-m_t))[..., None]
        b_end = b[..., -1]
        logw_end = b_end[..., None] - b + li
        m_new = jnp.maximum(b_end + m, logw_end.max(-1))
        w_end = jnp.exp(logw_end - m_new[..., None])
        decay = jnp.exp(b_end + m - m_new)
        C_new = decay[..., None, None] * C + jnp.einsum('ghs,ghsd,ghse->ghde', w_end, kc, vc)
        n_new = decay[..., None] * n + jnp.einsum('ghs,ghsd->ghd', w_end, kc)
        return (C_new, n_new, m_new), h

    state, hs = lax.scan(step, state0, (chunks(q), chunks(k), chunks(v), chunks(log_i), chunks(log_f)))
    return jnp.moveaxis(hs, 0, 2).reshape(G, H, L, dh), state

def mlstm_zero_state(batch):
    g = 2 * batch
    return (jnp.zeros((g, MLSTM_HEADS, MLSTM_HEAD_DIM, MLSTM_HEAD_DIM), jnp.float32),
            jnp.zeros((g, MLSTM_HEADS, MLSTM_HEAD_DIM), jnp.float32),
            jnp.zeros((g, MLSTM_HEADS), jnp.float32))

def mlstm_branch(ml_p, gate_p, conv_w, norm_g, rows, row_len, state0):
    B, L, _ = ml_p.shape
    q_pre, k_pre, v, o = jnp.split(ml_p, 4, axis=-1)
    qk = jax.nn.silu(short_conv(jnp.concatenate([q_pre, k_pre], axis=-1), conv_w, rows, row_len))
    q, k = jnp.split(qk, 2, axis=-1)

    def heads(a):
        return a.reshape(B, L, MLSTM_HEADS, MLSTM_HEAD_DIM).transpose(0, 2, 1, 3).astype(jnp.float32)

    q = heads(q) * (MLSTM_HEAD_DIM ** -0.5)
    k = heads(k)
    v = heads(v)
    g = gate_p.astype(jnp.float32).reshape(B, L, 4, MLSTM_HEADS).transpose(2, 0, 3, 1)
    i_f, f_f, i_b, f_b = g[0], g[1], g[2], g[3]
    flip = lambda a: jnp.flip(a, axis=2)
    q2 = jnp.concatenate([q, flip(q)], axis=0)
    k2 = jnp.concatenate([k, flip(k)], axis=0)
    v2 = jnp.concatenate([v, flip(v)], axis=0)
    log_i = jnp.concatenate([i_f, flip(i_b)], axis=0)
    log_f = jax.nn.log_sigmoid(jnp.concatenate([f_f, flip(f_b)], axis=0))
    h2, state = mlstm_chunk_scan(q2, k2, v2, log_i, log_f, state0)
    h = h2[:B] + flip(h2[B:])
    h = h * lax.rsqrt(jnp.mean(h * h, axis=-1, keepdims=True) + RMS_EPS)
    h = h.transpose(0, 2, 1, 3).reshape(B, L, D_MLSTM).astype(ml_p.dtype) * norm_g
    return h * jax.nn.sigmoid(o), state

def token_mixer(h, w_in, b_in, hy_conv, hy_f_w1, hy_f_b1, hy_f_w2, hy_f_b2, hy_f_w3, hy_skip,
                ml_conv, ml_norm_g, w_branch_hy, w_branch_ml, w_out, rows, row_len, state0):
    p = h @ w_in + b_in
    y_a = hyena_branch(p[..., :ML_START], hy_conv, hy_f_w1, hy_f_b1, hy_f_w2, hy_f_b2, hy_f_w3, hy_skip, rows, row_len)
    y_b, state = mlstm_branch(p[..., ML_START:GATE_START], p[..., GATE_START:MERGE_START], ml_conv, ml_norm_g, rows, row_len, state0)
    g_a, g_b = jnp.split(jax.nn.sigmoid(p[..., MERGE_START:]), N_BRANCHES, axis=-1)
    y = (g_a * (y_a @ w_branch_hy) + g_b * (y_b @ w_branch_ml)) @ w_out
    return y, state

def expert_choice_ffn(h, w_router, w1, w3, w2):
    B, N, D = h.shape
    cap = EC_CAPACITY_FACTOR * N // N_EXPERTS
    aff = jax.nn.softmax((h @ w_router).astype(jnp.float32), axis=-1)
    gate, idx = lax.top_k(jnp.swapaxes(aff, 1, 2), cap)
    bidx = jnp.arange(B)[:, None, None]
    xg = h[bidx, idx]
    a = jnp.einsum('becd,edf->becf', xg, w1)
    b = jnp.einsum('becd,edf->becf', xg, w3)
    ye = jnp.einsum('becf,efd->becd', jax.nn.silu(a) * b, w2) * gate[..., None].astype(h.dtype)
    return jnp.zeros_like(h).at[bidx, idx].add(ye)

def first_inputs(seed: int = 0) -> dict:
    key = jax.random.key(seed)
    ks = jax.random.split(key, 32)
    D = D_MODEL
    nrm = lambda k, shape, scale: jax.random.normal(k, shape, jnp.float32) * scale
    forget_offset = np.zeros((D_IN_PROJ,), np.float32)
    forget_offset[GATE_START + MLSTM_HEADS:GATE_START + 2 * MLSTM_HEADS] = np.linspace(3.0, 6.0, MLSTM_HEADS)
    forget_offset[GATE_START + 3 * MLSTM_HEADS:GATE_START + 4 * MLSTM_HEADS] = np.linspace(3.0, 6.0, MLSTM_HEADS)
    return {
        'x': nrm(ks[0], (BATCH, SEQ, D), 1.0),
        'c': nrm(ks[1], (BATCH, D), 1.0),
        'ctx': nrm(ks[2], (BATCH, CTX_LEN, D), 1.0),
        'c_ctx': nrm(ks[3], (D,), 1.0),
        'w_ada': nrm(ks[4], (DEPTH, D, 6 * D), 0.5 * D ** -0.5),
        'b_ada': nrm(ks[5], (DEPTH, 6 * D), 0.02),
        'norm_mix_g': 1.0 + nrm(ks[6], (DEPTH, D), 0.02),
        'norm_ffn_g': 1.0 + nrm(ks[7], (DEPTH, D), 0.02),
        'w_in': nrm(ks[8], (DEPTH, D, D_IN_PROJ), D ** -0.5),
        'b_in': nrm(ks[9], (DEPTH, D_IN_PROJ), 0.02) + jnp.asarray(forget_offset),
        'hy_conv': nrm(ks[10], (DEPTH, SHORT_CONV, HY_COLS), 0.5),
        'hy_f_w1': nrm(ks[11], (DEPTH, HYENA_EMB_DIM, HYENA_FILTER_HIDDEN), HYENA_EMB_DIM ** -0.5),
        'hy_f_b1': nrm(ks[12], (DEPTH, HYENA_FILTER_HIDDEN), 0.1),
        'hy_f_w2': nrm(ks[13], (DEPTH, HYENA_FILTER_HIDDEN, HYENA_FILTER_HIDDEN), HYENA_FILTER_HIDDEN ** -0.5),
        'hy_f_b2': nrm(ks[14], (DEPTH, HYENA_FILTER_HIDDEN), 0.1),
        'hy_f_w3': nrm(ks[15], (DEPTH, HYENA_FILTER_HIDDEN, HYENA_ORDER * 2 * D_HYENA), 0.03 * HYENA_FILTER_HIDDEN ** -0.5),
        'hy_skip': nrm(ks[16], (DEPTH, HYENA_ORDER, D_HYENA), 1.0),
        'ml_conv': nrm(ks[17], (DEPTH, SHORT_CONV, 2 * D_MLSTM), 0.5),
        'ml_norm_g': 1.0 + nrm(ks[18], (DEPTH, D_MLSTM), 0.02),
        'w_branch_hy': nrm(ks[19], (DEPTH, D_HYENA, D), D_HYENA ** -0.5),
        'w_branch_ml': nrm(ks[20], (DEPTH, D_MLSTM, D), D_MLSTM ** -0.5),
        'w_out': nrm(ks[21], (DEPTH, D, D), D ** -0.5),
        'w_router': nrm(ks[22], (DEPTH, D, N_EXPERTS), D ** -0.5),
        'w_exp1': nrm(ks[23], (DEPTH, N_EXPERTS, D, D_FF_EXPERT), D ** -0.5),
        'w_exp3': nrm(ks[24], (DEPTH, N_EXPERTS, D, D_FF_EXPERT), D ** -0.5),
        'w_exp2': nrm(ks[25], (DEPTH, N_EXPERTS, D_FF_EXPERT, D), D_FF_EXPERT ** -0.5),
        'final_norm_g': 1.0 + nrm(ks[26], (D,), 0.02),
    }

def first_block(x, c, ctx, c_ctx, w_ada, b_ada, norm_mix_g, norm_ffn_g, w_in, b_in,
              hy_conv, hy_f_w1, hy_f_b1, hy_f_w2, hy_f_b2, hy_f_w3, hy_skip,
              ml_conv, ml_norm_g, w_branch_hy, w_branch_ml, w_out,
              w_router, w_exp1, w_exp3, w_exp2, final_norm_g):
    B, L, _ = x.shape
    rows = L // GRID_W
    Lc = ctx.shape[1]
    s_lat = jax.nn.silu(c)
    s_ctx = jax.nn.silu(c_ctx)[None, :]
    for l in range(DEPTH):
        last = l == DEPTH - 1
        ada_x = jnp.split(s_lat @ w_ada[l] + b_ada[l], 6, axis=-1)
        ada_c = jnp.split(s_ctx @ w_ada[l] + b_ada[l], 6, axis=-1)
        mix_params = (w_in[l], b_in[l], hy_conv[l], hy_f_w1[l], hy_f_b1[l], hy_f_w2[l], hy_f_b2[l], hy_f_w3[l],
                      hy_skip[l], ml_conv[l], ml_norm_g[l], w_branch_hy[l], w_branch_ml[l], w_out[l])
        hc = modulate(rmsnorm(ctx, norm_mix_g[l]), ada_c[0], ada_c[1])
        if last:
            pc = hc @ w_in[l][:, ML_START:MERGE_START] + b_in[l][ML_START:MERGE_START]
            _, ctx_state = mlstm_branch(pc[..., :ML_COLS], pc[..., ML_COLS:], ml_conv[l], ml_norm_g[l],
                                        1, Lc, mlstm_zero_state(B))
        else:
            yc, ctx_state = token_mixer(hc, *mix_params, 1, Lc, mlstm_zero_state(B))
            ctx = ctx + ada_c[2][:, None, :] * yc
            hc2 = modulate(rmsnorm(ctx, norm_ffn_g[l]), ada_c[3], ada_c[4])
            ctx = ctx + ada_c[5][:, None, :] * expert_choice_ffn(hc2, w_router[l], w_exp1[l], w_exp3[l], w_exp2[l])
        hx = modulate(rmsnorm(x, norm_mix_g[l]), ada_x[0], ada_x[1])
        yx, _ = token_mixer(hx, *mix_params, rows, GRID_W, ctx_state)
        x = x + ada_x[2][:, None, :] * yx
        hx2 = modulate(rmsnorm(x, norm_ffn_g[l]), ada_x[3], ada_x[4])
        x = x + ada_x[5][:, None, :] * expert_choice_ffn(hx2, w_router[l], w_exp1[l], w_exp3[l], w_exp2[l])
    return rmsnorm(x, final_norm_g)


DEPTH_2 = 2

HEAD_DIM = 64
ATTN_GROUPS = ((128, 1), (512, 4), (2048, 16))
N_GROUPS = len(ATTN_GROUPS)
HEADS_PER_GROUP = 6
N_ATTN_HEADS = N_GROUPS * HEADS_PER_GROUP
ATTN_WIDTH = N_ATTN_HEADS * HEAD_DIM
ATTN_OUT_WIDTH = HEADS_PER_GROUP * HEAD_DIM
NUM_BUCKETS = 32
MAX_DISTANCE = 2048
RET_HEADS = 4
RET_QK_DIM = 256
RET_V_DIM = 2 * RET_QK_DIM
RET_QK_WIDTH = RET_HEADS * RET_QK_DIM
RET_V_WIDTH = RET_HEADS * RET_V_DIM
RET_CHUNK = 128
ROPE_BASE = 10000.0
D_FF = -(-8 * D_MODEL // (3 * 256)) * 256
ALPHA = (2 * DEPTH_2) ** 0.25
BETA = (8 * DEPTH_2) ** -0.25
LN_EPS = 1e-5
GN_EPS = 1e-5
SPLIT_SIZES = (ATTN_WIDTH, ATTN_WIDTH, ATTN_WIDTH,
               RET_QK_WIDTH, RET_QK_WIDTH, RET_V_WIDTH, RET_V_WIDTH,
               D_MODEL, D_MODEL)
IN_COLS = sum(SPLIT_SIZES)
SPLIT_POINTS = tuple(int(v) for v in np.cumsum(SPLIT_SIZES)[:-1])


def _t5_bucket(dist):
    max_exact = NUM_BUCKETS // 2
    large = max_exact + (np.log(np.maximum(dist, max_exact) / max_exact)
                         / np.log(MAX_DISTANCE / max_exact)
                         * (NUM_BUCKETS - max_exact)).astype(np.int32)
    large = np.minimum(large, NUM_BUCKETS - 1)
    return np.where(dist < max_exact, dist, large).astype(np.int32)

def _layer_norm(x, g, b):
    xf = x.astype(jnp.float32)
    mu = jnp.mean(xf, axis=-1, keepdims=True)
    var = jnp.mean(jnp.square(xf - mu), axis=-1, keepdims=True)
    return ((xf - mu) * lax.rsqrt(var + LN_EPS) * g + b).astype(x.dtype)

def _dilated_window_attention(q, k, v, bias_table, window, dilation):
    B, S, H, Dh = q.shape
    W = window // dilation
    L = S // dilation
    nb = -(-L // W)
    Lp = nb * W

    def to_sub(t):
        t = t.reshape(B, L, dilation, H, Dh).transpose(0, 2, 3, 1, 4)
        return jnp.pad(t, ((0, 0), (0, 0), (0, 0), (0, Lp - L), (0, 0)))

    def band(t):
        t = jnp.pad(to_sub(t), ((0, 0), (0, 0), (0, 0), (W, 0), (0, 0)))
        prev = t[:, :, :, :Lp].reshape(B, dilation, H, nb, W, Dh)
        cur = t[:, :, :, W:].reshape(B, dilation, H, nb, W, Dh)
        return jnp.concatenate([prev, cur], axis=-2)

    qs = to_sub(q).reshape(B, dilation, H, nb, W, Dh)
    kb, vb = band(k), band(v)

    qi = np.arange(W)[:, None]
    kj = np.arange(2 * W)[None, :]
    rel = qi + W - kj
    in_win = (rel >= 0) & (rel <= W)
    key_idx = np.arange(nb)[:, None, None] * W + kj[None] - W
    mask = in_win[None] & (key_idx >= 0)
    buckets = _t5_bucket(np.clip(rel, 0, W) * dilation)
    bias = jnp.moveaxis(jnp.take(bias_table, buckets, axis=0), -1, 0).astype(jnp.float32)

    s = jnp.einsum('bghnqe,bghnke->bghnqk', qs, kb).astype(jnp.float32) * (Dh ** -0.5)
    s = s + bias[None, None, :, None]
    s = jnp.where(mask[None, None, None], s, -jnp.inf)
    m = jnp.max(s, axis=-1, keepdims=True)
    p = jnp.exp(s - m)
    l = jnp.sum(p, axis=-1, keepdims=True)
    o = jnp.einsum('bghnqk,bghnke->bghnqe', (p / l).astype(v.dtype), vb)
    lse = (m + jnp.log(l))[..., 0]
    o = o.reshape(B, dilation, H, Lp, Dh)[:, :, :, :L].transpose(0, 3, 1, 2, 4).reshape(B, S, H, Dh)
    lse = lse.reshape(B, dilation, H, Lp)[..., :L].transpose(0, 3, 1, 2).reshape(B, S, H)
    return o, lse

def _retention(q, k, v):
    B, S, H, dk = q.shape
    dv = v.shape[-1]
    half = dk // 2
    pos = jnp.arange(S, dtype=jnp.float32)
    inv_freq = ROPE_BASE ** (-jnp.arange(half, dtype=jnp.float32) / half)
    ang = pos[:, None] * inv_freq[None]
    cos = jnp.cos(ang)[None, :, None]
    sin = jnp.sin(ang)[None, :, None]

    def rot(t):
        t1, t2 = t[..., :half], t[..., half:]
        return jnp.concatenate([t1 * cos - t2 * sin, t1 * sin + t2 * cos], axis=-1).astype(t.dtype)

    q = rot(q)
    k = rot(k) * (dk ** -0.5)
    log_g = jnp.log(1.0 - 2.0 ** (-5.0 - jnp.arange(H, dtype=jnp.float32)))
    C = RET_CHUNK
    nC = S // C
    n = jnp.arange(C, dtype=jnp.float32)
    diff = n[:, None] - n[None, :]
    decay_mask = jnp.where(diff >= 0, jnp.exp(log_g[:, None, None] * jnp.maximum(diff, 0.0)), 0.0)
    q_dec = jnp.exp(log_g[:, None] * (n + 1.0))
    k_dec = jnp.exp(log_g[:, None] * (C - 1.0 - n))
    chunk_dec = jnp.exp(log_g * C)

    def chunks(t):
        return t.reshape(B, nC, C, H, t.shape[-1]).transpose(1, 0, 3, 2, 4)

    def step(state, xs):
        qc, kc, vc = xs
        sc = jnp.einsum('bhnd,bhmd->bhnm', qc, kc) * decay_mask
        o = (jnp.einsum('bhnm,bhmv->bhnv', sc, vc)
             + jnp.einsum('bhnd,bhdv->bhnv', qc * q_dec[..., None], state))
        state = (state * chunk_dec[:, None, None]
                 + jnp.einsum('bhmd,bhmv->bhdv', kc * k_dec[..., None], vc))
        return state.astype(jnp.float32), o.astype(jnp.float32)

    state0 = jnp.zeros((B, H, dk, dv), jnp.float32)
    _, ys = lax.scan(step, state0, (chunks(q), chunks(k), chunks(v)))
    o = ys.transpose(1, 0, 3, 2, 4).reshape(B, S, H, dv)
    mu = jnp.mean(o, axis=-1, keepdims=True)
    var = jnp.mean(jnp.square(o - mu), axis=-1, keepdims=True)
    return (o - mu) * lax.rsqrt(var + GN_EPS)

def _hybrid_mixer(x, rel_bias, w_in, b_in, w_attn_proj, w_ret_proj, w_out):
    B, S, _ = x.shape
    z = jnp.einsum('bsd,dc->bsc', x, w_in) + b_in
    q_a, k_a, v_a, q_r, k_r, v_r, g_r, gate_a, gate_b = jnp.split(z, SPLIT_POINTS, axis=-1)
    q_a = q_a.reshape(B, S, N_GROUPS, HEADS_PER_GROUP, HEAD_DIM)
    k_a = k_a.reshape(B, S, N_GROUPS, HEADS_PER_GROUP, HEAD_DIM)
    v_a = v_a.reshape(B, S, N_GROUPS, HEADS_PER_GROUP, HEAD_DIM)
    outs, lses = [], []
    for gi, (window, dilation) in enumerate(ATTN_GROUPS):
        o, lse = _dilated_window_attention(
            q_a[:, :, gi], k_a[:, :, gi], v_a[:, :, gi],
            rel_bias[:, gi * HEADS_PER_GROUP:(gi + 1) * HEADS_PER_GROUP], window, dilation)
        outs.append(o.astype(jnp.float32))
        lses.append(lse)
    wts = jax.nn.softmax(jnp.stack(lses, axis=0), axis=0)
    y_a = jnp.sum(wts[..., None] * jnp.stack(outs, axis=0), axis=0)
    y_a = y_a.astype(x.dtype).reshape(B, S, ATTN_OUT_WIDTH)
    y_r = _retention(q_r.reshape(B, S, RET_HEADS, RET_QK_DIM),
                     k_r.reshape(B, S, RET_HEADS, RET_QK_DIM),
                     v_r.reshape(B, S, RET_HEADS, RET_V_DIM))
    y_b = (jax.nn.silu(g_r) * y_r.reshape(B, S, RET_V_WIDTH)).astype(x.dtype)
    merged = (jax.nn.sigmoid(gate_a) * jnp.einsum('bsc,cd->bsd', y_a, w_attn_proj)
              + jax.nn.sigmoid(gate_b) * jnp.einsum('bsc,cd->bsd', y_b, w_ret_proj))
    return jnp.einsum('bsd,de->bse', merged, w_out)

def _swiglu(x, w_gate, w_up, w_down):
    h = jax.nn.silu(jnp.einsum('bsd,df->bsf', x, w_gate)) * jnp.einsum('bsd,df->bsf', x, w_up)
    return jnp.einsum('bsf,fd->bsd', h, w_down)

def second_inputs(seed: int = 0) -> dict:
    key = jax.random.key(seed)
    ks = jax.random.split(key, 14)
    f32 = jnp.float32

    def nrm(k, shape, scale):
        return jax.random.normal(k, shape, f32) * scale

    return {
        "x": nrm(ks[0], (BATCH, SEQ, D_MODEL), 1.0),
        "rel_bias": nrm(ks[1], (NUM_BUCKETS, N_ATTN_HEADS), 0.2),
        "w_in": nrm(ks[2], (DEPTH_2, D_MODEL, IN_COLS), D_MODEL ** -0.5),
        "b_in": nrm(ks[3], (DEPTH_2, IN_COLS), 0.02),
        "w_attn_proj": nrm(ks[4], (DEPTH_2, ATTN_OUT_WIDTH, D_MODEL), BETA * ATTN_OUT_WIDTH ** -0.5),
        "w_ret_proj": nrm(ks[5], (DEPTH_2, RET_V_WIDTH, D_MODEL), BETA * RET_V_WIDTH ** -0.5),
        "w_out": nrm(ks[6], (DEPTH_2, D_MODEL, D_MODEL), BETA * D_MODEL ** -0.5),
        "ln1_g": 1.0 + nrm(ks[7], (DEPTH_2, D_MODEL), 0.02),
        "ln1_b": nrm(ks[8], (DEPTH_2, D_MODEL), 0.02),
        "w_ffn_gate": nrm(ks[9], (DEPTH_2, D_MODEL, D_FF), D_MODEL ** -0.5),
        "w_ffn_up": nrm(ks[10], (DEPTH_2, D_MODEL, D_FF), D_MODEL ** -0.5),
        "w_ffn_down": nrm(ks[11], (DEPTH_2, D_FF, D_MODEL), BETA * D_FF ** -0.5),
        "ln2_g": 1.0 + nrm(ks[12], (DEPTH_2, D_MODEL), 0.02),
        "ln2_b": nrm(ks[13], (DEPTH_2, D_MODEL), 0.02),
    }

def second_block(x, rel_bias, w_in, b_in, w_attn_proj, w_ret_proj, w_out, ln1_g, ln1_b,
              w_ffn_gate, w_ffn_up, w_ffn_down, ln2_g, ln2_b):
    for l in range(DEPTH_2):
        mix = _hybrid_mixer(x, rel_bias, w_in[l], b_in[l], w_attn_proj[l], w_ret_proj[l], w_out[l])
        x = _layer_norm(ALPHA * x + mix, ln1_g[l], ln1_b[l])
        ffn = _swiglu(x, w_ffn_gate[l], w_ffn_up[l], w_ffn_down[l])
        x = _layer_norm(ALPHA * x + ffn, ln2_g[l], ln2_b[l])
    return x


def setup_inputs(seed=0):
    out = dict(first_inputs(seed))
    for name, value in second_inputs(seed + 1).items():
        if name != "x":
            out[name + "_2"] = value
    return out


def reference(
    x, c, ctx, c_ctx, w_ada, b_ada, norm_mix_g, norm_ffn_g, w_in, b_in, hy_conv, hy_f_w1,
    hy_f_b1, hy_f_w2, hy_f_b2, hy_f_w3, hy_skip, ml_conv, ml_norm_g, w_branch_hy, w_branch_ml,
    w_out, w_router, w_exp1, w_exp3, w_exp2, final_norm_g, rel_bias_2, w_in_2, b_in_2,
    w_attn_proj_2, w_ret_proj_2, w_out_2, ln1_g_2, ln1_b_2, w_ffn_gate_2, w_ffn_up_2,
    w_ffn_down_2, ln2_g_2, ln2_b_2,
):
    x = first_block(
        x, c, ctx, c_ctx, w_ada, b_ada, norm_mix_g, norm_ffn_g, w_in, b_in, hy_conv, hy_f_w1,
        hy_f_b1, hy_f_w2, hy_f_b2, hy_f_w3, hy_skip, ml_conv, ml_norm_g, w_branch_hy,
        w_branch_ml, w_out, w_router, w_exp1, w_exp3, w_exp2, final_norm_g,
    )
    return second_block(
        x, rel_bias_2, w_in_2, b_in_2, w_attn_proj_2, w_ret_proj_2, w_out_2, ln1_g_2, ln1_b_2,
        w_ffn_gate_2, w_ffn_up_2, w_ffn_down_2, ln2_g_2, ln2_b_2,
    )


_drawn_inputs = setup_inputs


def setup_inputs(seed=0):
    import zlib

    import numpy as np

    out = dict(_drawn_inputs(seed))
    spreads = {}
    factors = {'b_ada': 3.164,
     'norm_mix_g': 8.0,
     'norm_ffn_g': 38.953,
     'hy_f_b1': 8.0,
     'hy_f_w2': 2.803,
     'hy_f_b2': 7.081,
     'hy_f_w3': 2.897,
     'ml_norm_g': 64.0,
     'rel_bias_2': 8.0,
     'b_in_2': 8.0,
     'ctx': 8.0,
     'c_ctx': 8.0,
     'b_in': 4.856,
     'ml_conv': 8.0,
     'w_branch_ml': 2.889,
     'final_norm_g': 2.704}
    for name, (base, spread) in spreads.items():
        noise = np.random.default_rng([zlib.crc32(name.encode()), seed]).standard_normal(out[name].shape)
        drawn = base * np.exp(spread * noise) if base else spread * noise
        out[name] = __import__('jax').numpy.asarray(drawn.astype(out[name].dtype))
    for name, factor in factors.items():
        out[name] = (out[name] * factor).astype(out[name].dtype)
    return out
```

```python
from contextlib import ExitStack

import numpy as np

import concourse.bass as bass
from concourse import mybir

F32 = mybir.dt.float32
ACT = mybir.ActivationFunctionType
ALU = mybir.AluOpType
AX = mybir.AxisListType

P = 128
T = 256
D = 1024
KD = D // P
DEPTH_2 = 2
RING = 4
SLOT = 4096
HALF = SLOT // 2

HY, HYC = 1536, 512
HEADS, DH = 4, 128
ML0, GATE0, MERGE0, IN1 = 1536, 3584, 3600, 5648
EXPERTS, CAP, FF = 16, 32, 2048
NFFT = 511
EPS = 1e-6
BIG = 1e4

AH, AD, NG = 18, 64, 3
HPG = AH // NG
IN2 = 11648
QK_A, V_A, QK_R, V_R, G_R, GATE_2 = 0, 2304, 3456, 5504, 7552, 9600
RH = 4
DFF = 2816
NF = DFF // P
ALPHA = (2 * DEPTH_2) ** 0.25
LN_EPS = 1e-5
NEG = -1e30

C_ADA, C_NMIX, C_NFFN, C_BIN, C_BMERGE = 0, 48, 56, 64, 92
D_HYC, D_MLC, D_MLG, D_C, D_CC, D_HSKIP = 0, 36, 60, 64, 72, 80
E_QKA, E_QKR, E_GG = 0, 18, 34


class Units:

    def __init__(self):
        self.first, self.engine, self.count, self.per = {}, [], [], {"A": 0, "V": 0}

    def add(self, name, n, engines="V"):
        self.first[name] = len(self.engine)
        for i in range(n):
            e = engines[i % len(engines)]
            self.per[e] += 1
            self.engine.append(e)
            self.count.append(self.per[e])

    def at(self, name, i=0):
        return self.first[name] + i


def layer_units(units, l):
    units.add(f"xT{l}", 4, "AV")
    units.add(f"qka{l}", 9, "A")
    units.add(f"va{l}", 6, "V")
    for j in range(HPG):
        units.add(f"score{l}.{j}", 3, "V")
        if j < 4:
            units.add(f"qkr_v{l}.{j}", 4, "A" if j < 2 else "V")
        units.add(f"pT{l}.{j}", 3, "A")
        units.add(f"attn{l}.{j}", 1, "V")
    units.add(f"yaT{l}", 2, "V")
    for h in range(RH):
        units.add(f"rs{l}.{h}", 1, "V")
        units.add(f"ro{l}.{h}", 2, "A")
    units.add(f"gate{l}", 8, "A")
    for c in range(8):
        units.add(f"gr{l}.{c}", 1, "A")
        units.add(f"yrT{l}.{c}", 1, "V")
    units.add(f"mixA{l}", 4, "V")
    units.add(f"mixB{l}", 4, "V")
    units.add(f"mixo{l}", 4, "V")
    units.add(f"x2T{l}", 4, "AV")
    for c in range(NF // 2):
        units.add(f"ffg{l}.{c}", 1, "A")
        units.add(f"ffu{l}.{c}", 1, "V")
    units.add(f"down{l}", 4, "V")


def plan_units():
    u = Units()
    u.add("packs", 2)
    u.add("reltab", 1)
    u.add("sin1", 1)
    u.add("sin2", 1)
    u.add("filt", 8)
    u.add("filtK", 8, "AV")
    u.add("ada", 12, "AV")
    u.add("adacol", 1)
    u.add("hx", 4, "AV")
    u.add("hc", 4, "AV")
    u.add("kx", 2, "A")
    u.add("kc", 2, "A")
    u.add("vx", 2)
    u.add("vc", 2)
    u.add("mgate", 1)
    u.add("q", 2, "A")
    u.add("crow", 2)
    u.add("xrow", 2)
    u.add("hy0", 2, "A")
    u.add("wcol", 1)
    u.add("hy1", 2, "A")
    u.add("kcn", 2)
    u.add("hy2", 2, "A")
    u.add("state", 4, "A")
    u.add("o", 2, "A")
    u.add("cols", 1)
    for h in range(HEADS):
        u.add(f"mb{h}", 1)
        u.add(f"sT{h}", 1)
        for t in range(2):
            u.add(f"inter{h}.{t}", 1, "A")
            u.add(f"num{h}.{t}", 1)
    u.add("mergeA", 4, "A")
    u.add("hT", 2)
    for o in range(2):
        u.add(f"uT{o}", 2, "AV")
        u.add(f"uf{o}", 4)
        u.add(f"merge{o}", 2, "A")
        u.add(f"yo{o}", 2)
    u.add("bc2", 2, "AV")
    for c in range(4):
        u.add(f"bra{c}", 2)
    u.add("out1", 4)
    u.add("h2T", 4, "AV")
    u.add("route", 1)
    u.add("affT", 1)
    u.add("affbc", 8)
    u.add("gather", 8, "AV")
    u.add("bc5", 2, "AV")
    for l in range(DEPTH_2):
        layer_units(u, l)
    return u


def kernel_program(nc, a, k, out):
    U = plan_units()

    with ExitStack() as ctx:
        def sb(name, cols, rows=P):
            return ctx.enter_context(nc.sbuf_tensor(name + "_sb", [rows, cols], F32))

        def sem(name):
            return ctx.enter_context(nc.semaphore(name))

        bank = [ctx.enter_context(nc.psum_tensor(f"bank{i}", [P, 512], F32)) for i in range(8)]
        ring = sb("ring", RING * SLOT)
        x = sb("x", 2 * D)
        hT = sb("hT", KD * T)
        ident = sb("ident", P)
        colA = sb("colA", P)
        colB = sb("colB", P)
        colC = sb("colC", 2 * P)
        sm = sb("sm", 640)
        arena = sb("arena", 29800)
        rel_table = nc.dram_tensor("rel_table", (AH, P, 384), F32, kind="Internal").ap()

        def region(off, *dims):
            n = int(np.prod(dims))
            v = arena[:, off:off + n]
            if len(dims) == 2:
                return v.rearrange("p (a b) -> p a b", a=dims[0])
            if len(dims) == 3:
                return v.rearrange("p (a b c) -> p a b c", a=dims[0], b=dims[1])
            if len(dims) == 4:
                return v.rearrange("p (a b c d) -> p a b c d", a=dims[0], b=dims[1], c=dims[2])
            return v

        x3 = x[:].rearrange("p (t d) -> p t d", t=2)
        hT3 = hT[:].rearrange("p (k t) -> p k t", k=KD)
        ones = sb("ones", P)

        filtK = region(0, 2, 2, 2, 512)
        filt = region(4096, 2, 2, 2, 512)
        gates = region(4096, 16, T)
        adarow = region(4096, 12, 512)
        zhy = region(8192, 12, T)
        win = region(10240, 2, 2, 512)
        w3 = region(17424, 2048)
        qT = region(11264, 4, T)
        kT = region(12288, 4, T)
        NUM = region(13312, 2, 4, 2, 129)
        ctxn = region(13312, 2, D)
        xn = region(15376, 2, D)
        W = region(15376, 2, 4, T)
        hcT = region(17424, KD, T)
        kw = region(17424, 2, 2, 512)
        Y = region(17424, 2, 2, 512)
        vx = region(19472, 2, 4, 129)
        vc = region(20504, 2, 4, 129)
        unat = region(20504, 2, 512)
        CA = region(21536, 4, 2, 129)
        oT = region(22568, 4, T)
        tri = region(23592, 2, 2, T)
        dft = region(24616, 2, 2, T)
        praw = region(25640, 4, 2, T)
        emb = region(25640, T)
        w1s = region(25896, 64)
        w2s = region(25960, 64)
        sv = region(26024, 4, T)
        sTad = region(27688, 8, 32)
        YB = region(27688, 4, T)
        kcT = region(28712, 4, T)
        Utmp = region(25640, 4, 512)
        merged = region(0, 8, T)
        bc2 = region(2048, D)
        bctmp = region(3072, D)
        hm = region(25640, 8, P)
        hsq = region(26664, 8, P)
        tmpB = region(28712, 2, 2, 129)
        mtmp = region(17424, 3, 512)
        diag = region(20504, 8, P)

        xn2 = region(4096, 2, D)
        sel = region(6144, 2, 512)
        sel16 = arena[0:16, 13312:15360]
        ltmask = region(15376, 2, T)
        iota = region(15888, 32)
        w_router = region(15920, KD, 16)
        fnorm = region(16048, D)
        xgT = region(17424, KD, 512)
        acc = region(21552, 2, D)
        sgs = region(23616, 2, P)
        sgT = region(23872, T)
        xg = region(24128, KD, CAP)
        sact = region(24616, 512)
        hact = region(25128, 512)
        hTs = region(25640, 4, P)
        ysb = region(26152, T)
        affn = region(26408, 2, 16)
        rank = region(26440, 2, 2, 16)
        affT = arena[0:16, 26504:26760]
        diag5 = region(26760, 8, P)
        bc5 = region(27784, D)
        rjunk = region(28812, 3, T)

        qka = region(0, 18, T)
        va = region(4608, 2, AH * AD)
        relB = region(6912, AH, T)
        qkr = region(11520, 16, T)
        vr = region(15616, 2, 2048)
        sc = region(19712, 9, P)
        vbias_a = region(19712, AH * AD)
        rraw = region(20864, 2, T)
        rm1 = region(21376, 2, T)
        pT = region(22016, 9, P)
        ya = region(23168, 2, 384)
        yaT = region(23936, 3, T)
        decay = region(24704, RH, 384)
        rope = region(26240, 2, T)
        vbias_r = region(26752, 2048)
        rm2 = region(28800, 2, T)
        yr = region(0, 2, 2048)
        ybT = region(4608, 16, T)
        merged2 = region(8704, 8, T)
        ln1 = region(11520, 2, D)
        ln2 = region(13568, 2, D)
        gates2 = region(15616, 16, T)
        pr = region(19712, 2, 384)
        gtmp = region(20864, 2, 512)
        btmp = region(22016, 2, 512)
        hF = region(0, NF, T)

        relbuf = hT[0:AH, 0:384]
        distmask = arena[0:AH, 21536:21920]
        onehot = arena[0:32, 21920:22304]
        rel_bias = arena[0:32, 22304:22322]
        skipb = arena[0:1, 22336:23360]
        adacol = sb("adacol", 96)
        adaT = adacol[:].rearrange("p (j s) -> p j s", s=2)
        gcol = sb("gcol", 32)
        rows = arena[0:4, 4096:4096 + 3136]
        gl = sb("gl", 64 + 32 + 32)
        cst = sb("cst", 8)
        mcols = sb("mcols", 48 + 16)
        w_gate = sb("w_gate", KD * 16)
        b_rows = sb("b_rows", 512 + 16)
        dftw = sb("dftw", 2)
        selsum = sb("selsum", 2)
        sel4 = sb("sel4", 512, 4)
        fb = sb("fb", 2, 64)

        def rw(i):
            return rows[0:4, i * 512:(i + 1) * 512]

        rsm = rows[0:4, 3072:3136]
        G4 = gl[:, 0:64].rearrange("p (s k h) -> p s k h", s=4, k=4)
        nlf = gl[:, 64:96].rearrange("p (s d h) -> p s d h", s=4, d=2)
        wk = gl[:, 96:128].rearrange("p (s d h) -> p s d h", s=4, d=2)

        def spread_row(ap, off, n):
            return bass.AP(ap.tensor, off, [[0, P], [1, n]])

        early = [
            (x3, a["x"][0].rearrange("(t p) d -> p t d", p=P)),
            (ident[:], k["ident"]), (dft.rearrange("p a b c -> p (a b c)"), k["dft"]),
            (emb[0:33], k["emb"]), (w1s[0:33], a["hy_f_w1"][0]), (w2s[0:64], a["hy_f_w2"][0]),
            (w3[0:64], a["hy_f_w3"][0]),
            (fb[:, 0:1], a["hy_f_b1"].rearrange("a b -> b a")), (fb[:, 1:2], a["hy_f_b2"].rearrange("a b -> b a")),
            (win.rearrange("p a b c -> p (a b c)"), k["win"]), (dftw[:], k["dftw"]),
            (distmask, k["distmask"]), (onehot, k["onehot"]), (rel_bias, a["rel_bias_2"]),
            (skipb, a["hy_skip"].rearrange("a o c -> a (o c)")), (selsum[:], k["selsum"]),
            (ctxn, a["ctx"][0].rearrange("(t p) d -> p t d", p=P)),
            (tri.rearrange("p a b c -> p (a b c)"), k["tri"]), (sel4[:], k["sel4"]),
            (w_gate[:].rearrange("p (k c) -> p k c", k=KD),
             a["w_in"][0].rearrange("(k p) c -> p k c", p=P)[:, :, GATE0:MERGE0]),
            (b_rows[:, 0:512], spread_row(a["b_in"], ML0 + 1024, 512)),
            (b_rows[:, 512:528], spread_row(a["b_in"], GATE0, 16)),
        ]

        names = """packs_landed const_landed cst_set x_norm ctx_norm filt_sum sin_arg1 sin_arg2 sin1_ready sin2_ready
            silu_c cols_ready conv_done qk_ready lf_ready m_ready softplus_arg softplus_l w_row_arg
            w_row inter_arg inter_rows w_arg w_exp hm_ready y_spec merged_ready bc_diag dve_step
            act_step var_ready sqrt_ready unit_done freed_act freed_dve rel_saved rel_ready moe_landed
            xn2_ready x1_ready aff_ready rank_ready sel_ready slots_used xg_copied sg_copied hact a_read
            hT_evac sgT_evac y_evac scat_done acc_done lay_landed ln_landed out_saved y_ready exp_done
            x_done rot_done yr_ready sc_ready soft_arg sg_turned hT_turned aff_exp""".split()
        s = {n: sem(n) for n in names}
        landed = [sem(f"slot{i}_landed") for i in range(RING)]

        def w_cols(w, c0, width):
            v = w.rearrange("(k p) c -> p k c", p=P)[:, :, c0:c0 + width]
            h = v.shape[1] // 2
            return [((0, h * width), v[:, 0:h]), ((h * width, (v.shape[1] - h) * width), v[:, h:])]

        def w_rows(w, r0, nk):
            v = w[r0:r0 + nk * P].rearrange("(k p) c -> p k c", p=P)
            h = (nk + 1) // 2
            return [((0, h * D), v[:, 0:h]), ((h * D, (nk - h) * D), v[:, h:])]

        w_in, w_ada = a["w_in"][0], a["w_ada"][0]
        slots = []
        for i in range(12):
            slots.append((w_cols(w_ada, 512 * i, 512), U.at("ada", i)))
        for c0, last in ((ML0 + 512, U.at("kc", 1)), (ML0 + 1024, U.at("vc", 1)), (ML0, U.at("q", 1)),
                         (0, U.at("hy0", 1)), (512, U.at("hy1", 1)), (1024, U.at("hy2", 1)),
                         (ML0 + 1536, U.at("o", 1)),
                         (MERGE0, U.at("mergeA", 1)), (MERGE0 + 512, U.at("mergeA", 3)),
                         (MERGE0 + 1024, U.at("merge0", 1)), (MERGE0 + 1536, U.at("merge1", 1))):
            slots.append((w_cols(w_in, c0, 512), last))
        slots.append((w_rows(a["w_branch_hy"][0], 0, 4), U.at("bra3", 1)))
        slots.append((w_rows(a["w_branch_ml"][0], 0, 4), U.at("bra3", 1)))
        slots.append((w_cols(a["w_out"][0], 0, 512), U.at("out1", 1)))
        slots.append((w_cols(a["w_out"][0], 512, 512), U.at("out1", 3)))
        N_PRE = len(slots)
        S_KC, S_V, S_Q, S_HY, S_O, S_MERGE, S_BR, S_OUT = 12, 13, 14, 15, 18, 19, 23, 25
        E1 = a["w_exp1"][0].rearrange("e (k p) f -> e p k f", p=P)
        E3 = a["w_exp3"][0].rearrange("e (k p) f -> e p k f", p=P)
        E2 = a["w_exp2"][0].rearrange("e (k p) f -> e p k f", p=P)
        PER_EXPERT = 12
        N_POST = N_PRE + PER_EXPERT * EXPERTS
        post = []
        for l in range(DEPTH_2):
            w2 = a["w_in_2"][l]
            for i in range(5):
                post.append((w_cols(w2, QK_A + 512 * i, 512 if i < 4 else 256), U.at(f"qka{l}", min(2 * i + 1, 8))))
            for i in range(3):
                post.append((w_cols(w2, V_A + 512 * i, 512 if i < 2 else 128), U.at(f"va{l}", 2 * i + 1)))
            for i in range(8):
                j, r = divmod(i, 2)
                c0 = QK_R + 512 * i
                post.append((w_cols(w2, c0, 512), U.at(f"qkr_v{l}.{j}", 2 * r + 1)))
            for i in range(4):
                post.append((w_cols(w2, GATE_2 + 512 * i, 512), U.at(f"gate{l}", 2 * i + 1)))
            for i in range(4):
                post.append((w_cols(w2, G_R + 512 * i, 512), U.at(f"gr{l}.{2 * i + 1}")))
            wap = a["w_attn_proj_2"][l].rearrange("(k p) c -> p k c", p=P)
            post.append(([((0, 2048), wap[:, 0:2]), ((2048, 1024), wap[:, 2:3])], U.at(f"mixA{l}", 3)))
            for i in range(4):
                post.append((w_cols(a["w_ret_proj_2"][l], 256 * i, 256), U.at(f"mixB{l}", i)))
            for i in range(2):
                post.append((w_cols(a["w_out_2"][l], 512 * i, 512), U.at(f"mixo{l}", 2 * i + 1)))
            for i in range(NF // 2):
                g = a["w_ffn_gate_2"][l].rearrange("(k p) c -> p k c", p=P)[:, :, 256 * i:256 * i + 256]
                u = a["w_ffn_up_2"][l].rearrange("(k p) c -> p k c", p=P)[:, :, 256 * i:256 * i + 256]
                post.append(([((0, 2048), g), ((2048, 2048), u)], U.at(f"ffu{l}.{i}")))
            for i in range(6):
                post.append((w_rows(a["w_ffn_down_2"][l], 512 * i, 4 if i < 5 else 2),
                             ("down", l, i) if i < 5 else U.at(f"down{l}", 3)))
        PER_LAYER = len(post) // DEPTH_2
        O_QKA, O_VA, O_QKR, O_GATE, O_GR, O_ATTN, O_RET, O_OUT, O_FF, O_DOWN = 0, 5, 8, 16, 20, 24, 25, 29, 31, 42

        def slot(n, *dims):
            o = (n % RING) * SLOT
            v = ring[:, o:o + int(np.prod(dims))]
            return v.rearrange("p (k c) -> p k c", k=dims[0])

        def arrived(eng, n):
            eng.wait_ge(landed[n % RING], 32 * (n // RING + 1))

        freed = {"A": s["freed_act"], "V": s["freed_dve"]}

        def wait_emptied(eng, name, n=None):
            last = {}
            i0 = U.first[name]
            total = n
            if total is None:
                later = [f for f in U.first.values() if f > i0]
                total = (min(later) if later else len(U.engine)) - i0
            for u in range(i0, i0 + total):
                last[U.engine[u]] = U.count[u]
            for e, v in last.items():
                eng.wait_ge(freed[e], v)

        block = ctx.enter_context(nc.Block())

        @block.sync
        def _(sp):
            def load(n, parts):
                for (off, size), src in parts:
                    o = (n % RING) * SLOT + off
                    dst = ring[:, o:o + size]
                    if len(src.shape) == 3:
                        dst = dst.rearrange("p (k c) -> p k c", k=src.shape[1])
                    sp.dma_start(dst, src).then_inc(landed[n % RING], 16)

            for n, (parts, last) in enumerate(slots):
                if n >= RING:
                    sp.wait_ge(s["unit_done"], slots[n - RING][1] + 1)
                load(n, parts)

            def expert_load(kslot, e, c):
                w, r = ((E1, c), (E3, c - 4), (E2, c - 8))[c // 4]
                n = 2 if c < 8 else 4
                src = w[e, :, n * r:n * r + n]
                o = (kslot % RING) * SLOT
                for h in range(2):
                    m = n // 2
                    dst = ring[:, o + h * HALF:o + (h + 1) * HALF].rearrange("p (k c) -> p k c", k=m)
                    sp.dma_start(dst, src[:, h * m:(h + 1) * m]).then_inc(landed[kslot % RING], 16)

            for c in range(4):
                sp.wait_ge(s["unit_done"], slots[N_PRE - RING + c][1] + 1)
                expert_load(N_PRE + c, 0, c)
            with sp.Fori(0, EXPERTS - 1) as e:
                for c in range(4, 16):
                    sp.wait_ge(s["slots_used"], e * PER_EXPERT + (c - 3))
                    expert_load(N_PRE + c, e + (c // 12), c % 12)
            for c in range(4, 12):
                sp.wait_ge(s["slots_used"], (EXPERTS - 1) * PER_EXPERT + c - 3)
                expert_load(N_PRE + c, EXPERTS - 1, c)
            for i, (parts, last) in enumerate(post):
                if i < RING:
                    sp.wait_ge(s["slots_used"], EXPERTS * PER_EXPERT - RING + 1 + i)
                else:
                    prev = post[i - RING][1]
                    if isinstance(prev, tuple):
                        _, l, j = prev
                        sp.wait_ge(s["slots_used"], EXPERTS * PER_EXPERT + 5 * l + j + 1)
                    else:
                        sp.wait_ge(s["unit_done"], prev + 1)
                load(N_POST + i, parts)
            for tile in range(2):
                sp.wait_ge(s["y_ready"], tile + 1)
                sp.dma_start(out[0, tile * P:(tile + 1) * P], x3[:, tile]).then_inc(s["out_saved"], 16)
            sp.wait_ge(s["out_saved"], 32)
            sp.wait_ge(s["rel_saved"], 16)

        @block.gpsimd
        def _(pool):
            g = nc.gpsimd
            colsrc = [(colA, [(C_ADA, a["b_ada"][0], 48), (C_NMIX, a["norm_mix_g"][0], 8),
                              (C_NFFN, a["norm_ffn_g"][0], 8), (C_BIN, a["b_in"][0][0:3584], 28),
                              (C_BMERGE, a["b_in"][0][MERGE0:IN1], 16)]),
                      (colB, [(D_HYC, a["hy_conv"][0].rearrange("k c -> (k c)"), 36),
                              (D_MLC, a["ml_conv"][0].rearrange("k c -> (k c)"), 24),
                              (D_MLG, a["ml_norm_g"][0], 4), (D_C, a["c"][0], 8), (D_CC, a["c_ctx"], 8)])]
            g.memset(colA[:], 0.0)
            g.memset(colB[:], 0.0)
            g.memset(colC[:], 0.0)
            g.memset(ones[:], 1.0)
            g.memset(cst[:, 0:1], EPS)
            g.memset(cst[:, 1:2], 1.0)
            g.memset(cst[:, 2:3], 0.0)
            g.memset(sTad, 0.0)
            g.memset(vx[:, :, :, 128:129], 1.0)
            g.memset(vc[:, :, :, 128:129], 1.0).then_inc(s["cst_set"], 1)
            pool.wait_ge(s["cst_set"], 1)
            n = 0
            for dst, parts in colsrc:
                for r0, src, nr in parts:
                    g.dma_start(dst[r0:r0 + nr, :], src.rearrange("(r c) -> r c", c=P)).then_inc(s["packs_landed"], 16)
                    n += 1
            for l in range(DEPTH_2):
                b2 = a["b_in_2"][l]
                for r0, c0, nr in ((E_QKA, QK_A, 18), (E_QKR, QK_R, 16), (E_GG, G_R, 32)):
                    g.dma_start(colC[r0:r0 + nr, l * P:(l + 1) * P],
                                b2[c0:c0 + nr * P].rearrange("(r c) -> r c", c=P)).then_inc(s["packs_landed"], 16)
                    n += 1
            pool.wait_ge(s["rel_ready"], 1)
            g.dma_start(rel_table, relbuf.unsqueeze(1).broadcast_to([AH, P, 384])).then_inc(s["rel_saved"], 16)
            pool.wait_ge(s["unit_done"], U.at("hT", 1) + 1)
            for dst, src in ((sel16, k["sel16"]), (ltmask.rearrange("p t s -> p (t s)"), k["ltmask"]), (iota, k["iota"]),
                             (w_router, a["w_router"][0].rearrange("(k p) c -> p k c", p=P)),
                             (fnorm, spread_row(a["final_norm_g"], 0, D))):
                g.dma_start(dst, src).then_inc(s["moe_landed"], 16)
            for l in range(DEPTH_2):
                if l == 0:
                    pool.wait_ge(s["x1_ready"], 1)
                    pool.wait_ge(s["rel_saved"], 16)
                    loads = [(decay.rearrange("p h t -> p (h t)"), k["decay"]), (rope.rearrange("p c t -> p (c t)"), k["rope"])]
                else:
                    pool.wait_ge(s["unit_done"], U.at(f"mixo{l - 1}", 3) + 1)
                    loads = []
                loads += [(vbias_a, spread_row(a["b_in_2"], l * IN2 + V_A, AH * AD)),
                          (relB, bass.AP(rel_table.tensor, 127, [[383, P], [P * 384, AH], [1, T]])),
                          (vbias_r, spread_row(a["b_in_2"], l * IN2 + V_R, 2048))]
                for dst, src in loads:
                    g.dma_start(dst, src).then_inc(s["lay_landed"], 16)
                pool.wait_ge(s["unit_done"], U.at(f"rs{l}.3") + 1)
                for dst, w in ((ln1[:, 0], "ln1_g_2"), (ln1[:, 1], "ln1_b_2"), (ln2[:, 0], "ln2_g_2"), (ln2[:, 1], "ln2_b_2")):
                    g.dma_start(dst, spread_row(a[w], l * D, D)).then_inc(s["ln_landed"], 16)

        @block.scalar
        def _(act):
            A = nc.scalar
            chain = [0]

            def link(ins):
                chain[0] += 1
                ins.then_inc(s["act_step"], 1)
                act.wait_ge(s["act_step"], chain[0])

            def take(name, i=0):
                u = U.at(name, i)
                assert U.engine[u] == "A", name
                act.wait_ge(s["unit_done"], u + 1)
                return bank[u % 8]

            def give(ins):
                ins.then_inc(s["freed_act"], 1)

            def root(k, dst, src):
                act.wait_ge(s["var_ready"], k)
                A.activation(dst, src, ACT.Sqrt).then_inc(s["sqrt_ready"], 1)

            for dst, src in early:
                act.dma_start(dst, src).then_inc(s["const_landed"], 16)

            act.wait_ge(s["const_landed"], 16 * len(early))
            act.wait_ge(s["cst_set"], 1)
            act.wait_ge(s["sin_arg1"], 1)
            A.activation(sv[0:64, 1], sv[0:64, 0], ACT.Sin).then_inc(s["sin1_ready"], 1)
            act.wait_ge(s["sin_arg2"], 1)
            A.activation(sv[0:64, 3], sv[0:64, 2], ACT.Sin).then_inc(s["sin2_ready"], 1)
            for i in range(8):
                if U.engine[U.at("filtK", i)] == "A":
                    b = take("filtK", i)
                    o, f, q = i // 4, (i // 2) % 2, i % 2
                    give(A.activation(filtK[:, o, q, f], b[:], ACT.Identity, scale=dftw[:, f:f + 1]))
            act.wait_ge(s["cols_ready"], 1)
            A.activation(sTad[:, :, 0], colB[:, D_C:D_C + 8], ACT.Silu)
            A.activation(sTad[:, :, 1], colB[:, D_CC:D_CC + 8], ACT.Silu).then_inc(s["silu_c"], 1)
            for i in range(12):
                if U.engine[U.at("ada", i)] == "A":
                    give(A.copy(adarow[:, i], take("ada", i)[:]))
            root(1, sm[:, 8:12], sm[:, 4:8])

            def modulate(name, dst3, g0, src, sh0=0):
                act.wait_ge(s["m_ready"], 1)
                for i in range(4):
                    if U.engine[U.at(name, i)] == "A":
                        b = take(name, i)
                        for j in range(2):
                            d = 2 * i + j
                            ins = A.activation(dst3[:, d], b[:, j * T:(j + 1) * T], ACT.Identity,
                                               scale=gcol[:, g0 + d:g0 + d + 1], bias=adaT[:, sh0 + d, src:src + 1])
                        give(ins)
            act.wait_ge(s["rel_saved"], 16)
            modulate("hx", hT3, 0, 0)
            modulate("hc", hcT, 8, 1)

            def raw(name, n, tile0, k):
                for i in range(n):
                    b = take(name, i)
                    if k + i >= 4:
                        act.wait_ge(s["conv_done"], k + i - 3)
                    for j in range(2):
                        c = C_BIN + tile0 + 2 * i + j
                        ins = A.activation(praw[:, (k + i) % 4, j], b[:, j * T:(j + 1) * T], ACT.Identity,
                                           bias=colA[:, c:c + 1])
                    ins.then_inc(s["freed_act"], 1)

            def silu_conv(k, dst):
                act.wait_ge(s["conv_done"], k + 1)
                A.activation(dst, dst, ACT.Silu).then_inc(s["qk_ready"], 1)

            raw("kx", 2, 16, 0)
            raw("kc", 2, 16, 2)
            silu_conv(0, kT[:, 0:2])
            silu_conv(1, kT[:, 2:4])
            silu_conv(2, kcT[:, 0:2])
            silu_conv(3, kcT[:, 2:4])
            raw("q", 2, 12, 4)
            silu_conv(4, qT[:, 0:2])
            silu_conv(5, qT[:, 2:4])
            act.wait_ge(s["softplus_arg"], 1)
            link(A.activation(gl[:, 96:128], gl[:, 96:128], ACT.Exp, scale=-1.0))
            A.activation(gl[:, 96:128], gl[:, 96:128], ACT.Ln, bias=cst[:, 1:2]).then_inc(s["softplus_l"], 1)
            act.wait_ge(s["w_row_arg"], 1)
            for d in range(2):
                ins = A.activation(rw(5)[:, d * T:(d + 1) * T], rw(1)[:, d * T:(d + 1) * T], ACT.Exp,
                                   bias=rsm[:, 2 + d:3 + d])
            ins.then_inc(s["w_row"], 1)
            raw("hy0", 2, 0, 6)
            raw("hy1", 2, 4, 8)
            act.wait_ge(s["inter_arg"], 1)
            for d in range(2):
                A.activation(rw(0)[:, d * T:(d + 1) * T], rw(4)[:, d * T:(d + 1) * T], ACT.Exp, scale=-1.0,
                             bias=rsm[:, 4 + d:5 + d])
            A.activation(rw(2), rw(2), ACT.Exp).then_inc(s["inter_rows"], 1)
            raw("hy2", 2, 8, 10)
            for i in range(4):
                b = take("state", i)
                give(A.copy(CA[:, i].rearrange("p d c -> p (d c)"), b[:, 0:258]))
            for i in range(2):
                b = take("o", i)
                for j in range(2):
                    c = C_BIN + 24 + 2 * i + j
                    ins = A.activation(oT[:, 2 * i + j], b[:, j * T:(j + 1) * T], ACT.Sigmoid, bias=colA[:, c:c + 1])
                give(ins)
            act.wait_ge(s["cols_ready"], 2)
            for h in range(HEADS):
                act.wait_ge(s["w_arg"], h + 1)
                A.activation(W[:, h % 2], W[:, h % 2], ACT.Exp, scale=-1.0).then_inc(s["w_exp"], 1)
                for t in range(2):
                    b = take(f"inter{h}.{t}")
                    if h:
                        act.wait_ge(s["freed_dve"], U.count[U.at(f"num{h - 1}.{t}")])
                    for d in range(2):
                        c = 16 + (d * 2 + t) * 4 + h
                        ins = A.activation(tmpB[:, t, d], b[:, d * 129:(d + 1) * 129], ACT.Identity,
                                           scale=mcols[:, c:c + 1])
                    give(ins)

            def merge_gates(name, n, g0):
                for i in range(n):
                    b = take(name, i)
                    for j in range(2):
                        m = g0 + 2 * i + j
                        ins = A.activation(gates[:, m], b[:, j * T:(j + 1) * T], ACT.Sigmoid,
                                           bias=colA[:, C_BMERGE + m:C_BMERGE + m + 1])
                    give(ins)
            merge_gates("mergeA", 4, 0)
            root(2, sm[:, 40:48], sm[:, 32:40])
            for o in range(2):
                b = take(f"uT{o}", 0)
                if o == 0:
                    wait_emptied(act, "cols")
                    wait_emptied(act, "state")
                else:
                    act.wait_ge(s["unit_done"], U.at("uf0", 3) + 1)
                give(A.copy(unat[:, 0], b[:]))
                merge_gates(f"merge{o}", 2, 8 + 4 * o)
            act.wait_ge(s["unit_done"], U.at("yo1", 1) + 1)
            give(A.copy(bc2[:, 0:512], take("bc2", 0)[:]))

            root(3, sm[:, 8:10], sm[:, 4:6])
            modulate("h2T", hT3, 16, 0, 24)
            act.wait_ge(s["soft_arg"], 1)
            A.activation(affn.rearrange("p t e -> p (t e)"), affn.rearrange("p t e -> p (t e)"), ACT.Exp).then_inc(s["aff_exp"], 1)
            for d in range(8):
                if U.engine[U.at("gather", d)] == "A":
                    b = take("gather", d)
                    give(A.activation(xgT[:, d], b[:], ACT.Identity, scale=gcol[:, 16 + d:17 + d], bias=adaT[:, 24 + d, 0:1]))
            give(A.copy(bc5[:, 0:512], take("bc5", 0)[:]))
            wait_emptied(act, "gather")
            A.copy(xg, xgT[:, :, 0:CAP]).then_inc(s["xg_copied"], 1)

            def expert(e, last=False):
                act.wait_ge(s["slots_used"], e * PER_EXPERT + 4)
                A.activation(sact, bank[0][:], ACT.Silu).then_inc(s["a_read"], 1)
                if not last:
                    act.wait_ge(s["slots_used"], e * PER_EXPERT + 8)
                    A.copy(xg, xgT[:, :, bass.ds(e * CAP + CAP, CAP)]).then_inc(s["xg_copied"], 1)
                act.wait_ge(s["slots_used"], e * PER_EXPERT + 12)
                A.copy(ysb, bank[0][:, 0:T]).then_inc(s["y_evac"], 1)
            with act.Fori(0, EXPERTS - 1) as e:
                expert(e)
            expert(EXPERTS - 1, True)
            root(4, sm[:, 8:10], sm[:, 4:6])

            nroot = [4]

            def next_root(n):
                nroot[0] += 1
                root(nroot[0], sm[:, 8:8 + n], sm[:, 0:n])

            for l in range(DEPTH_2):
                for i in (0, 2):
                    give(A.copy(hT3[:, 2 * i:2 * i + 2].rearrange("p k t -> p (k t)"), take(f"xT{l}", i)[:]))
                for i in range(9):
                    b = take(f"qka{l}", i)
                    for j in range(2):
                        m = 2 * i + j
                        c = l * P + E_QKA + m
                        ins = A.activation(qka[:, m], b[:, j * T:(j + 1) * T], ACT.Identity, bias=colC[:, c:c + 1])
                    give(ins)
                for j in range(HPG):
                    def softmax_exp():
                        act.wait_ge(s["sc_ready"], HPG * l + j + 1)
                        A.activation(sc[:, 0:3], sc[:, 0:3], ACT.Exp, bias=sm[:, 58:59], accum_out=sm[:, 60:61])
                        A.activation(sc[:, 3:9], sc[:, 3:9], ACT.Exp, bias=sm[:, 59:60],
                                     accum_out=sm[:, 61:62]).then_inc(s["exp_done"], 1)
                    softmax_exp()
                    if j < 2:
                        for i in range(4):
                            b = take(f"qkr_v{l}.{j}", i)
                            n = 8 * l + 4 * j + i
                            if n:
                                act.wait_ge(s["rot_done"], n)
                            for q in range(2):
                                c = l * P + E_QKR + 2 * (4 * j + i) + q
                                ins = A.activation(rraw[:, q], b[:, q * T:(q + 1) * T], ACT.Identity, bias=colC[:, c:c + 1])
                            give(ins)
                    for i in range(3):
                        b = take(f"pT{l}.{j}", i)
                        give(A.copy(pT[:, 3 * i:3 * i + 3].rearrange("p k t -> p (k t)"), b[:, 0:384]))
                for h in range(RH):
                    for t in range(2):
                        give(A.copy(yr[:, t, h * 512:(h + 1) * 512], take(f"ro{l}.{h}", t)[:]))
                for i in range(8):
                    b = take(f"gate{l}", i)
                    for q in range(2):
                        c = l * P + E_GG + 16 + 2 * i + q
                        ins = A.activation(gates2[:, 2 * i + q], b[:, q * T:(q + 1) * T], ACT.Sigmoid, bias=colC[:, c:c + 1])
                    give(ins)
                    if i == 3:
                        next_root(8)
                for i in range(8):
                    b = take(f"gr{l}.{i}")
                    if i >= 2:
                        act.wait_ge(s["freed_dve"], U.count[U.at(f"yrT{l}.{i - 2}")])
                    for q in range(2):
                        c = l * P + E_GG + 2 * i + q
                        ins = A.activation(gtmp[:, i % 2, q * T:(q + 1) * T], b[:, q * T:(q + 1) * T], ACT.Silu, bias=colC[:, c:c + 1])
                    give(ins)
                next_root(2)
                for i in (0, 2):
                    give(A.copy(hT3[:, 2 * i:2 * i + 2].rearrange("p k t -> p (k t)"), take(f"x2T{l}", i)[:]))
                for i in range(NF // 2):
                    b = take(f"ffg{l}.{i}")
                    if i >= 2:
                        act.wait_ge(s["freed_dve"], U.count[U.at(f"ffu{l}.{i - 2}")])
                    give(A.activation(gtmp[:, i % 2], b[:], ACT.Silu))
                next_root(2)

        @block.vector
        def _(dve):
            V = nc.vector
            chain = [0]

            def link(ins):
                chain[0] += 1
                ins.then_inc(s["dve_step"], 1)
                dve.wait_ge(s["dve_step"], chain[0])

            def take(name, i=0):
                u = U.at(name, i)
                assert U.engine[u] == "V", name
                dve.wait_ge(s["unit_done"], u + 1)
                return bank[u % 8]

            def give(ins):
                ins.then_inc(s["freed_dve"], 1)

            def tt(o, i0, i1, op=ALU.mult):
                return V.tensor_tensor(o, i0, i1, op)

            def stt(o, i0, sc, i1, op0, op1):
                return V.scalar_tensor_tensor(o, i0, sc, i1, op0, op1)

            def inv_root(k, var, rt, inv):
                dve.wait_ge(s["sqrt_ready"], k)
                link(V.reciprocal(inv, rt))

            dve.wait_ge(s["const_landed"], 16 * len(early))
            dve.wait_ge(s["cst_set"], 1)
            b = take("packs", 0)
            V.tensor_copy(colA[:], b[:, 0:P])
            V.tensor_copy(colB[:], b[:, P:2 * P]).then_inc(s["freed_dve"], 1)
            b = take("packs", 1)
            give(V.tensor_copy(colC[:], b[:, 0:2 * P]))
            dve.wait_ge(s["freed_dve"], 2)
            dve.sem_inc(s["cols_ready"], 1)
            b = take("reltab")
            give(tt(relbuf, b[0:AH, 0:384], distmask, ALU.add))
            dve.wait_ge(s["freed_dve"], 3)
            dve.sem_inc(s["rel_ready"], 1)

            def sine_arg(b, col, dst, tmp):
                magic, c1 = 12582912.0, 6.28125
                c2 = 2 * np.pi - c1
                link(V.tensor_scalar(dst, b, fb[:, col:col + 1], None, ALU.add))
                link(V.tensor_scalar(tmp, dst, 1 / (2 * np.pi), magic, ALU.mult, ALU.add))
                link(V.tensor_scalar(tmp, tmp, -magic, None, ALU.add))
                link(stt(dst, tmp, -c1, dst, ALU.mult, ALU.add))
                link(stt(dst, tmp, -c2, dst, ALU.mult, ALU.add))
                return V.tensor_scalar(dst, dst, 3.1415925, -3.1415925, ALU.min, ALU.max)

            b = take("sin1")
            link(sine_arg(b[0:64, 0:T], 0, sv[0:64, 0], sv[0:64, 3]))
            dve.sem_inc(s["sin_arg1"], 1)
            dve.sem_inc(s["freed_dve"], 1)
            b = take("sin2")
            link(sine_arg(b[0:64, 0:T], 1, sv[0:64, 2], sv[0:64, 0]))
            dve.sem_inc(s["sin_arg2"], 1)
            dve.sem_inc(s["freed_dve"], 1)
            for i in range(8):
                t, o, side = i // 4, (i // 2) % 2, i % 2
                b = take("filt", i)
                give(tt(filt[:, t, o, side], b[:], win[:, side, t]))
            dve.wait_ge(s["freed_dve"], U.count[U.at("filt", 7)])
            for o in range(2):
                link(tt(filt[0:1, 0, o, 0], filt[0:1, 0, o, 0], skipb[:, o * 512:(o + 1) * 512], ALU.add))
            for t in range(2):
                for o in range(2):
                    link(tt(Utmp[:, 0], filt[:, t, o, 0], filt[:, t, o, 1], ALU.subtract))
                    link(tt(filt[:, t, o, 0], filt[:, t, o, 0], filt[:, t, o, 1], ALU.add))
                    link(V.tensor_copy(filt[:, t, o, 1], Utmp[:, 0]))
            dve.sem_inc(s["filt_sum"], 1)
            for i in range(8):
                if U.engine[U.at("filtK", i)] == "V":
                    b = take("filtK", i)
                    o, f, q = i // 4, (i // 2) % 2, i % 2
                    give(V.tensor_scalar(filtK[:, o, q, f], b[:], dftw[:, f:f + 1], None, ALU.mult))
            bn = sm[:, 64:64 + 48].rearrange("p (t h c) -> p t h c", t=4, h=2)

            def mean_square(src3, t0, n):
                for t in range(n):
                    for h in range(2):
                        link(V.bn_stats(bn[:, t0 + t, h], src3[:, t, h * 512:(h + 1) * 512]))
                    link(V.bn_aggr(sm[:, 16 + 2 * (t0 + t):18 + 2 * (t0 + t)], bn[:, t0 + t].rearrange("p h c -> p (h c)")))
            mean_square(x3, 0, 2)
            mean_square(ctxn, 2, 2)
            mv = sm[:, 16:24].rearrange("p (t c) -> p t c", c=2)
            link(tt(sm[:, 4:8], mv[:, :, 0], mv[:, :, 0]))
            link(tt(sm[:, 4:8], sm[:, 4:8], mv[:, :, 1], ALU.add))
            link(V.tensor_scalar(sm[:, 4:8], sm[:, 4:8], EPS, None, ALU.add))
            dve.sem_inc(s["var_ready"], 1)
            for i in range(12):
                if U.engine[U.at("ada", i)] == "V":
                    give(V.tensor_copy(adarow[:, i], take("ada", i)[:]))
            inv_root(1, sm[:, 4:8], sm[:, 8:12], sm[:, 12:16])
            for t in range(2):
                ins = V.tensor_scalar(xn[:, t], x3[:, t], sm[:, 12 + t:13 + t], None, ALU.mult)
            ins.then_inc(s["x_norm"], 1)
            b = take("adacol")
            for j in range(2):
                link(tt(adaT[:, :, j], b[:, 0:96].rearrange("p (c j) -> p c j", j=2)[:, :, j], colA[:, 0:48], ALU.add))
            for g0, j, r0, gc in ((0, 0, 8, C_NMIX), (8, 1, 8, C_NMIX), (16, 0, 32, C_NFFN)):
                link(stt(gcol[:, g0:g0 + 8], adaT[:, r0:r0 + 8, j], 1.0, colA[:, gc:gc + 8], ALU.add, ALU.mult))
            dve.sem_inc(s["m_ready"], 1)
            dve.sem_inc(s["freed_dve"], 1)

            def modulate(name, dst3, g0, src, sh0=0):
                for i in range(4):
                    if U.engine[U.at(name, i)] == "V":
                        b = take(name, i)
                        for j in range(2):
                            d = 2 * i + j
                            ins = V.tensor_scalar(dst3[:, d], b[:, j * T:(j + 1) * T], gcol[:, g0 + d:g0 + d + 1],
                                                  adaT[:, sh0 + d, src:src + 1], ALU.mult, ALU.add)
                        give(ins)
            dve.wait_ge(s["rel_saved"], 16)
            modulate("hx", hT3, 0, 0)
            dve.wait_ge(s["unit_done"], U.at("hx", 3) + 1)
            for t in range(2):
                ins = V.tensor_scalar(xn[:, t], ctxn[:, t], sm[:, 14 + t:15 + t], None, ALU.mult)
            ins.then_inc(s["ctx_norm"], 1)
            modulate("hc", hcT, 8, 1)

            def conv(k, dst, wc, stride, rows, last_unit):
                dve.wait_ge(s["freed_act"], U.count[last_unit])
                src = praw[:, k % 4]
                L = T // rows
                for j in range(2):
                    link(V.tensor_scalar(dst[:, j], src[:, j], colB[:, wc + stride + j:wc + stride + j + 1], None, ALU.mult))
                for j in range(2):
                    y = dst[:, j].rearrange("p (r l) -> p r l", r=rows)
                    v = src[:, j].rearrange("p (r l) -> p r l", r=rows)
                    link(stt(y[:, :, 1:L], v[:, :, 0:L - 1], colB[:, wc + j:wc + j + 1], y[:, :, 1:L], ALU.mult, ALU.add))
                for j in range(2):
                    y = dst[:, j].rearrange("p (r l) -> p r l", r=rows)
                    v = src[:, j].rearrange("p (r l) -> p r l", r=rows)
                    c = wc + 2 * stride + j
                    ins = stt(y[:, :, 0:L - 1], v[:, :, 1:L], colB[:, c:c + 1], y[:, :, 0:L - 1], ALU.mult, ALU.add)
                    if j == 0:
                        link(ins)
                ins.then_inc(s["conv_done"], 1)

            conv(0, kT[:, 0:2], D_MLC + 4, 8, 4, U.at("kx", 0))
            conv(1, kT[:, 2:4], D_MLC + 6, 8, 4, U.at("kx", 1))
            conv(2, kcT[:, 0:2], D_MLC + 4, 8, 1, U.at("kc", 0))
            conv(3, kcT[:, 2:4], D_MLC + 6, 8, 1, U.at("kc", 1))
            for name, dst in (("vx", vx), ("vc", vc)):
                for t in range(2):
                    b = take(name, t)
                    give(tt(dst[:, t, :, 0:128], b[:].rearrange("p (h c) -> p h c", h=4),
                            b_rows[:, 0:512].rearrange("p (h c) -> p h c", h=4), ALU.add))
            b = take("mgate")
            link(tt(gl[:, 0:64].rearrange("p (s c) -> p s c", s=4), b[:, 0:64].rearrange("p (s c) -> p s c", s=4),
                    b_rows[:, 512:528].unsqueeze(1).broadcast_to([P, 4, 16]), ALU.add))
            for d in range(2):
                link(V.tensor_scalar(nlf[:, :, d], G4[:, :, 2 * d + 1], -1.0, 0.0, ALU.mult, ALU.max))
                link(stt(wk[:, :, d], G4[:, :, 2 * d + 1], -1.0, G4[:, :, 2 * d + 1], ALU.mult, ALU.max))
            dve.sem_inc(s["softplus_arg"], 1)
            dve.sem_inc(s["freed_dve"], 1)
            conv(4, qT[:, 0:2], D_MLC + 0, 8, 4, U.at("q", 0))
            conv(5, qT[:, 2:4], D_MLC + 2, 8, 4, U.at("q", 1))
            dve.wait_ge(s["softplus_l"], 1)
            link(tt(gl[:, 64:96], gl[:, 64:96], gl[:, 96:128], ALU.add))
            dve.sem_inc(s["lf_ready"], 1)
            give(V.tensor_copy(rw(0), take("crow", 0)[0:4, :]))
            give(V.tensor_copy(rw(1), take("crow", 1)[0:4, :]))
            dve.wait_ge(s["freed_dve"], U.count[U.at("crow", 1)])
            link(V.tensor_reduce(rsm[:, 0:2], rw(1).rearrange("p (d t) -> p d t", d=2), AX.X, ALU.max))
            link(V.tensor_scalar(rsm[:, 0:2], rsm[:, 0:2], 0.0, None, ALU.max))
            link(V.tensor_scalar(rsm[:, 2:4], rsm[:, 0:2], -1.0, None, ALU.mult))
            link(tt(rsm[:, 4:5], rsm[:, 0:1], rw(0)[:, T - 1:T], ALU.subtract))
            link(tt(rsm[:, 5:6], rsm[:, 1:2], rw(0)[:, T:T + 1], ALU.subtract))
            dve.sem_inc(s["w_row_arg"], 1)
            give(V.tensor_copy(rw(2), take("xrow", 0)[0:4, :]))
            give(V.tensor_copy(rw(3), take("xrow", 1)[0:4, :]))
            dve.wait_ge(s["freed_dve"], U.count[U.at("xrow", 1)])
            link(V.tensor_tensor_scan(rw(4)[:, 0:T], rw(3)[:, 0:T], rw(3)[:, 0:T], rsm[:, 4:5], ALU.max, ALU.max))
            link(V.tensor_tensor_scan(rw(4)[:, 2 * T - 1:T - 1:-1], rw(3)[:, 2 * T - 1:T - 1:-1],
                                      rw(3)[:, 2 * T - 1:T - 1:-1], rsm[:, 5:6], ALU.max, ALU.max))
            link(tt(rw(2), rw(2), rw(4), ALU.subtract))
            dve.sem_inc(s["inter_arg"], 1)
            link(V.tensor_scalar(tri, tri, -BIG, BIG, ALU.mult, ALU.add))
            conv(6, zhy[:, 0:2], D_HYC + 0, 12, 4, U.at("hy0", 0))
            conv(7, zhy[:, 2:4], D_HYC + 2, 12, 4, U.at("hy0", 1))
            link(V.tensor_copy(mcols[:, 48:64], take("wcol")[:, 0:16]))
            dve.sem_inc(s["freed_dve"], 1)
            conv(8, zhy[:, 4:6], D_HYC + 4, 12, 4, U.at("hy1", 0))
            conv(9, zhy[:, 6:8], D_HYC + 6, 12, 4, U.at("hy1", 1))
            for i in range(2):
                b = take("kcn", i)
                for d in range(2):
                    w0 = 48 + (d * 2 + i) * 4
                    ins = tt(kw[:, d, i].rearrange("p (h c) -> p h c", h=4), b[:].rearrange("p (h c) -> p h c", h=4),
                             mcols[:, w0:w0 + 4].unsqueeze(2).broadcast_to([P, 4, P]))
                give(ins)
            conv(10, zhy[:, 8:10], D_HYC + 8, 12, 4, U.at("hy2", 0))
            conv(11, zhy[:, 10:12], D_HYC + 10, 12, 4, U.at("hy2", 1))
            b = take("cols")
            link(V.tensor_copy(mcols[:, 0:48], b[:, 0:48]))
            link(V.tensor_scalar(mcols[:, 16:32], mcols[:, 16:32], float(DH) ** -0.5, None, ALU.mult))
            dve.sem_inc(s["cols_ready"], 1)
            dve.sem_inc(s["freed_dve"], 1)

            def w_distance(h):
                b = take(f"mb{h}")
                if h >= 2:
                    dve.wait_ge(s["unit_done"], U.at(f"num{h - 2}.1") + 1)
                elif h == 0:
                    dve.wait_ge(s["unit_done"], U.at("hc", 3) + 1)
                for d in range(2):
                    for i in range(2):
                        c = (d * 2 + i) * 4 + h
                        ins = stt(W[:, h % 2, 2 * d + i], b[:, d * T:(d + 1) * T], mcols[:, c:c + 1], tri[:, d, i],
                                  ALU.subtract, ALU.max)
                        if d + i < 2:
                            link(ins)
                link(ins)
                dve.sem_inc(s["w_arg"], 1)
                dve.sem_inc(s["freed_dve"], 1)

            for h in range(HEADS):
                w_distance(h)
                b = take(f"sT{h}")
                dve.wait_ge(s["w_exp"], h + 1)
                for d in range(2):
                    wd = W[:, h % 2, 2 * d:2 * d + 2].rearrange("p i t -> p (i t)")
                    ins = stt(wd, b[:], float(DH) ** -0.5, wd, ALU.mult, ALU.mult)
                give(ins)
                for t in range(2):
                    b = take(f"num{h}.{t}")
                    dve.wait_ge(s["freed_act"], U.count[U.at(f"inter{h}.{t}")])
                    give(tt(NUM[:, t, h], b[:, 0:258].rearrange("p (d c) -> p d c", d=2), tmpB[:, t], ALU.add))
            dve.wait_ge(s["freed_dve"], U.count[U.at("num3.1")])
            den = NUM[:, :, :, :, 128:129].rearrange("p t h d c -> p (t h d) c")[:, :, 0]
            dn = sm[:, 24:40]
            link(stt(dn, den, -1.0, den, ALU.mult, ALU.max))
            for t in range(2):
                fl = mcols[:, 32:48].rearrange("p (d i h) -> p i h d", d=2, i=2)[:, t]
                dt = dn[:, 8 * t:8 * t + 8].rearrange("p (h d) -> p h d", d=2)
                link(tt(dt, dt, fl, ALU.max))
            link(V.reciprocal(dn, dn))
            nv = NUM[:].rearrange("p t h d c -> p (t h d) c")
            link(tt(nv[:, :, 0:128], nv[:, :, 0:128], dn.unsqueeze(2).broadcast_to([P, 16, P])))
            nh = NUM[:].rearrange("p t h d c -> p (t h) d c")
            link(tt(hm, nh[:, :, 0, 0:128], nh[:, :, 1, 0:128], ALU.add))
            link(tt(hsq, hm, hm))
            link(V.tensor_reduce(sm[:, 32:40], hsq, AX.X, ALU.add))
            link(V.tensor_scalar(sm[:, 32:40], sm[:, 32:40], 1.0 / DH, EPS, ALU.mult, ALU.add))
            dve.sem_inc(s["var_ready"], 1)
            inv_root(2, sm[:, 32:40], sm[:, 40:48], sm[:, 48:56])
            link(tt(hm, hm, sm[:, 48:56].unsqueeze(2).broadcast_to([P, 8, P])))
            dve.sem_inc(s["hm_ready"], 1)
            for i in range(2):
                b = take("hT", i)
                for j in range(2):
                    h = 2 * i + j
                    ins = stt(YB[:, h], b[:, j * T:(j + 1) * T], colB[:, D_MLG + h:D_MLG + h + 1], oT[:, h], ALU.mult, ALU.mult)
                give(ins)
            dve.wait_ge(s["unit_done"], U.at("hT", 1) + 1)
            for o in range(2):
                b = take(f"uT{o}", 1)
                if o:
                    dve.wait_ge(s["unit_done"], U.at("uf0", 3) + 1)
                give(V.tensor_copy(unat[:, 1], b[:]))
                if o:
                    dve.wait_ge(s["unit_done"], U.at("yo0", 1) + 1)
                for f in range(2):
                    bc_, bs = take(f"uf{o}", 2 * f), take(f"uf{o}", 2 * f + 1)
                    Kr, Ks = filtK[:, o, 0, f], filtK[:, o, 1, f]
                    link(tt(Utmp[:, 0], bc_[:], Kr))
                    tt(Utmp[:, 1], bc_[:], Ks).then_inc(s["freed_dve"], 1)
                    link(tt(Utmp[:, 2], bs[:], Ks))
                    tt(Utmp[:, 3], bs[:], Kr).then_inc(s["freed_dve"], 1)
                    dve.wait_ge(s["freed_dve"], U.count[U.at(f"uf{o}", 2 * f + 1)])
                    link(tt(Y[:, 0, f], Utmp[:, 0], Utmp[:, 2], ALU.subtract))
                    link(tt(Y[:, 1, f], Utmp[:, 1], Utmp[:, 3], ALU.add))
                dve.sem_inc(s["y_spec"], 1)
                for i in range(2):
                    b = take(f"yo{o}", i)
                    give(tt(zhy[:, 2 * i:2 * i + 2].rearrange("p c t -> p (c t)"), b[:],
                            zhy[:, 4 * (o + 1) + 2 * i:4 * (o + 1) + 2 * i + 2].rearrange("p c t -> p (c t)")))

            def make_diag(chunk, dst, signal):
                for d in range(8):
                    ins = V.tensor_scalar(dst[:, d], ident[:], adaT[:, 8 * chunk + d, 0:1], None, ALU.mult)
                ins.then_inc(signal, 1)
            make_diag(2, diag, s["bc_diag"])
            give(V.tensor_copy(bc2[:, 512:1024], take("bc2", 1)[:]))
            for c in range(4):
                ba, bb = take(f"bra{c}", 0), take(f"bra{c}", 1)
                ga = gates[:, 2 * c:2 * c + 2].rearrange("p c t -> p (c t)")
                gb = gates[:, 8 + 2 * c:8 + 2 * c + 2].rearrange("p c t -> p (c t)")
                if c == 0:
                    wait_emptied(dve, "merge1")
                else:
                    dve.wait_ge(s["merged_ready"], c)
                tt(mtmp[:, 0], ba[:], ga).then_inc(s["freed_dve"], 1)
                tt(mtmp[:, 1], bb[:], gb).then_inc(s["freed_dve"], 1)
                dve.wait_ge(s["freed_dve"], U.count[U.at(f"bra{c}", 1)])
                tt(merged[:, 2 * c:2 * c + 2].rearrange("p c t -> p (c t)"), mtmp[:, 0], mtmp[:, 1], ALU.add).then_inc(s["merged_ready"], 1)
            dve.wait_ge(s["freed_act"], U.count[U.at("bc2", 0)])
            for i in range(4):
                n, t = divmod(i, 2)
                b = take("out1", i)
                dve.wait_ge(s["freed_dve"], U.count[U.at("out1", i)] - 1)
                link(tt(mtmp[:, 2], b[:], bc2[:, 512 * n:512 * n + 512]))
                give(tt(x3[:, t, 512 * n:512 * n + 512], x3[:, t, 512 * n:512 * n + 512], mtmp[:, 2], ALU.add))

            def rms(kroot):
                link(V.tensor_copy(sm[:, 56:57], cst[:, 0:1]))
                mean_square(x3, 0, 2)
                m2 = sm[:, 16:20].rearrange("p (t c) -> p t c", c=2)
                link(tt(sm[:, 4:6], m2[:, :, 0], m2[:, :, 0]))
                link(tt(sm[:, 4:6], sm[:, 4:6], m2[:, :, 1], ALU.add))
                link(V.tensor_scalar(sm[:, 4:6], sm[:, 4:6], EPS, None, ALU.add))
                dve.sem_inc(s["var_ready"], 1)
                inv_root(kroot, sm[:, 4:6], sm[:, 8:10], sm[:, 12:14])
            dve.wait_ge(s["freed_dve"], U.count[U.at("out1", 3)])
            rms(3)
            for t in range(2):
                ins = V.tensor_scalar(xn2[:, t], x3[:, t], sm[:, 12 + t:13 + t], None, ALU.mult)
            ins.then_inc(s["xn2_ready"], 1)
            modulate("h2T", hT3, 16, 0, 24)
            dve.wait_ge(s["moe_landed"], 80)
            b = take("route")
            lg = b[:, 0:32].rearrange("p (t e) -> p t e", t=2)
            link(V.tensor_reduce(sm[:, 24:26], lg, AX.X, ALU.max))
            link(tt(affn, lg, sm[:, 24:26].unsqueeze(2).broadcast_to([P, 2, 16]), ALU.subtract))
            dve.sem_inc(s["soft_arg"], 1)
            dve.sem_inc(s["freed_dve"], 1)
            dve.wait_ge(s["aff_exp"], 1)
            link(V.tensor_reduce(sm[:, 26:28], affn, AX.X, ALU.add))
            link(V.reciprocal(sm[:, 28:30], sm[:, 26:28]))
            link(tt(affn, affn, sm[:, 28:30].unsqueeze(2).broadcast_to([P, 2, 16])))
            dve.sem_inc(s["aff_ready"], 1)
            give(V.tensor_copy(affT, take("affT")[0:16, 0:T]))
            n = 0
            for i in range(8):
                b = take("affbc", i)
                for q in range(2):
                    e = 2 * i + q
                    row = b[:, q * T:(q + 1) * T]
                    for t in range(2):
                        if n:
                            dve.wait_ge(s["rank_ready"], n)
                        own = affn[:, t, e:e + 1]
                        V.tensor_scalar(rjunk[:, 0], row, own, 0.0, ALU.is_gt, ALU.add, accum_out=rank[:, 0, t, e:e + 1])
                        ins = V.scalar_tensor_tensor(rjunk[:, 1], row, own, ltmask[:, t], ALU.is_equal, ALU.mult,
                                                     accum_out=rank[:, 1, t, e:e + 1])
                        ins.then_inc(s["rank_ready"], 1)
                        n += 1
                dve.wait_ge(s["rank_ready"], n)
                dve.sem_inc(s["freed_dve"], 1)
            link(tt(rank[:, 0], rank[:, 0], rank[:, 1], ALU.add))
            for t in range(2):
                ins = tt(sel[:, t].rearrange("p (e c) -> p e c", e=16), iota.unsqueeze(1).broadcast_to([P, 16, CAP]),
                         rank[:, 0, t].unsqueeze(2).broadcast_to([P, 16, CAP]), ALU.is_equal)
            link(ins)
            dve.sem_inc(s["sel_ready"], 1)
            make_diag(5, diag5, s["bc_diag"])
            for d in range(8):
                if U.engine[U.at("gather", d)] == "V":
                    b = take("gather", d)
                    give(V.tensor_scalar(xgT[:, d], b[:], gcol[:, 16 + d:17 + d], adaT[:, 24 + d, 0:1], ALU.mult, ALU.add))
            give(V.tensor_copy(bc5[:, 512:1024], take("bc5", 1)[:]))

            def gated_selection(e, at):
                for t in range(2):
                    ins = V.tensor_scalar(sgs[:, t].rearrange("p (g c) -> p g c", g=4),
                                          sel[:, t, at].unsqueeze(1).broadcast_to([P, 4, CAP]),
                                          affn[:, t, bass.ds(e, 1)], None, ALU.mult)
                ins.then_inc(s["sg_copied"], 1)
            gated_selection(0, slice(0, CAP))
            V.memset(acc, 0.0).then_inc(s["acc_done"], 1)

            def expert(e, last=False):
                dve.wait_ge(s["slots_used"], e * PER_EXPERT + 8)
                dve.wait_ge(s["a_read"], e + 1)
                tt(hact, bank[1][:], sact).then_inc(s["hact"], 1)
                dve.wait_ge(s["sg_turned"], e + 1)
                V.tensor_copy(sgT, bank[3][:, 0:T]).then_inc(s["sgT_evac"], 1)
                if not last:
                    gated_selection(e + 1, bass.ds(e * CAP + CAP, CAP))
                dve.wait_ge(s["hT_turned"], e + 1)
                V.tensor_copy(hTs.rearrange("p c t -> p (c t)"), bank[2][:]).then_inc(s["hT_evac"], 1)
                dve.wait_ge(s["scat_done"], e + 1)
                dve.wait_ge(s["acc_done"], e + 1)
                for n in range(4):
                    o = acc[:, :, n * T:(n + 1) * T]
                    ins = tt(o, bank[4 + n][:].rearrange("p (t d) -> p t d", t=2), o, ALU.add)
                ins.then_inc(s["acc_done"], 1)
            with dve.Fori(0, EXPERTS - 1) as e:
                expert(e)
            expert(EXPERTS - 1, True)
            dve.wait_ge(s["acc_done"], EXPERTS + 1)
            wait_emptied(dve, "bc5")
            for t in range(2):
                link(tt(acc[:, t], acc[:, t], bc5))
                link(tt(x3[:, t], x3[:, t], acc[:, t], ALU.add))
            rms(4)
            for t in range(2):
                ins = stt(x3[:, t], x3[:, t], sm[:, 12 + t:13 + t], fnorm, ALU.mult, ALU.mult)
            ins.then_inc(s["x1_ready"], 1)

            nroot = [4]

            def next_root(n):
                nroot[0] += 1
                dve.sem_inc(s["var_ready"], 1)
                inv_root(nroot[0], sm[:, 0:n], sm[:, 8:8 + n], sm[:, 16:16 + n])

            def layer_norm(w, signal):
                for t in range(2):
                    for h in range(2):
                        ins = V.bn_stats(bn[:, t, h], x3[:, t, h * 512:(h + 1) * 512])
                link(ins)
                for t in range(2):
                    ins = V.bn_aggr(sm[:, 24 + 2 * t:26 + 2 * t], bn[:, t].rearrange("p h c -> p (h c)"))
                link(ins)
                mv2 = sm[:, 24:28].rearrange("p (t c) -> p t c", c=2)
                link(V.tensor_scalar(sm[:, 0:2], mv2[:, :, 1], LN_EPS, None, ALU.add))
                next_root(2)
                for t in range(2):
                    link(V.tensor_scalar(x3[:, t], x3[:, t], sm[:, 24 + 2 * t:25 + 2 * t], sm[:, 16 + t:17 + t],
                                         ALU.subtract, ALU.mult))
                    link(tt(x3[:, t], x3[:, t], w[:, 0]))
                    tt(x3[:, t], x3[:, t], w[:, 1], ALU.add).then_inc(signal, 1)

            for l in range(DEPTH_2):
                for i in (1, 3):
                    give(V.tensor_copy(hT3[:, 2 * i:2 * i + 2].rearrange("p k t -> p (k t)"), take(f"xT{l}", i)[:]))
                dve.wait_ge(s["lay_landed"], 80 + 48 * l)
                for i in range(3):
                    wd = 512 if i < 2 else 128
                    for t in range(2):
                        b = take(f"va{l}", 2 * i + t)
                        give(tt(va[:, t, 512 * i:512 * i + wd], b[:, 0:wd], vbias_a[:, 512 * i:512 * i + wd], ALU.add))
                relg = relB.rearrange("p (g j) t -> p g j t", g=NG)
                for j in range(HPG):
                    b0, b1, b2 = (take(f"score{l}.{j}", i) for i in range(3))
                    if j:
                        dve.wait_ge(s["unit_done"], U.at(f"pT{l}.{j - 1}", 2) + 1)
                    else:
                        dve.wait_ge(s["freed_dve"], U.count[U.at(f"va{l}", 5)])
                    scale = AD ** -0.5
                    c1 = sc[:, 3:9].rearrange("p (g k) t -> p g (k t)", g=NG)
                    give(stt(sc[:, 0:3], b0[:, 0:384].rearrange("p (g t) -> p g t", g=3), scale, relg[:, :, j, P:T], ALU.mult, ALU.add))
                    give(stt(c1[:, 0:2], b1[:].rearrange("p (g t) -> p g t", g=2), scale, relg[:, 0:2, j], ALU.mult, ALU.add))
                    give(stt(c1[:, 2], b2[:, 0:T], scale, relg[:, 2, j], ALU.mult, ALU.add))
                    dve.wait_ge(s["freed_dve"], U.count[U.at(f"score{l}.{j}", 2)])
                    V.tensor_reduce(sm[:, 56:57], sc[:, 0:3], AX.XY, ALU.max)
                    link(V.tensor_reduce(sm[:, 57:58], sc[:, 3:9], AX.XY, ALU.max))
                    link(V.tensor_scalar(sm[:, 58:60], sm[:, 56:58], -1.0, None, ALU.mult))
                    dve.sem_inc(s["sc_ready"], 1)
                    if j < 2:
                        for i in range(4):
                            hh = 4 * j + i
                            dve.wait_ge(s["freed_act"], U.count[U.at(f"qkr_v{l}.{j}", i)])
                            cos2 = rope[:, 0].unsqueeze(1).broadcast_to([P, 2, T])
                            sin2 = rope[:, 1].unsqueeze(1).broadcast_to([P, 2, T])
                            tt(rm1, rraw, cos2)
                            link(tt(rm2, rraw, sin2))
                            tt(qkr[:, 2 * hh], rm1[:, 0], rm2[:, 1], ALU.subtract)
                            link(tt(qkr[:, 2 * hh + 1], rm2[:, 0], rm1[:, 1], ALU.add))
                            dve.sem_inc(s["rot_done"], 1)
                    elif j < 4:
                        for i in range(4):
                            n = 2 * (j - 2) + i // 2
                            b = take(f"qkr_v{l}.{j}", i)
                            give(tt(vr[:, i % 2, 512 * n:512 * n + 512], b[:], vbias_r[:, 512 * n:512 * n + 512], ALU.add))
                    dve.wait_ge(s["exp_done"], HPG * l + j + 1)
                    link(V.reciprocal(sm[:, 62:64], sm[:, 60:62]))
                    b = take(f"attn{l}.{j}")
                    for t in range(2):
                        ins = V.tensor_scalar(ya[:, t, j * AD:(j + 1) * AD], b[:, t * AD:(t + 1) * AD], sm[:, 62 + t:63 + t], None, ALU.mult)
                    give(ins)
                give(V.tensor_copy(yaT[:, 0:2].rearrange("p k t -> p (k t)"), take(f"yaT{l}", 0)[:]))
                give(V.tensor_copy(yaT[:, 2], take(f"yaT{l}", 1)[:, 0:T]))
                for h in range(RH):
                    b = take(f"rs{l}.{h}")
                    if h >= 2:
                        dve.wait_ge(s["unit_done"], U.at(f"ro{l}.{h - 2}", 1) + 1)
                    give(tt(pr[:, h % 2], b[:, 0:384], decay[:, h]))
                for h in range(RH):
                    for t in range(2):
                        dve.wait_ge(s["freed_act"], U.count[U.at(f"ro{l}.{h}", t)])
                        c = 2 * (2 * h + t)
                        link(V.bn_stats(bn[:, 0, 0], yr[:, t, h * 512:(h + 1) * 512]))
                        link(V.bn_aggr(sm[:, 24 + c:26 + c], bn[:, 0, 0]))
                mvr = sm[:, 24:40].rearrange("p (n c) -> p n c", c=2)
                link(V.tensor_scalar(sm[:, 0:8], mvr[:, :, 1], LN_EPS, None, ALU.add))
                next_root(8)
                for h in range(RH):
                    for t in range(2):
                        n = 2 * h + t
                        v = yr[:, t, h * 512:(h + 1) * 512]
                        link(V.tensor_scalar(v, v, sm[:, 24 + 2 * n:25 + 2 * n], sm[:, 16 + n:17 + n], ALU.subtract, ALU.mult))
                    dve.sem_inc(s["yr_ready"], 1)
                for c in range(8):
                    b = take(f"yrT{l}.{c}")
                    dve.wait_ge(s["freed_act"], U.count[U.at(f"gr{l}.{c}")])
                    give(tt(ybT[:, 2 * c:2 * c + 2].rearrange("p k t -> p (k t)"), b[:], gtmp[:, c % 2]))
                wait_emptied(dve, f"gate{l}")
                for i in range(4):
                    give(tt(merged2[:, 2 * i:2 * i + 2].rearrange("p k t -> p (k t)"), take(f"mixA{l}", i)[:],
                            gates2[:, 2 * i:2 * i + 2].rearrange("p k t -> p (k t)")))
                for i in range(4):
                    m = merged2[:, 2 * i:2 * i + 2].rearrange("p k t -> p (k t)")
                    link(tt(btmp[:, i % 2], take(f"mixB{l}", i)[:], gates2[:, 8 + 2 * i:10 + 2 * i].rearrange("p k t -> p (k t)")))
                    dve.wait_ge(s["freed_dve"], U.count[U.at(f"mixA{l}", 3)] + i)
                    give(tt(m, m, btmp[:, i % 2], ALU.add))
                for i in range(4):
                    n, t = divmod(i, 2)
                    v = x3[:, t, 512 * n:512 * n + 512]
                    give(stt(v, v, ALPHA, take(f"mixo{l}", i)[:], ALU.mult, ALU.add))
                dve.wait_ge(s["freed_dve"], U.count[U.at(f"mixo{l}", 3)])
                dve.wait_ge(s["ln_landed"], 64 * (l + 1))
                layer_norm(ln1, s["x_done"])
                dve.wait_ge(s["x_done"], 2 * (l + 1) if l == 0 else 6)
                for i in (1, 3):
                    give(V.tensor_copy(hT3[:, 2 * i:2 * i + 2].rearrange("p k t -> p (k t)"), take(f"x2T{l}", i)[:]))
                for i in range(NF // 2):
                    b = take(f"ffu{l}.{i}")
                    dve.wait_ge(s["freed_act"], U.count[U.at(f"ffg{l}.{i}")])
                    give(tt(hF[:, 2 * i:2 * i + 2].rearrange("p k t -> p (k t)"), b[:], gtmp[:, i % 2]))
                for i in range(4):
                    n, t = divmod(i, 2)
                    v = x3[:, t, 512 * n:512 * n + 512]
                    give(stt(v, v, ALPHA, take(f"down{l}", i)[:], ALU.mult, ALU.add))
                dve.wait_ge(s["freed_dve"], U.count[U.at(f"down{l}", 3)])
                layer_norm(ln2, s["x_done"] if l < DEPTH_2 - 1 else s["y_ready"])
                if l < DEPTH_2 - 1:
                    dve.wait_ge(s["x_done"], 4)

        @block.tensor
        def _(pe):
            M = nc.tensor

            def open_unit(name, i=0):
                u = U.at(name, i)
                if u >= 8:
                    v = u - 8
                    pe.wait_ge(freed[U.engine[v]], U.count[v])
                return bank[u % 8]

            def close(ins):
                ins.then_inc(s["unit_done"], 1)

            def mm(o, l, r, first=True, last=True):
                return M.matmul(o, l, r, start=first, stop=last)

            def tr(o, i):
                return M.transpose(o, i, ident[:])

            def gemm_T(name, i, w, cols, xT, nk=KD):
                b = open_unit(name, i)
                for j, c in enumerate(cols):
                    for q in range(nk):
                        ins = mm(b[:, j * T:(j + 1) * T], w[:, q, c:c + P], xT[:, q], q == 0, q == nk - 1)
                close(ins)

            def gemm_N(name, i, w, width, xT, t, nk=KD):
                b = open_unit(name, i)
                for q in range(nk):
                    ins = mm(b[:, 0:width], xT[:, q, t * P:(t + 1) * P], w[:, q, 0:width], q == 0, q == nk - 1)
                close(ins)

            def turn(name, src3, n=4):
                for i in range(n):
                    b = open_unit(name, i)
                    for j in range(2):
                        for t in range(2):
                            ins = tr(b[:, j * T + t * P:j * T + t * P + P], src3[:, t, (2 * i + j) * P:(2 * i + j + 1) * P])
                    close(ins)

            pe.wait_ge(s["const_landed"], 16 * len(early))
            pe.wait_ge(s["cst_set"], 1)
            pe.wait_ge(s["packs_landed"], 16 * 16)
            b = open_unit("packs", 0)
            tr(b[:, 0:P], colA[:])
            close(tr(b[:, P:2 * P], colB[:]))
            b = open_unit("packs", 1)
            tr(b[:, 0:P], colC[:, 0:P])
            close(tr(b[:, P:2 * P], colC[:, P:2 * P]))
            b = open_unit("reltab")
            close(mm(b[0:AH, 0:384], rel_bias, onehot))
            b = open_unit("sin1")
            close(mm(b[0:64, 0:T], w1s[0:33], emb[0:33]))
            b = open_unit("sin2")
            pe.wait_ge(s["sin1_ready"], 1)
            close(mm(b[0:64, 0:T], w2s[0:64], sv[0:64, 1]))
            pe.wait_ge(s["sin2_ready"], 1)
            for i in range(8):
                t, c = divmod(i, 4)
                b = open_unit("filt", i)
                close(mm(b[:], sv[0:64, 3, t * P:(t + 1) * P], w3[0:64, 512 * c:512 * c + 512]))
            pe.wait_ge(s["filt_sum"], 1)
            for i in range(8):
                o, f, q = i // 4, (i // 2) % 2, i % 2
                b = open_unit("filtK", i)
                for t in range(2):
                    ins = mm(b[:], dft[:, q, t, f * P:(f + 1) * P], filt[:, t, o, q], t == 0, t == 1)
                close(ins)
            pe.wait_ge(s["silu_c"], 1)
            for i in range(12):
                arrived(pe, i)
                w = slot(i, 8, 512)
                b = open_unit("ada", i)
                for q in range(2):
                    for g in range(4):
                        ins = mm(b[32 * g:32 * g + 32, :], sTad[:, 2 * g + q], w[:, 2 * g + q], q == 0, q == 1)
                close(ins)
            wait_emptied(pe, "ada")
            b = open_unit("adacol")
            for c in range(48):
                ins = mm(b[:, 2 * c:2 * c + 2], adarow[:, c // 4, (c % 4) * P:(c % 4 + 1) * P], selsum[:])
            close(ins)
            pe.wait_ge(s["x_norm"], 1)
            turn("hx", xn)
            pe.wait_ge(s["ctx_norm"], 1)
            turn("hc", xn)
            wait_emptied(pe, "hx")
            wait_emptied(pe, "hc")

            def gemm_slot_T(n, name, i0, xT, nk=KD, width=512):
                arrived(pe, n)
                w = slot(n, nk, width)
                for i in range(width // 256):
                    gemm_T(name, i0 + i, w, (256 * i, 256 * i + P), xT, nk)

            gemm_slot_T(S_KC, "kx", 0, hT3)
            gemm_slot_T(S_KC, "kc", 0, hcT)
            arrived(pe, S_V)
            for name, act_ in (("vx", hT3), ("vc", hcT)):
                for t in range(2):
                    gemm_N(name, t, slot(S_V, 8, 512), 512, act_, t)
            b = open_unit("mgate")
            wg = w_gate[:].rearrange("p (k c) -> p k c", k=KD)
            for i, act_ in enumerate((hT3, hcT)):
                for t in range(2):
                    for q in range(KD):
                        ins = mm(b[:, (2 * i + t) * 16:(2 * i + t + 1) * 16], act_[:, q, t * P:(t + 1) * P], wg[:, q],
                                 q == 0, q == KD - 1)
            close(ins)
            gemm_slot_T(S_Q, "q", 0, hT3)
            pe.wait_ge(s["lf_ready"], 1)
            for name, i in (("crow", 1), ("xrow", 0)):
                b = open_unit(name, 0)
                for d in range(2):
                    for t in range(2):
                        ins = mm(b[0:4, d * T:(d + 1) * T], nlf[:, 2 * i + t, d], tri[:, d, t], t == 0, t == 1)
                close(ins)
                b = open_unit(name, 1)
                for d in range(2):
                    for t in range(2):
                        o = b[0:4, d * T + t * P:d * T + (t + 1) * P]
                        mm(o, G4[:, 2 * i + t, 2 * d], ident[:], True, False)
                        for q in range(2):
                            ins = mm(o, nlf[:, 2 * i + q, d], tri[:, d, q, t * P:(t + 1) * P], False, q == 1)
                close(ins)
            gemm_slot_T(S_HY, "hy0", 0, hT3)
            pe.wait_ge(s["w_row"], 1)
            b = open_unit("wcol")
            for d in range(2):
                for t in range(2):
                    c = (d * 2 + t) * 4
                    ins = mm(b[:, c:c + 4], rw(5)[:, d * T + t * P:d * T + (t + 1) * P], ident[0:4, 0:4])
            close(ins)
            gemm_slot_T(S_HY + 1, "hy1", 0, hT3)
            pe.wait_ge(s["qk_ready"], 4)
            wait_emptied(pe, "wcol")
            for t in range(2):
                b = open_unit("kcn", t)
                for h in range(4):
                    ins = tr(b[:, h * P:(h + 1) * P], kcT[:, h, t * P:(t + 1) * P])
                close(ins)
            gemm_slot_T(S_HY + 2, "hy2", 0, hT3)
            wait_emptied(pe, "kcn")
            wait_emptied(pe, "vc")
            for h in range(4):
                b = open_unit("state", h)
                for d in range(2):
                    for t in range(2):
                        ins = mm(b[:, d * 129:(d + 1) * 129], kw[:, d, t, h * P:(h + 1) * P], vc[:, t, h], t == 0, t == 1)
                close(ins)
            gemm_slot_T(S_O, "o", 0, hT3)
            pe.wait_ge(s["inter_rows"], 1)
            b = open_unit("cols")
            for kind, r in enumerate((3, 0, 2)):
                for d in range(2):
                    for t in range(2):
                        c = kind * 16 + (d * 2 + t) * 4
                        ins = mm(b[:, c:c + 4], rw(r)[:, d * T + t * P:d * T + (t + 1) * P], ident[0:4, 0:4])
            close(ins)
            wait_emptied(pe, "state")
            pe.wait_ge(s["qk_ready"], 6)
            for h in range(HEADS):
                b = open_unit(f"mb{h}")
                close(mm(b[:], sel4[0:4, h * P:(h + 1) * P], rw(4)))
                b = open_unit(f"sT{h}")
                for i in range(2):
                    ins = mm(b[:, i * T:(i + 1) * T], kT[:, h, i * P:(i + 1) * P], qT[:, h])
                close(ins)
                for t in range(2):
                    b = open_unit(f"inter{h}.{t}")
                    close(mm(b[:, 0:258], qT[:, h, t * P:(t + 1) * P], CA[:, h].rearrange("p d c -> p (d c)")))
                    b = open_unit(f"num{h}.{t}")
                    if t == 0:
                        wait_emptied(pe, f"sT{h}")
                    for d in range(2):
                        keys = [i for i in range(2) if (i <= t if d == 0 else i >= t)]
                        for i in keys:
                            ins = mm(b[:, d * 129:(d + 1) * 129], W[:, h % 2, 2 * d + i, t * P:(t + 1) * P], vx[:, i, h],
                                     i == keys[0], i == keys[-1])
                    close(ins)
            gemm_slot_T(S_MERGE, "mergeA", 0, hT3)
            gemm_slot_T(S_MERGE + 1, "mergeA", 2, hT3)
            pe.wait_ge(s["hm_ready"], 1)
            for i in range(2):
                b = open_unit("hT", i)
                for j in range(2):
                    for t in range(2):
                        ins = tr(b[:, j * T + t * P:j * T + t * P + P], hm[:, t * 4 + 2 * i + j])
                close(ins)
            pe.wait_ge(s["conv_done"], 12)
            for o in range(2):
                if o:
                    wait_emptied(pe, "yo0")
                for t in range(2):
                    b = open_unit(f"uT{o}", t)
                    for c in range(4):
                        ins = tr(b[:, c * P:(c + 1) * P], zhy[:, c, t * P:(t + 1) * P])
                    close(ins)
                wait_emptied(pe, f"uT{o}")
                for f in range(2):
                    for q in range(2):
                        b = open_unit(f"uf{o}", 2 * f + q)
                        for t in range(2):
                            ins = mm(b[:], dft[:, q, t, f * P:(f + 1) * P], unat[:, t], t == 0, t == 1)
                        close(ins)
                gemm_slot_T(S_MERGE + 2 + o, f"merge{o}", 0, hT3)
                pe.wait_ge(s["y_spec"], o + 1)
                for i in range(2):
                    b = open_unit(f"yo{o}", i)
                    for j in range(2):
                        n = 0
                        for q in range(2):
                            for f in range(2):
                                ins = mm(b[:, j * T:(j + 1) * T], Y[:, q, f, (2 * i + j) * P:(2 * i + j + 1) * P], dft[:, q, f],
                                         n == 0, n == 3)
                                n += 1
                    close(ins)

            def spread(name, dg):
                for n in range(2):
                    b = open_unit(name, n)
                    for d in range(4):
                        ins = mm(b[:, d * P:(d + 1) * P], ones[:], dg[:, 4 * n + d])
                    close(ins)
            pe.wait_ge(s["bc_diag"], 1)
            spread("bc2", diag)
            arrived(pe, S_BR)
            arrived(pe, S_BR + 1)
            wait_emptied(pe, "yo1")
            wait_emptied(pe, "hT")
            for c in range(4):
                for m, z in ((0, zhy), (1, YB)):
                    gemm_T(f"bra{c}", m, slot(S_BR + m, 4, D), (256 * c, 256 * c + P), z, 4)
            pe.wait_ge(s["merged_ready"], 4)
            for n in range(2):
                arrived(pe, S_OUT + n)
                for t in range(2):
                    gemm_N("out1", 2 * n + t, slot(S_OUT + n, 8, 512), 512, merged, t)

            pe.wait_ge(s["xn2_ready"], 1)
            turn("h2T", xn2)
            pe.wait_ge(s["moe_landed"], 80)
            wait_emptied(pe, "h2T")
            b = open_unit("route")
            for t in range(2):
                for q in range(KD):
                    ins = mm(b[:, t * 16:(t + 1) * 16], hT3[:, q, t * P:(t + 1) * P], w_router[:, q], q == 0, q == KD - 1)
            close(ins)
            pe.wait_ge(s["aff_ready"], 1)
            b = open_unit("affT")
            for t in range(2):
                ins = tr(b[0:16, t * P:(t + 1) * P], affn[:, t])
            close(ins)
            wait_emptied(pe, "affT")
            for i in range(8):
                b = open_unit("affbc", i)
                for q in range(2):
                    e = 2 * i + q
                    ins = mm(b[:, q * T:(q + 1) * T], sel16[:, e * P:(e + 1) * P], affT)
                close(ins)
            pe.wait_ge(s["sel_ready"], 1)
            for d in range(8):
                b = open_unit("gather", d)
                for t in range(2):
                    ins = mm(b[:], xn2[:, t, d * P:(d + 1) * P], sel[:, t], t == 0, t == 1)
                close(ins)
            pe.wait_ge(s["bc_diag"], 2)
            spread("bc5", diag5)
            wait_emptied(pe, "gather")
            wait_emptied(pe, "bc5")

            def expert(e):
                pe.wait_ge(s["xg_copied"], e + 1)
                for c in range(8):
                    n = N_PRE + c
                    pe.wait_ge(landed[n % RING], 32 * (n // RING + 1) + e * (32 * PER_EXPERT // RING))
                    w = slot(n, 2, FF)
                    o = bank[c // 4]
                    for q in range(2):
                        kt_ = 2 * (c % 4) + q
                        for g in range(4):
                            ins = mm(o[32 * g:32 * g + 32, :], xg[:, kt_], w[:, q, 512 * g:512 * g + 512], kt_ == 0, kt_ == 7)
                    ins.then_inc(s["slots_used"], 1)
                pe.wait_ge(s["sg_copied"], e + 1)
                for t in range(2):
                    ins = tr(bank[3][:, t * P:(t + 1) * P], sgs[:, t])
                ins.then_inc(s["sg_turned"], 1)
                pe.wait_ge(s["hact"], e + 1)
                for c in range(4):
                    ins = tr(bank[2][:, c * P:(c + 1) * P], hact[:, c * P:(c + 1) * P])
                ins.then_inc(s["hT_turned"], 1)
                pe.wait_ge(s["hT_evac"], e + 1)
                for r in range(4):
                    n = N_PRE + 8 + r
                    pe.wait_ge(landed[n % RING], 32 * (n // RING + 1) + e * (32 * PER_EXPERT // RING))
                    w = slot(n, 4, D)
                    for c in range(4):
                        for g in range(4):
                            ins = mm(bank[0][32 * g:32 * g + 32, 0:T], hTs[:, c, 32 * r:32 * r + 32], w[:, c, T * g:T * (g + 1)],
                                     r + c == 0, r + c == 6)
                    ins.then_inc(s["slots_used"], 1)
                pe.wait_ge(s["y_evac"], e + 1)
                pe.wait_ge(s["sgT_evac"], e + 1)
                pe.wait_ge(s["acc_done"], e + 1)
                for t in range(2):
                    for g in range(4):
                        ins = mm(bank[4 + g][:, t * T:(t + 1) * T], sgT[32 * g:32 * g + 32, t * P:(t + 1) * P], ysb[32 * g:32 * g + 32])
                ins.then_inc(s["scat_done"], 1)
            with pe.Fori(0, EXPERTS - 1) as e:
                expert(e)
            expert(EXPERTS - 1)

            pe.wait_ge(s["acc_done"], EXPERTS + 1)
            for l in range(DEPTH_2):
                N0 = N_POST + l * PER_LAYER
                if l == 0:
                    pe.wait_ge(s["x1_ready"], 1)
                else:
                    pe.wait_ge(s["x_done"], 4)
                turn(f"xT{l}", x3)
                wait_emptied(pe, f"xT{l}")
                for i in range(5):
                    gemm_slot_T(N0 + O_QKA + i, f"qka{l}", 2 * i, hT3, KD, 512 if i < 4 else 256)
                for i in range(3):
                    n, wd = N0 + O_VA + i, 512 if i < 2 else 128
                    arrived(pe, n)
                    for t in range(2):
                        gemm_N(f"va{l}", 2 * i + t, slot(n, 8, wd), wd, hT3, t)
                wait_emptied(pe, f"qka{l}")
                for j in range(HPG):
                    def qk(h, t):
                        r = AD * (h % 2)
                        return qka[r:r + AD, h // 2, t * P:(t + 1) * P], qka[r:r + AD, 9 + h // 2]
                    b = open_unit(f"score{l}.{j}", 0)
                    for g in range(NG):
                        q_, k_ = qk(HPG * g + j, 0)
                        ins = mm(b[:, g * P:(g + 1) * P], q_, k_[:, 0:P])
                    close(ins)
                    b = open_unit(f"score{l}.{j}", 1)
                    for g in range(2):
                        q_, k_ = qk(HPG * g + j, 1)
                        ins = mm(b[:, g * T:(g + 1) * T], q_, k_)
                    close(ins)
                    b = open_unit(f"score{l}.{j}", 2)
                    q_, k_ = qk(HPG * 2 + j, 1)
                    close(mm(b[:, 0:T], q_, k_))
                    for r in range(2 if j < 4 else 0):
                        n = N0 + O_QKR + 2 * j + r
                        if j < 2:
                            gemm_slot_T(n, f"qkr_v{l}.{j}", 2 * r, hT3)
                        else:
                            arrived(pe, n)
                            for t in range(2):
                                gemm_N(f"qkr_v{l}.{j}", 2 * r + t, slot(n, 8, 512), 512, hT3, t)
                    pe.wait_ge(s["exp_done"], HPG * l + j + 1)
                    for i in range(3):
                        b = open_unit(f"pT{l}.{j}", i)
                        for q in range(3):
                            ins = tr(b[:, q * P:(q + 1) * P], sc[:, 3 * i + q])
                        close(ins)
                    wait_emptied(pe, f"pT{l}.{j}")
                    if j == 0:
                        wait_emptied(pe, f"va{l}")
                    b = open_unit(f"attn{l}.{j}")
                    for t in range(2):
                        terms = [(g, kt_) for g in range(NG) for kt_ in range(t + 1)]
                        for n, (g, kt_) in enumerate(terms):
                            c = (HPG * g + j) * AD
                            blk = g if t == 0 else 3 + 2 * g + kt_
                            ins = mm(b[:, t * AD:(t + 1) * AD], pT[:, blk], va[:, kt_, c:c + AD], n == 0, n == len(terms) - 1)
                    close(ins)
                wait_emptied(pe, f"attn{l}.{HPG - 1}")
                for i in range(2):
                    b = open_unit(f"yaT{l}", i)
                    for q in range(2 - i):
                        for t in range(2):
                            ins = tr(b[:, q * T + t * P:q * T + (t + 1) * P], ya[:, t, (2 * i + q) * P:(2 * i + q + 1) * P])
                    close(ins)
                pe.wait_ge(s["rot_done"], 8 * (l + 1))
                wait_emptied(pe, f"qkr_v{l}.3")
                for h in range(RH):
                    b = open_unit(f"rs{l}.{h}")
                    for kt_ in range(2):
                        o = b[:, 0:T] if kt_ == 0 else b[:, T:T + P]
                        for q in range(2):
                            ins = mm(o, qkr[:, 8 + 2 * h + q, kt_ * P:(kt_ + 1) * P], qkr[:, 2 * h + q, kt_ * P:T], q == 0, q == 1)
                    close(ins)
                    wait_emptied(pe, f"rs{l}.{h}")
                    b = open_unit(f"ro{l}.{h}", 0)
                    close(mm(b[:], pr[:, h % 2, 0:P], vr[:, 0, h * 512:(h + 1) * 512]))
                    b = open_unit(f"ro{l}.{h}", 1)
                    mm(b[:], pr[:, h % 2, P:T], vr[:, 0, h * 512:(h + 1) * 512], True, False)
                    close(mm(b[:], pr[:, h % 2, T:T + P], vr[:, 1, h * 512:(h + 1) * 512], False, True))
                for i in range(4):
                    gemm_slot_T(N0 + O_GATE + i, f"gate{l}", 2 * i, hT3)
                for c in range(8):
                    n = N0 + O_GR + c // 2
                    arrived(pe, n)
                    gemm_T(f"gr{l}.{c}", 0, slot(n, 8, 512), (T * (c % 2), T * (c % 2) + P), hT3)
                    pe.wait_ge(s["yr_ready"], RH * l + c // 2 + 1)
                    b = open_unit(f"yrT{l}.{c}")
                    for q in range(2):
                        for t in range(2):
                            ins = tr(b[:, q * T + t * P:q * T + (t + 1) * P], yr[:, t, (2 * c + q) * P:(2 * c + q + 1) * P])
                    close(ins)
                wait_emptied(pe, f"yaT{l}")
                arrived(pe, N0 + O_ATTN)
                for i in range(4):
                    gemm_T(f"mixA{l}", i, slot(N0 + O_ATTN, 3, D), (256 * i, 256 * i + P), yaT, 3)
                wait_emptied(pe, f"yrT{l}.7")
                for i in range(4):
                    arrived(pe, N0 + O_RET + i)
                    gemm_T(f"mixB{l}", i, slot(N0 + O_RET + i, 16, 256), (0, P), ybT, 16)
                wait_emptied(pe, f"mixB{l}")
                for n in range(2):
                    arrived(pe, N0 + O_OUT + n)
                    for t in range(2):
                        gemm_N(f"mixo{l}", 2 * n + t, slot(N0 + O_OUT + n, 8, 512), 512, merged2, t)
                pe.wait_ge(s["x_done"], 2 if l == 0 else 6)
                turn(f"x2T{l}", x3)
                wait_emptied(pe, f"x2T{l}")
                for i in range(NF // 2):
                    n = N0 + O_FF + i
                    arrived(pe, n)
                    w = slot(n, 16, 256)
                    gemm_T(f"ffg{l}.{i}", 0, w[:, 0:8], (0, P), hT3)
                    gemm_T(f"ffu{l}.{i}", 0, w[:, 8:16], (0, P), hT3)
                wait_emptied(pe, f"ffu{l}.{NF // 2 - 1}")
                banks = [open_unit(f"down{l}", i) for i in range(4)]
                for i in range(6):
                    n, nk = N0 + O_DOWN + i, 4 if i < 5 else 2
                    arrived(pe, n)
                    w = slot(n, nk, D)
                    for u in range(4):
                        c, t = divmod(u, 2)
                        for q in range(nk):
                            kt_ = 4 * i + q
                            ins = mm(banks[u][:], hF[:, kt_, t * P:(t + 1) * P], w[:, q, 512 * c:512 * c + 512], kt_ == 0, kt_ == NF - 1)
                        if i == 5:
                            close(ins)
                    if i < 5:
                        ins.then_inc(s["slots_used"], 1)


def constants():
    f = np.float32
    k = {}
    k["ident"] = np.eye(P, dtype=f)
    n = np.arange(T, dtype=np.float64)
    ang = 2 * np.pi * np.outer(n, n) / NFFT
    cs = np.stack([np.cos(ang), np.sin(ang)])
    k["dft"] = cs.reshape(2, 2, P, T).transpose(2, 0, 1, 3).reshape(P, -1).astype(f)
    w = np.full(T, 2.0 / NFFT)
    w[0] = 1.0 / NFFT
    k["dftw"] = w.reshape(2, P).T.astype(f)
    tt = np.linspace(0.0, 1.0, T, dtype=f)[:, None]
    bands = np.linspace(1e-4, 15, 16, dtype=f)[None, :]
    an = f(2.0 * np.pi / T) * np.arange(T, dtype=f)[:, None] * bands
    k["emb"] = np.concatenate([tt, np.cos(an), np.sin(an)], axis=1).T.astype(f)
    lo, hi = np.log(1e-2) / 1.5, np.log(1e-2) / 0.3
    deltas = np.abs(np.linspace(lo, hi, HYC, dtype=f))
    win = np.exp(-tt * deltas).astype(f)
    win = np.stack([win, win])
    win[1, 0] = 0.0
    k["win"] = win.reshape(2, 2, P, HYC).transpose(2, 0, 1, 3).reshape(P, -1).copy()
    sidx, tidx = np.arange(T)[:, None], np.arange(T)[None, :]
    tri = np.stack([sidx <= tidx, sidx >= tidx]).astype(f)
    k["tri"] = tri.reshape(2, 2, P, T).transpose(2, 0, 1, 3).reshape(P, -1).copy()
    sel = np.zeros((4, 4, P), f)
    for h in range(4):
        sel[h, h] = 1.0
    k["sel4"] = sel.reshape(4, -1)
    ss = np.zeros((P, 2), f)
    for g in range(4):
        ss[32 * g, 0] = ss[32 * g + 1, 1] = 1.0
    k["selsum"] = ss
    dist = 255 - np.arange(384)
    big = np.maximum(dist, 16)
    large = 16 + (np.log(big / 16) / np.log(2048 / 16) * 16).astype(np.int32)
    bucket = np.where(dist < 16, np.maximum(dist, 0), np.minimum(large, 31))
    oh = np.zeros((32, 384), f)
    oh[bucket, np.arange(384)] = (dist >= 0)
    k["onehot"] = oh
    dm = np.zeros((AH, 384), f)
    for gi, (window, dil) in enumerate(((128, 1), (512, 4), (2048, 16))):
        ok = (dist >= 0) & (dist <= window) & (dist % dil == 0)
        dm[gi * HPG:(gi + 1) * HPG] = np.where(ok, 0.0, NEG)
    k["distmask"] = dm
    sel = np.zeros((16, 16, P), f)
    for e in range(16):
        sel[e, e] = 1.0
    k["sel16"] = sel.reshape(16, -1)
    k["ltmask"] = (np.arange(T)[None, :] < np.arange(T)[:, None]).astype(f).reshape(2, P, T).transpose(1, 0, 2).reshape(P, -1).copy()
    k["iota"] = np.tile(np.arange(CAP, dtype=f), (P, 1))
    log_g = np.log(1.0 - 2.0 ** (-5.0 - np.arange(RH)))
    dk = 256
    dec = np.where(tidx >= sidx, np.exp(log_g[:, None, None] * np.maximum(tidx - sidx, 0)), 0.0) * dk ** -0.5
    dec = np.concatenate([dec[:, 0:P, :], dec[:, P:, P:]], axis=2)
    k["decay"] = dec.transpose(1, 0, 2).reshape(P, -1).astype(f)
    inv = f(10000.0) ** (-np.arange(P, dtype=f) / f(P))
    rang = np.arange(T, dtype=f)[None, :] * inv[:, None].astype(f)
    k["rope"] = np.concatenate([np.cos(rang), np.sin(rang)], axis=1).astype(f)
    return k


_INS = """x c ctx c_ctx w_ada b_ada norm_mix_g norm_ffn_g w_in b_in hy_conv hy_f_w1 hy_f_b1 hy_f_w2 hy_f_b2
    hy_f_w3 hy_skip ml_conv ml_norm_g w_branch_hy w_branch_ml w_out w_router w_exp1 w_exp3 w_exp2 final_norm_g
    rel_bias_2 w_in_2 b_in_2 w_attn_proj_2 w_ret_proj_2 w_out_2 ln1_g_2 ln1_b_2 w_ffn_gate_2 w_ffn_up_2
    w_ffn_down_2 ln2_g_2 ln2_b_2""".split()


def kernel(**inputs):
    import concourse.bacc as bacc
    from concourse.bass_utils import run_bass_kernel_spmd

    nc = bacc.Bacc("TRN2", target_bir_lowering=False, num_devices=1)
    arrays, a, k = {}, {}, {}
    for name in _INS:
        v = np.ascontiguousarray(inputs[name])
        arrays[name] = v
        a[name] = nc.dram_tensor(name, v.shape, F32, kind="ExternalInput").ap()
    for name, v in constants().items():
        arrays["const_" + name] = np.ascontiguousarray(v)
        k[name] = nc.dram_tensor("const_" + name, v.shape, F32, kind="ExternalInput").ap()
    out = nc.dram_tensor("out", (1, T, D), F32, kind="ExternalOutput").ap()
    kernel_program(nc, a, k, out)
    r = run_bass_kernel_spmd(nc, [arrays], core_ids=[0])
    return r.results[0]["out"]
```

```python
from contextlib import ExitStack

import numpy as np

import concourse.bass as bass
from concourse import mybir

F32 = mybir.dt.float32
F32R = mybir.dt.float32r
ACT = mybir.ActivationFunctionType
ALU = mybir.AluOpType
AX = mybir.AxisListType

P = 128
T = 256
D = 1024
KD = D // P
DEPTH_2 = 2
RING = 4
XRING = 6
SLOT = 4096
HALF = SLOT // 2
ARENA = 29800
PART_PLACES = ((0, 11520), (11520, 4096), (23936, 768), (26752, 2048))

HYC = 512
HEADS, DH = 4, 128
ML0, GATE0, MERGE0 = 1536, 3584, 3600
EXPERTS, CAP, FF = 16, 32, 2048
NFFT = 511
EPS = 1e-6
BIG = 1e4

AH, AD, NG = 18, 64, 3
HPG = AH // NG
IN2 = 11648
QK_A, V_A, QK_R, V_R, G_R, GATE_2 = 0, 2304, 3456, 5504, 7552, 9600
RH = 4
DFF = 2816
NF = DFF // P
ALPHA = (2 * DEPTH_2) ** 0.25
LN_EPS = 1e-5
NEG = -1e30

C_ADA, C_NMIX, C_NFFN, C_BIN, C_BMERGE = 0, 48, 56, 64, 92
D_HYC, D_MLC, D_MLG, D_C, D_CC, D_HSKIP = 0, 36, 60, 64, 72, 80
E_QKA, E_QKR, E_GG = 0, 18, 34
QKR_AT = (3, 3, 2, 0, 0, 0)
VR_AT = (0, 0, 0, 2, 1, 1)
AHEAD = 2


class Units:

    def __init__(self):
        self.first, self.engine, self.count, self.per = {}, [], [], {"A": 0, "V": 0}

    def add(self, name, n, engines="V"):
        self.first[name] = len(self.engine)
        for i in range(n):
            e = engines[i % len(engines)]
            self.per[e] += 1
            self.engine.append(e)
            self.count.append(self.per[e])

    def at(self, name, i=0):
        return self.first[name] + i


def layer_units(units, l):
    units.add(f"xT{l}", 4, "V")
    units.add(f"qka{l}", 9, "A")
    units.add(f"va{l}", 6, "V")
    for j in range(HPG):
        units.add(f"score{l}.{j}", 3, "V")
        if j:
            units.add(f"attn{l}.{j - 1}", 1, "V")
        if QKR_AT[j]:
            units.add(f"qkr{l}.{j}", QKR_AT[j], "A")
        if VR_AT[j]:
            units.add(f"vr{l}.{j}", 2 * VR_AT[j], "V")
        units.add(f"pT{l}.{j}", 3, "A")
    units.add(f"attn{l}.{HPG - 1}", 1, "V")
    units.add(f"yaT{l}", 2, "V")
    units.add(f"rs{l}.0", 1, "V")
    for h in range(RH):
        if h < RH - 1:
            units.add(f"rs{l}.{h + 1}", 1, "V")
        units.add(f"ro{l}.{h}", 2, "A")
    units.add(f"gate{l}", 8, "A")
    for c in range(8):
        units.add(f"gr{l}.{c}", 1, "A")
        units.add(f"yrT{l}.{c}", 1, "V")
    units.add(f"mixA{l}", 4, "V")
    units.add(f"mixB{l}", 4, "V")
    units.add(f"mixo{l}", 4, "V")
    units.add(f"x2T{l}", 4, "V")
    for c in range(NF // 2):
        units.add(f"ffg{l}.{c}", 1, "A")
        units.add(f"ffu{l}.{c}", 1, "V")
    units.add(f"down{l}", 4, "V")


def plan_units():
    u = Units()
    u.add("packs", 2)
    u.add("sin1", 1)
    u.add("sin2", 1)
    u.add("filt", 8)
    u.add("ada0", 4, "AV")
    u.add("filtK", 8, "AV")
    u.add("adacol0", 1)
    u.add("hx", 4, "AV")
    u.add("hc", 4, "AV")
    u.add("reltab", 1)
    u.add("kx", 2, "A")
    u.add("kc", 2, "A")
    u.add("ada1", 4, "AV")
    u.add("vx", 2)
    u.add("vc", 2)
    u.add("mgate", 1)
    u.add("adacol1", 1)
    u.add("q", 2, "A")
    u.add("ada2", 4, "AV")
    u.add("crow", 2)
    u.add("xrow", 2)
    u.add("hy0", 2, "A")
    u.add("adacol2", 1)
    u.add("wcol", 1)
    u.add("hy1", 2, "A")
    u.add("kcn", 2)
    u.add("hy2", 2, "A")
    u.add("state", 4, "A")
    u.add("o", 2, "A")
    u.add("cols", 1)
    for h in range(HEADS):
        u.add(f"mb{h}", 1)
        u.add(f"sT{h}", 1)
        for t in range(2):
            u.add(f"inter{h}.{t}", 1, "A")
            u.add(f"num{h}.{t}", 1)
    u.add("mergeA", 4, "A")
    u.add("hT", 2)
    for o in range(2):
        u.add(f"uT{o}", 2, "AV")
        u.add(f"uf{o}", 4)
        u.add(f"merge{o}", 2, "A")
        u.add(f"yo{o}", 2)
    u.add("bc2", 2, "AV")
    for c in range(4):
        u.add(f"bra{c}", 2)
    u.add("out1", 4)
    u.add("h2T", 4, "AV")
    u.add("route", 1)
    u.add("bc5", 2, "AV")
    u.add("affT", 1)
    for l in range(DEPTH_2):
        layer_units(u, l)
    return u


def kernel_program(nc, a, k, out):
    U = plan_units()

    with ExitStack() as ctx:
        def sb(name, cols, rows=P):
            return ctx.enter_context(nc.sbuf_tensor(name + "_sb", [rows, cols], F32))

        def sem(name):
            return ctx.enter_context(nc.semaphore(name))

        bank = [ctx.enter_context(nc.psum_tensor(f"bank{i}", [P, 512], F32)) for i in range(8)]
        arena_r = {}
        with ExitStack() as places:
            def part_tensor(name, cols):
                return places.enter_context(nc.sbuf_tensor(name + "_parts", [P, cols], F32R))

            ring_r, hT_r, at = part_tensor("ring", RING * SLOT), part_tensor("hT", KD * T), 0
            for off, size in PART_PLACES:
                if off > at:
                    part_tensor(f"no{off}", off - at)
                arena_r[off] = part_tensor(f"arena{off}", size)
                at = off + size
        ring = sb("ring", RING * SLOT)
        hT = sb("hT", KD * T)
        arena = sb("arena", ARENA)
        x = sb("x", 2 * D)
        ident = sb("ident", P)
        colA = sb("colA", P)
        colB = sb("colB", P)
        colC = sb("colC", 2 * P)
        sm = sb("sm", 640)
        rel_table = nc.dram_tensor("rel_table", (AH, P, 384), F32, kind="Internal").ap()

        def region(off, *dims):
            n = int(np.prod(dims))
            v = arena[:, off:off + n]
            if len(dims) == 2:
                return v.rearrange("p (a b) -> p a b", a=dims[0])
            if len(dims) == 3:
                return v.rearrange("p (a b c) -> p a b c", a=dims[0], b=dims[1])
            if len(dims) == 4:
                return v.rearrange("p (a b c d) -> p a b c d", a=dims[0], b=dims[1], c=dims[2])
            return v

        def parts(off, k):
            base = max(o for o in arena_r if o <= off)
            return arena_r[base][:, off - base:off - base + k * T].rearrange("p (k t) -> p k t", k=k)

        x3 = x[:].rearrange("p (t d) -> p t d", t=2)
        hT3 = hT[:].rearrange("p (k t) -> p k t", k=KD)
        ones = sb("ones", P)

        filtK = region(0, 2, 2, 2, 512)
        filt = region(4096, 2, 2, 2, 512)
        gates = region(4096, 16, T)
        adarow = region(8192, 4, 512)
        zhy = region(8192, 12, T)
        win = region(10240, 2, 2, 512)
        w3 = region(17424, 2048)
        qT = region(11264, 4, T)
        kT = region(12288, 4, T)
        NUM = region(13312, 2, 4, 2, 129)
        ctxn = region(13312, 2, D)
        xn = region(15376, 2, D)
        W = region(15376, 2, 4, T)
        hcT = region(17424, KD, T)
        kw = region(17424, 2, 2, 512)
        Y = region(17424, 2, 2, 512)
        vx = region(19472, 2, 4, 129)
        vc = region(20504, 2, 4, 129)
        unat = region(20504, 2, 512)
        CA = region(21536, 4, 2, 129)
        oT = region(22568, 4, T)
        tri = region(23592, 2, 2, T)
        dft = region(24616, 2, 2, T)
        praw = region(25640, 4, 2, T)
        emb = region(25640, T)
        w1s = region(25896, 64)
        w2s = region(25960, 64)
        sv = region(26024, 4, T)
        sTad = region(27688, 8, 32)
        YB = region(27688, 4, T)
        kcT = region(28712, 4, T)
        Utmp = region(25640, 4, 512)
        merged = region(0, 8, T)
        bc2 = region(2048, D)
        hm = region(25640, 8, P)
        hsq = region(26664, 8, P)
        tmpB = region(28712, 2, 2, 129)
        mtmp = region(21536, 3, 512)
        diag = region(20504, 8, P)

        xn2 = region(4096, 2, D)
        sel = region(6144, 2, CAP)
        aff1 = arena[0:16, 13312:13312 + T]
        ltmask = region(15376, 2, T)
        iota = region(15888, 32)
        w_router = region(15920, KD, 16)
        fnorm = region(16048, D)
        acc = region(21552, 2, D)
        sgs = region(23616, 2, P)
        sgT = region(23872, T)
        xg = region(24128, KD, CAP)
        sact = region(24616, 512)
        hact = region(25128, 512)
        hTs = region(25640, 4, P)
        ysb = region(26152, T)
        affn = region(26408, 2, 16)
        rank = region(26440, 2, 2)
        affT = arena[0:16, 26504:26760]
        diag5 = region(26760, 8, P)
        bc5 = region(27784, D)
        rjunk = region(0, 4, T)

        qka = region(0, 18, T)
        va = region(4608, 2, AH * AD)
        relB = region(6912, AH, T)
        qkr = region(11520, 16, T)
        vr = region(15616, 2, 2048)
        sc = region(19712, 9, P)
        vbias_a = region(19712, AH * AD)
        rraw = region(20864, 2, T)
        rm1 = region(21376, 2, T)
        pT = region(22016, 9, P)
        ya = region(23168, 2, 384)
        decay = region(24704, RH, 384)
        rope = region(26240, 2, T)
        rm2 = region(28800, 2, T)
        yr = region(0, 2, 2048)
        merged2 = region(8704, 8, T)
        ln1 = region(11520, 2, D)
        ln2 = region(13568, 2, D)
        gates2 = region(15616, 16, T)
        pr = region(19712, 2, 384)
        gtmp = region(20864, 2, 512)
        btmp = region(22016, 2, 512)
        hTp = (hT_r[:].rearrange("p (k t) -> p k t", k=KD), parts(26752, KD))
        yaTp = (parts(23936, 3), parts(10752, 3))
        ybTp = (parts(4608, 16), parts(11520, 16))
        mergedp = (parts(0, 8), parts(8704, 8))
        hFp = (parts(0, NF), parts(NF * T, NF))

        relbuf = arena[0:AH, 28712:29096]
        distmask = arena[0:AH, 21536:21920]
        onehot = arena[0:32, 21920:22304]
        rel_bias = arena[0:32, 22304:22322]
        skipb = arena[0:1, 22336:23360]
        adacol = sb("adacol", 96)
        adaT = adacol[:].rearrange("p (j s) -> p j s", s=2)
        gcol = sb("gcol", 32)
        rows = arena[0:4, 4096:4096 + 3136]
        gl = sb("gl", 64 + 32 + 32)
        cst = sb("cst", 8)
        mcols = sb("mcols", 48 + 16)
        w_gate = sb("w_gate", KD * 16)
        b_rows = sb("b_rows", 512 + 16)
        dftw = sb("dftw", 2)
        selsum = sb("selsum", 2)
        sel4 = sb("sel4", 512, 4)
        fb = sb("fb", 2, 64)

        def rw(i):
            return rows[0:4, i * 512:(i + 1) * 512]

        rsm = rows[0:4, 3072:3136]
        G4 = gl[:, 0:64].rearrange("p (s k h) -> p s k h", s=4, k=4)
        nlf = gl[:, 64:96].rearrange("p (s d h) -> p s d h", s=4, d=2)
        wk = gl[:, 96:128].rearrange("p (s d h) -> p s d h", s=4, d=2)

        def spread_row(ap, off, n):
            return bass.AP(ap.tensor, off, [[0, P], [1, n]])

        first_loads = [(ident[:], k["ident"]), (colB[0:80], a["pack_b"]), (colA[0:108], a["pack_a"]),
                       (colC[0:66].rearrange("p (l c) -> p l c", l=2), a["pack_c"].rearrange("l p c -> p l c"))]
        filter_loads = [
            (emb[0:33], k["emb"]), (w1s[0:33], a["hy_f_w1"][0]),
            (fb[:, 0:1], a["hy_f_b1"].rearrange("a b -> b a")), (fb[:, 1:2], a["hy_f_b2"].rearrange("a b -> b a")),
            (w2s[0:64], a["hy_f_w2"][0]), (w3[0:64], a["hy_f_w3"][0]),
            (skipb, a["hy_skip"].rearrange("a o c -> a (o c)")),
        ]
        window_loads = [
            (x3, a["x"][0].rearrange("(t p) d -> p t d", p=P)),
            (win.rearrange("p a b c -> p (a b c)"), k["win"]),
        ]
        table_loads = [
            (dft.rearrange("p a b c -> p (a b c)"), k["dft"]), (dftw[:], k["dftw"]),
        ]
        other_loads = [
            (selsum[:], k["selsum"]),
            (ctxn, a["ctx"][0].rearrange("(t p) d -> p t d", p=P)),
            (distmask, k["distmask"]), (onehot, k["onehot"]), (rel_bias, a["rel_bias_2"]),
            (tri.rearrange("p a b c -> p (a b c)"), k["tri"]), (sel4[:], k["sel4"]),
            (w_gate[:].rearrange("p (k c) -> p k c", k=KD),
             a["w_in"][0].rearrange("(k p) c -> p k c", p=P)[:, :, GATE0:MERGE0]),
            (b_rows[:, 0:512], spread_row(a["b_in"], ML0 + 1024, 512)),
            (b_rows[:, 512:528], spread_row(a["b_in"], GATE0, 16)),
        ]

        names = """x_landed packs_landed tables_landed filt_landed small_landed cst_set x_norm ctx_norm filt_sum sin_arg1
            sin_arg2 sin1_ready sin2_ready silu_c cols_ready conv_done qk_ready vaug_ones lf_ready
            m_ready softplus_arg softplus_l w_row_arg w_row inter_arg inter_rows w_arg w_exp hm_ready
            y_spec merged_ready bc_diag dve_step act_step var_ready sqrt_ready unit_done freed_act
            freed_dve rel_saved rel_ready moe_landed xn2_ready x1_ready aff_ready rank_ready sel_ready
            row_masked row_spread gathered slots_used xg_copied xg_scaled sg_copied hact a_read hT_evac
            sgT_evac y_evac scat_done acc_done lay_landed vr_landed ln1_landed ln2_landed hi_ready
            lo_ready x_hi prod_split out_saved y_ready exp_done x_done rot_done yr_ready sc_ready
            soft_arg sg_turned hT_turned aff_exp""".split()
        s = {n: sem(n) for n in names}
        landed = [sem(f"slot{i}_landed") for i in range(RING)]
        expert_landed = [sem(f"expert{i}_landed") for i in range(XRING)]
        half_landed = [sem(f"half{i}_landed") for i in range(RING)]

        def w_cols(w, c0, width):
            v = w.rearrange("(k p) c -> p k c", p=P)[:, :, c0:c0 + width]
            h = v.shape[1] // 2
            return [((0, h * width), v[:, 0:h]), ((h * width, (v.shape[1] - h) * width), v[:, h:])]

        def w_rows(w, r0, nk):
            v = w[r0:r0 + nk * P].rearrange("(k p) c -> p k c", p=P)
            h = (nk + 1) // 2
            return [((0, h * D), v[:, 0:h]), ((h * D, (nk - h) * D), v[:, h:])]

        w_in, w_ada = a["w_in"][0], a["w_ada"][0]
        slots = []

        def ada_slots(batch):
            for i in range(4):
                slots.append((w_cols(w_ada, 512 * (4 * batch + i), 512), U.at(f"ada{batch}", i)))

        ada_slots(0)
        slots.append((w_cols(w_in, ML0 + 512, 512), U.at("kc", 1)))
        ada_slots(1)
        slots.append((w_cols(w_in, ML0 + 1024, 512), U.at("vc", 1)))
        slots.append((w_cols(w_in, ML0, 512), U.at("q", 1)))
        ada_slots(2)
        for c0, last in ((0, U.at("hy0", 1)), (512, U.at("hy1", 1)), (1024, U.at("hy2", 1)),
                         (ML0 + 1536, U.at("o", 1)),
                         (MERGE0, U.at("mergeA", 1)), (MERGE0 + 512, U.at("mergeA", 3)),
                         (MERGE0 + 1024, U.at("merge0", 1)), (MERGE0 + 1536, U.at("merge1", 1))):
            slots.append((w_cols(w_in, c0, 512), last))
        slots.append((w_rows(a["w_branch_hy"][0], 0, 4), U.at("bra3", 1)))
        slots.append((w_rows(a["w_branch_ml"][0], 0, 4), U.at("bra3", 1)))
        slots.append((w_cols(a["w_out"][0], 0, 512), U.at("out1", 1)))
        slots.append((w_cols(a["w_out"][0], 512, 512), U.at("out1", 3)))
        N_PRE = len(slots)
        S_ADA, S_KC, S_V, S_Q, S_HY, S_O, S_MERGE, S_BR, S_OUT = (0, 5, 11), 4, 9, 10, 15, 18, 19, 23, 25
        E1 = a["w_exp1"][0].rearrange("e (k p) f -> e p k f", p=P)
        E3 = a["w_exp3"][0].rearrange("e (k p) f -> e p k f", p=P)
        E2 = a["w_exp2"][0].rearrange("e (k p) f -> e p k f", p=P)
        PER_EXPERT = 12
        N_POST = N_PRE + PER_EXPERT * EXPERTS
        def expert_slot(c, *dims):
            i = c % XRING
            if i < RING:
                o = ((N_PRE + i) % RING) * SLOT
                v = ring[:, o:o + SLOT]
            else:
                v = region((7168, 17424)[i - RING], SLOT)
            return v.rearrange("p (k c) -> p k c", k=dims[0])

        halves, half_at, n_part = [], {}, 0

        def add_half(key, src, unit, part=False):
            nonlocal n_part
            half_at.setdefault(key, len(halves))
            n_part += part
            halves.append((src, tuple(src.shape[1:]), unit, n_part if part else None))

        def add_chunks(key, w, c0, width, unit):
            v = w.rearrange("(k p) c -> p k c", p=P)[:, :, c0:c0 + width]
            if width < 512:
                add_half(key, v, unit)
            else:
                add_half(key, v[:, 0:4], unit, True)
                add_half(key, v[:, 4:8], unit)

        def columns(w, c0, width):
            return w.rearrange("(k p) c -> p k c", p=P)[:, :, c0:c0 + width]

        for l in range(DEPTH_2):
            w2 = a["w_in_2"][l]
            for i in range(9):
                add_half(("qka", l), columns(w2, QK_A + 256 * i, 256), U.at(f"qka{l}", i))
            for i in range(3):
                add_chunks(("va", l), w2, V_A + 512 * i, 512 if i < 2 else 128, U.at(f"va{l}", 2 * i + 1))
            nq = nv = 0
            for j in range(HPG):
                for i in range(QKR_AT[j]):
                    add_half(("qkr", l, j), columns(w2, QK_R + 256 * nq, 256), U.at(f"qkr{l}.{j}", i))
                    nq += 1
                for i in range(VR_AT[j]):
                    add_chunks(("vr", l, j), w2, V_R + 512 * nv, 512, U.at(f"vr{l}.{j}", 2 * i + 1))
                    nv += 1
            for i in range(8):
                add_half(("gate", l), columns(w2, GATE_2 + 256 * i, 256), U.at(f"gate{l}", i))
            for i in range(8):
                add_half(("gr", l), columns(w2, G_R + 256 * i, 256), U.at(f"gr{l}.{i}"))
            for i in range(2):
                add_half(("mixA", l), columns(a["w_attn_proj_2"][l], 512 * i, 512), U.at(f"mixA{l}", 2 * i + 1))
            for i in range(8):
                add_half(("mixB", l), columns(a["w_ret_proj_2"][l], P * i, P), U.at(f"mixB{l}", i // 2), i % 2 == 0)
            for i in range(2):
                add_chunks(("mixo", l), a["w_out_2"][l], 512 * i, 512, U.at(f"mixo{l}", 2 * i + 1))
            for i in range(NF // 2):
                add_half(("ff", l), columns(a["w_ffn_gate_2"][l], 256 * i, 256), U.at(f"ffg{l}.{i}"))
                add_half(("ff", l), columns(a["w_ffn_up_2"][l], 256 * i, 256), U.at(f"ffu{l}.{i}"))
            for i in range(NF // 2):
                src = a["w_ffn_down_2"][l][2 * P * i:2 * P * (i + 1)].rearrange("(k p) c -> p k c", p=P)
                add_half(("down", l), src, U.at(f"down{l}", 3), i < NF // 2 - 1)

        def halves_by(name, i=0):
            return sum(h[2] <= U.at(name, i) for h in halves)

        def half(n, t=ring):
            o, (kk, c) = ((N_POST + n) % RING) * SLOT, halves[n][1]
            return tuple(t[:, b:b + kk * c].rearrange("p (k c) -> p k c", k=kk) for b in (o, o + HALF))

        def slot(n, *dims):
            o = (n % RING) * SLOT
            v = ring[:, o:o + int(np.prod(dims))]
            return v.rearrange("p (k c) -> p k c", k=dims[0])

        def arrived(eng, n):
            eng.wait_ge(landed[n % RING], 32 * (n // RING + 1))

        freed = {"A": s["freed_act"], "V": s["freed_dve"]}

        def wait_emptied(eng, name, n=None):
            last = {}
            i0 = U.first[name]
            total = n
            if total is None:
                later = [f for f in U.first.values() if f > i0]
                total = (min(later) if later else len(U.engine)) - i0
            for u in range(i0, i0 + total):
                last[U.engine[u]] = U.count[u]
            for e, v in last.items():
                eng.wait_ge(freed[e], v)

        block = ctx.enter_context(nc.Block())

        @block.sync
        def _(sp):
            def load(n, parts):
                for (off, size), src in parts:
                    o = (n % RING) * SLOT + off
                    dst = ring[:, o:o + size]
                    if len(src.shape) == 3:
                        dst = dst.rearrange("p (k c) -> p k c", k=src.shape[1])
                    sp.dma_start(dst, src).then_inc(landed[n % RING], 16)

            for dst, src in first_loads:
                sp.dma_start(dst, src).then_inc(s["packs_landed"], 16)
            for dst, src in filter_loads:
                sp.dma_start(dst, src).then_inc(s["filt_landed"], 16)
            for dst, src in window_loads:
                sp.dma_start(dst, src).then_inc(s["x_landed"], 16)
            for n, (parts, last) in enumerate(slots):
                if n >= RING:
                    sp.wait_ge(s["unit_done"], slots[n - RING][1] + 1)
                load(n, parts)

            def expert_load(e, c):
                w, r = ((E1, c), (E3, c - 4), (E2, c - 8))[c // 4]
                n = 2 if c < 8 else 4
                src = w[e, :, n * r:n * r + n]
                m = n // 2
                for h in range(2):
                    sp.dma_start(expert_slot(c, n)[:, h * m:(h + 1) * m],
                                 src[:, h * m:(h + 1) * m]).then_inc(expert_landed[c % XRING], 16)

            for c in range(XRING):
                sp.wait_ge(s["unit_done"], slots[min(N_PRE - RING + c, N_PRE - 1)][1] + 1)
                expert_load(0, c)
            for c in range(XRING, 8):
                sp.wait_ge(s["slots_used"], c - XRING + 1)
                expert_load(0, c)
            with sp.Fori(0, EXPERTS - 1) as e:
                for c in range(8, PER_EXPERT + 8):
                    sp.wait_ge(s["slots_used"], e * PER_EXPERT + (c - XRING + 1))
                    expert_load(e + (c // PER_EXPERT), c % PER_EXPERT)
            for c in range(8, PER_EXPERT):
                sp.wait_ge(s["slots_used"], (EXPERTS - 1) * PER_EXPERT + c - XRING + 1)
                expert_load(EXPERTS - 1, c)
            for n, (src, _, _, _) in enumerate(halves):
                if n < RING:
                    sp.wait_ge(s["slots_used"], EXPERTS * PER_EXPERT - XRING + 1 + n)
                elif halves[n - RING][3]:
                    sp.wait_ge(s["slots_used"], EXPERTS * PER_EXPERT + halves[n - RING][3])
                else:
                    sp.wait_ge(s["unit_done"], halves[n - RING][2] + 1)
                sp.dma_start(half(n)[0], src).then_inc(half_landed[n % RING], 16)
                for l in range(DEPTH_2):
                    i = n - half_at["qka", l] - RING
                    if i == 0:
                        sp.dma_start(vbias_a, spread_row(a["b_in_2"], l * IN2 + V_A, AH * AD)).then_inc(s["lay_landed"], 16)
                        if l == 0:
                            sp.wait_ge(s["rel_saved"], 16)
                    if 1 <= i <= 3:
                        h = HPG * (i - 1)
                        src = bass.AP(rel_table.tensor, 127 + h * P * 384, [[383, P], [P * 384, HPG], [1, T]])
                        sp.dma_start(relB[:, h:h + HPG], src).then_inc(s["lay_landed"], 16)
                    if i == 4:
                        src = bass.AP(a["b_in_2"].tensor, l * IN2 + V_R, [[0, P], [0, 2], [1, 2048]])
                        sp.dma_start(vr, src).then_inc(s["vr_landed"], 16)
                    if i == 5 and l == 0:
                        sp.dma_start(decay.rearrange("p h t -> p (h t)"), k["decay"]).then_inc(s["vr_landed"], 16)
                        sp.dma_start(rope.rearrange("p c t -> p (c t)"), k["rope"]).then_inc(s["vr_landed"], 16)
                    if n == half_at["mixo", l] + RING - 1:
                        for dst, w in ((ln1[:, 0], "ln1_g_2"), (ln1[:, 1], "ln1_b_2")):
                            sp.dma_start(dst, spread_row(a[w], l * D, D)).then_inc(s["ln1_landed"], 16)
                    if n == half_at["ff", l] + RING:
                        for dst, w in ((ln2[:, 0], "ln2_g_2"), (ln2[:, 1], "ln2_b_2")):
                            sp.dma_start(dst, spread_row(a[w], l * D, D)).then_inc(s["ln2_landed"], 16)
            for h in range(2):
                sp.wait_ge(s["y_ready"], h + 1)
                sp.dma_start(out[0].rearrange("(t p) d -> p t d", p=P)[:, :, 512 * h:512 * h + 512],
                             x3[:, :, 512 * h:512 * h + 512]).then_inc(s["out_saved"], 16)
            sp.wait_ge(s["out_saved"], 32)
            sp.wait_ge(s["rel_saved"], 16)

        @block.gpsimd
        def _(pool):
            g = nc.gpsimd
            g.memset(sTad, 0.0)
            g.memset(ones[:], 1.0)
            g.memset(cst[:, 0:1], EPS)
            g.memset(cst[:, 1:2], 1.0).then_inc(s["cst_set"], 1)
            for dst, src in other_loads:
                g.dma_start(dst, src).then_inc(s["small_landed"], 16)
            pool.wait_ge(s["unit_done"], U.at("filt", 7) + 1)
            g.memset(vx[:, :, :, 128:129], 1.0)
            g.memset(vc[:, :, :, 128:129], 1.0).then_inc(s["vaug_ones"], 1)
            pool.wait_ge(s["rel_ready"], 1)
            g.dma_start(rel_table, relbuf.unsqueeze(1).broadcast_to([AH, P, 384])).then_inc(s["rel_saved"], 16)
            pool.wait_ge(s["unit_done"], U.at("hT", 1) + 1)
            for dst, src in ((ltmask.rearrange("p t s -> p (t s)"), k["ltmask"]), (iota, k["iota"]),
                             (w_router, a["w_router"][0].rearrange("(k p) c -> p k c", p=P)),
                             (fnorm, spread_row(a["final_norm_g"], 0, D))):
                g.dma_start(dst, src).then_inc(s["moe_landed"], 16)
            for n in range(len(halves)):
                pool.wait_ge(s["hi_ready"], n + 1)
                low, high = half(n, ring_r)
                g.tensor_tensor(low, half(n)[0], high.bitcast(F32), ALU.subtract).then_inc(s["lo_ready"], 1)

        @block.scalar
        def _(act):
            A = nc.scalar
            chain = [0]

            def link(ins):
                chain[0] += 1
                ins.then_inc(s["act_step"], 1)
                act.wait_ge(s["act_step"], chain[0])

            def take(name, i=0):
                u = U.at(name, i)
                assert U.engine[u] == "A", name
                act.wait_ge(s["unit_done"], u + 1)
                return bank[u % 8]

            def give(ins):
                ins.then_inc(s["freed_act"], 1)

            def root(k, dst, src):
                act.wait_ge(s["var_ready"], k)
                A.activation(dst, src, ACT.Sqrt).then_inc(s["sqrt_ready"], 1)

            for dst, src in table_loads:
                act.dma_start(dst, src).then_inc(s["tables_landed"], 16)
            act.wait_ge(s["cst_set"], 1)
            act.wait_ge(s["cols_ready"], 1)
            A.activation(sTad[:, :, 0], colB[:, D_C:D_C + 8], ACT.Silu)
            A.activation(sTad[:, :, 1], colB[:, D_CC:D_CC + 8], ACT.Silu).then_inc(s["silu_c"], 1)
            act.wait_ge(s["filt_landed"], 16 * len(filter_loads))
            act.wait_ge(s["sin_arg1"], 1)
            A.activation(sv[0:64, 1], sv[0:64, 0], ACT.Sin).then_inc(s["sin1_ready"], 1)
            act.wait_ge(s["sin_arg2"], 1)
            A.activation(sv[0:64, 3], sv[0:64, 2], ACT.Sin).then_inc(s["sin2_ready"], 1)

            def ada_rows(batch):
                for i in range(4):
                    if U.engine[U.at(f"ada{batch}", i)] == "A":
                        b = take(f"ada{batch}", i)
                        if batch:
                            act.wait_ge(s["unit_done"], U.at(f"adacol{batch - 1}") + 1)
                        give(A.copy(adarow[:, i], b[:]))
            ada_rows(0)
            root(1, sm[:, 8:12], sm[:, 4:8])
            act.wait_ge(s["tables_landed"], 16 * len(table_loads))
            for i in range(8):
                if U.engine[U.at("filtK", i)] == "A":
                    b = take("filtK", i)
                    o, f, q = i // 4, (i // 2) % 2, i % 2
                    give(A.activation(filtK[:, o, q, f], b[:], ACT.Identity, scale=dftw[:, f:f + 1]))

            def modulate(name, dst3, g0, src, sh0=0):
                act.wait_ge(s["m_ready"], 1)
                for i in range(4):
                    if U.engine[U.at(name, i)] == "A":
                        b = take(name, i)
                        for j in range(2):
                            d = 2 * i + j
                            ins = A.activation(dst3[:, d], b[:, j * T:(j + 1) * T], ACT.Identity,
                                               scale=gcol[:, g0 + d:g0 + d + 1], bias=adaT[:, sh0 + d, src:src + 1])
                        give(ins)
            modulate("hx", hT3, 0, 0)
            modulate("hc", hcT, 8, 1)

            def raw(name, n, tile0, k):
                for i in range(n):
                    b = take(name, i)
                    if k + i >= 4:
                        act.wait_ge(s["conv_done"], k + i - 3)
                    for j in range(2):
                        c = C_BIN + tile0 + 2 * i + j
                        ins = A.activation(praw[:, (k + i) % 4, j], b[:, j * T:(j + 1) * T], ACT.Identity,
                                           bias=colA[:, c:c + 1])
                    ins.then_inc(s["freed_act"], 1)

            def silu_conv(k, dst):
                act.wait_ge(s["conv_done"], k + 1)
                A.activation(dst, dst, ACT.Silu).then_inc(s["qk_ready"], 1)

            raw("kx", 2, 16, 0)
            raw("kc", 2, 16, 2)
            ada_rows(1)
            silu_conv(0, kT[:, 0:2])
            silu_conv(1, kT[:, 2:4])
            silu_conv(2, kcT[:, 0:2])
            silu_conv(3, kcT[:, 2:4])
            raw("q", 2, 12, 4)
            act.wait_ge(s["softplus_arg"], 1)
            link(A.activation(gl[:, 96:128], gl[:, 96:128], ACT.Exp, scale=-1.0))
            A.activation(gl[:, 96:128], gl[:, 96:128], ACT.Ln, bias=cst[:, 1:2]).then_inc(s["softplus_l"], 1)
            silu_conv(4, qT[:, 0:2])
            silu_conv(5, qT[:, 2:4])
            ada_rows(2)
            act.wait_ge(s["w_row_arg"], 1)
            for d in range(2):
                ins = A.activation(rw(5)[:, d * T:(d + 1) * T], rw(1)[:, d * T:(d + 1) * T], ACT.Exp,
                                   bias=rsm[:, 2 + d:3 + d])
            ins.then_inc(s["w_row"], 1)
            raw("hy0", 2, 0, 6)
            raw("hy1", 2, 4, 8)
            act.wait_ge(s["inter_arg"], 1)
            for d in range(2):
                A.activation(rw(0)[:, d * T:(d + 1) * T], rw(4)[:, d * T:(d + 1) * T], ACT.Exp, scale=-1.0,
                             bias=rsm[:, 4 + d:5 + d])
            A.activation(rw(2), rw(2), ACT.Exp).then_inc(s["inter_rows"], 1)
            raw("hy2", 2, 8, 10)
            for i in range(4):
                b = take("state", i)
                give(A.copy(CA[:, i].rearrange("p d c -> p (d c)"), b[:, 0:258]))
            for i in range(2):
                b = take("o", i)
                for j in range(2):
                    c = C_BIN + 24 + 2 * i + j
                    ins = A.activation(oT[:, 2 * i + j], b[:, j * T:(j + 1) * T], ACT.Sigmoid, bias=colA[:, c:c + 1])
                give(ins)
            act.wait_ge(s["cols_ready"], 2)
            for h in range(HEADS):
                act.wait_ge(s["w_arg"], h + 1)
                A.activation(W[:, h % 2], W[:, h % 2], ACT.Exp, scale=-1.0).then_inc(s["w_exp"], 1)
                for t in range(2):
                    b = take(f"inter{h}.{t}")
                    if h:
                        act.wait_ge(s["freed_dve"], U.count[U.at(f"num{h - 1}.{t}")])
                    for d in range(2):
                        c = 16 + (d * 2 + t) * 4 + h
                        ins = A.activation(tmpB[:, t, d], b[:, d * 129:(d + 1) * 129], ACT.Identity,
                                           scale=mcols[:, c:c + 1])
                    give(ins)

            def merge_gates(name, n, g0):
                for i in range(n):
                    b = take(name, i)
                    for j in range(2):
                        m = g0 + 2 * i + j
                        ins = A.activation(gates[:, m], b[:, j * T:(j + 1) * T], ACT.Sigmoid,
                                           bias=colA[:, C_BMERGE + m:C_BMERGE + m + 1])
                    give(ins)
            merge_gates("mergeA", 4, 0)
            root(2, sm[:, 40:48], sm[:, 32:40])
            for o in range(2):
                b = take(f"uT{o}", 0)
                if o == 0:
                    wait_emptied(act, "cols")
                    wait_emptied(act, "state")
                else:
                    act.wait_ge(s["unit_done"], U.at("uf0", 3) + 1)
                give(A.copy(unat[:, 0], b[:]))
                merge_gates(f"merge{o}", 2, 8 + 4 * o)
            act.wait_ge(s["unit_done"], U.at("yo1", 1) + 1)
            give(A.copy(bc2[:, 0:512], take("bc2", 0)[:]))

            root(3, sm[:, 8:10], sm[:, 4:6])
            modulate("h2T", hT3, 16, 0, 24)
            act.wait_ge(s["soft_arg"], 1)
            A.activation(affn.rearrange("p t e -> p (t e)"), affn.rearrange("p t e -> p (t e)"), ACT.Exp).then_inc(s["aff_exp"], 1)
            give(A.copy(bc5[:, 0:512], take("bc5", 0)[:]))

            def expert(e):
                act.wait_ge(s["slots_used"], e * PER_EXPERT + 4)
                A.activation(sact, bank[0][:], ACT.Silu).then_inc(s["a_read"], 1)
                act.wait_ge(s["slots_used"], e * PER_EXPERT + 12)
                A.copy(ysb, bank[0][:, 0:T]).then_inc(s["y_evac"], 1)
            with act.Fori(0, EXPERTS - 1) as e:
                expert(e)
            expert(EXPERTS - 1)
            high_made = [0]

            def high_parts(count):
                for n in range(high_made[0], min(count, len(halves))):
                    act.wait_ge(half_landed[n % RING], 16 * (n // RING + 1))
                    A.copy(half(n, ring_r)[1], half(n)[0]).then_inc(s["hi_ready"], 1)
                high_made[0] = max(high_made[0], count)

            root(4, sm[:, 8:10], sm[:, 4:6])

            nroot = [4]

            def take2(name, i=0):
                high_parts(halves_by(name, i) + AHEAD)
                return take(name, i)

            def next_root(n):
                nroot[0] += 1
                root(nroot[0], sm[:, 8:8 + n], sm[:, 0:n])

            def high_x(name):
                for i in range(4):
                    u = U.at(name, i)
                    act.wait_ge(s["unit_done"], u + 1)
                    A.copy(hTp[0][:, 2 * i:2 * i + 2].rearrange("p k t -> p (k t)"), bank[u % 8][:]).then_inc(s["x_hi"], 1)

            high_parts(AHEAD)
            for l in range(DEPTH_2):
                high_x(f"xT{l}")
                for i in range(9):
                    b = take2(f"qka{l}", i)
                    for j in range(2):
                        m = 2 * i + j
                        c = l * P + E_QKA + m
                        ins = A.activation(qka[:, m], b[:, j * T:(j + 1) * T], ACT.Identity, bias=colC[:, c:c + 1])
                    give(ins)
                high_parts(halves_by(f"va{l}", 5) + AHEAD)
                for j in range(HPG):
                    def softmax_exp():
                        act.wait_ge(s["sc_ready"], HPG * l + j + 1)
                        A.activation(sc[:, 0:3], sc[:, 0:3], ACT.Exp, bias=sm[:, 58:59], accum_out=sm[:, 60:61])
                        A.activation(sc[:, 3:9], sc[:, 3:9], ACT.Exp, bias=sm[:, 59:60],
                                     accum_out=sm[:, 61:62]).then_inc(s["exp_done"], 1)
                    softmax_exp()
                    for i in range(QKR_AT[j]):
                        b = take2(f"qkr{l}.{j}", i)
                        n = 8 * l + sum(QKR_AT[:j]) + i
                        if n:
                            act.wait_ge(s["rot_done"], n)
                        for q in range(2):
                            c = l * P + E_QKR + 2 * (sum(QKR_AT[:j]) + i) + q
                            ins = A.activation(rraw[:, q], b[:, q * T:(q + 1) * T], ACT.Identity, bias=colC[:, c:c + 1])
                        give(ins)
                    for i in range(3):
                        b = take2(f"pT{l}.{j}", i)
                        give(A.copy(pT[:, 3 * i:3 * i + 3].rearrange("p k t -> p (k t)"), b[:, 0:384]))
                for h in range(RH):
                    for t in range(2):
                        give(A.copy(yr[:, t, h * 512:(h + 1) * 512], take(f"ro{l}.{h}", t)[:]))
                for i in range(8):
                    b = take2(f"gate{l}", i)
                    for q in range(2):
                        c = l * P + E_GG + 16 + 2 * i + q
                        ins = A.activation(gates2[:, 2 * i + q], b[:, q * T:(q + 1) * T], ACT.Sigmoid, bias=colC[:, c:c + 1])
                    give(ins)
                    if i == 3:
                        next_root(8)
                for i in range(8):
                    b = take2(f"gr{l}.{i}")
                    if i >= 2:
                        act.wait_ge(s["freed_dve"], U.count[U.at(f"yrT{l}.{i - 2}")])
                    for q in range(2):
                        c = l * P + E_GG + 2 * i + q
                        ins = A.activation(gtmp[:, i % 2, q * T:(q + 1) * T], b[:, q * T:(q + 1) * T], ACT.Silu, bias=colC[:, c:c + 1])
                    give(ins)
                high_parts(halves_by(f"mixo{l}", 3) + AHEAD)
                next_root(2)
                high_x(f"x2T{l}")
                for i in range(NF // 2):
                    b = take2(f"ffg{l}.{i}")
                    if i >= 2:
                        act.wait_ge(s["freed_dve"], U.count[U.at(f"ffu{l}.{i - 2}")])
                    give(A.activation(gtmp[:, i % 2], b[:], ACT.Silu))
                high_parts(halves_by(f"down{l}", 3) + AHEAD)
                next_root(2)

        @block.vector
        def _(dve):
            V = nc.vector
            chain = [0]

            def link(ins):
                chain[0] += 1
                ins.then_inc(s["dve_step"], 1)
                dve.wait_ge(s["dve_step"], chain[0])

            def take(name, i=0):
                u = U.at(name, i)
                assert U.engine[u] == "V", name
                dve.wait_ge(s["unit_done"], u + 1)
                return bank[u % 8]

            def give(ins):
                ins.then_inc(s["freed_dve"], 1)

            def tt(o, i0, i1, op=ALU.mult):
                return V.tensor_tensor(o, i0, i1, op)

            def stt(o, i0, sc, i1, op0, op1):
                return V.scalar_tensor_tensor(o, i0, sc, i1, op0, op1)

            def inv_root(k, var, rt, inv):
                dve.wait_ge(s["sqrt_ready"], k)
                link(V.reciprocal(inv, rt))

            b = take("packs", 0)
            V.tensor_copy(colB[:, 0:80], b[:, P:P + 80])
            V.tensor_copy(colA[:, 0:108], b[:, 0:108]).then_inc(s["freed_dve"], 1)
            b = take("packs", 1)
            dve.wait_ge(s["freed_dve"], 1)
            dve.sem_inc(s["cols_ready"], 1)
            give(V.tensor_copy(colC[:].rearrange("p (l c) -> p l c", l=2)[:, :, 0:66],
                               b[:, 0:2 * P].rearrange("p (l c) -> p l c", l=2)[:, :, 0:66]))
            dve.wait_ge(s["filt_landed"], 16 * len(filter_loads))

            def sine_arg(b, col, dst, tmp):
                magic, c1 = 12582912.0, 6.28125
                c2 = 2 * np.pi - c1
                link(V.tensor_scalar(dst, b, fb[:, col:col + 1], None, ALU.add))
                link(V.tensor_scalar(tmp, dst, 1 / (2 * np.pi), magic, ALU.mult, ALU.add))
                link(V.tensor_scalar(tmp, tmp, -magic, None, ALU.add))
                link(stt(dst, tmp, -c1, dst, ALU.mult, ALU.add))
                link(stt(dst, tmp, -c2, dst, ALU.mult, ALU.add))
                return V.tensor_scalar(dst, dst, 3.1415925, -3.1415925, ALU.min, ALU.max)

            b = take("sin1")
            link(sine_arg(b[0:64, 0:T], 0, sv[0:64, 0], sv[0:64, 3]))
            dve.sem_inc(s["sin_arg1"], 1)
            dve.sem_inc(s["freed_dve"], 1)
            b = take("sin2")
            link(sine_arg(b[0:64, 0:T], 1, sv[0:64, 2], sv[0:64, 0]))
            dve.sem_inc(s["sin_arg2"], 1)
            dve.sem_inc(s["freed_dve"], 1)
            bn = sm[:, 64:64 + 48].rearrange("p (t h c) -> p t h c", t=4, h=2)

            def mean_square(src3, t0, n):
                for t in range(n):
                    for h in range(2):
                        ins = V.bn_stats(bn[:, t0 + t, h], src3[:, t, h * 512:(h + 1) * 512])
                    link(ins)
                    link(V.bn_aggr(sm[:, 16 + 2 * (t0 + t):18 + 2 * (t0 + t)], bn[:, t0 + t].rearrange("p h c -> p (h c)")))
            dve.wait_ge(s["x_landed"], 32)
            mean_square(x3, 0, 2)
            for i in range(8):
                t, o, side = i // 4, (i // 2) % 2, i % 2
                b = take("filt", i)
                give(tt(filt[:, t, o, side], b[:], win[:, side, t]))
            dve.wait_ge(s["freed_dve"], U.count[U.at("filt", 7)])
            for o in range(2):
                link(tt(filt[0:1, 0, o, 0], filt[0:1, 0, o, 0], skipb[:, o * 512:(o + 1) * 512], ALU.add))
            for t in range(2):
                for o in range(2):
                    link(tt(Utmp[:, 0], filt[:, t, o, 0], filt[:, t, o, 1], ALU.subtract))
                    link(tt(filt[:, t, o, 0], filt[:, t, o, 0], filt[:, t, o, 1], ALU.add))
                    link(V.tensor_copy(filt[:, t, o, 1], Utmp[:, 0]))
            dve.sem_inc(s["filt_sum"], 1)
            def ada_rows(batch):
                for i in range(4):
                    if U.engine[U.at(f"ada{batch}", i)] == "V":
                        b = take(f"ada{batch}", i)
                        if batch:
                            dve.wait_ge(s["unit_done"], U.at(f"adacol{batch - 1}") + 1)
                        give(V.tensor_copy(adarow[:, i], b[:]))

            ada_rows(0)
            dve.wait_ge(s["small_landed"], 16 * len(other_loads))
            mean_square(ctxn, 2, 2)
            mv = sm[:, 16:24].rearrange("p (t c) -> p t c", c=2)
            link(tt(sm[:, 4:8], mv[:, :, 0], mv[:, :, 0]))
            link(tt(sm[:, 4:8], sm[:, 4:8], mv[:, :, 1], ALU.add))
            link(V.tensor_scalar(sm[:, 4:8], sm[:, 4:8], EPS, None, ALU.add))
            dve.sem_inc(s["var_ready"], 1)

            def ada_columns(batch):
                b = take(f"adacol{batch}")
                c0 = 16 * batch
                for j in range(2):
                    ins = tt(adaT[:, c0:c0 + 16, j], b[:, 0:32].rearrange("p (c j) -> p c j", j=2)[:, :, j],
                             colA[:, c0:c0 + 16], ALU.add)
                link(ins)

            def gains(g0, j, r0, gc):
                link(stt(gcol[:, g0:g0 + 8], adaT[:, r0:r0 + 8, j], 1.0, colA[:, gc:gc + 8], ALU.add, ALU.mult))
            inv_root(1, sm[:, 4:8], sm[:, 8:12], sm[:, 12:16])
            for t in range(2):
                ins = V.tensor_scalar(xn[:, t], x3[:, t], sm[:, 12 + t:13 + t], None, ALU.mult)
            ins.then_inc(s["x_norm"], 1)
            for i in range(8):
                if U.engine[U.at("filtK", i)] == "V":
                    b = take("filtK", i)
                    o, f, q = i // 4, (i // 2) % 2, i % 2
                    give(V.tensor_scalar(filtK[:, o, q, f], b[:], dftw[:, f:f + 1], None, ALU.mult))
            ada_columns(0)
            gains(0, 0, 8, C_NMIX)
            gains(8, 1, 8, C_NMIX)
            dve.sem_inc(s["m_ready"], 1)
            dve.sem_inc(s["freed_dve"], 1)

            def modulate(name, dst3, g0, src, sh0=0):
                for i in range(4):
                    if U.engine[U.at(name, i)] == "V":
                        b = take(name, i)
                        for j in range(2):
                            d = 2 * i + j
                            ins = V.tensor_scalar(dst3[:, d], b[:, j * T:(j + 1) * T], gcol[:, g0 + d:g0 + d + 1],
                                                  adaT[:, sh0 + d, src:src + 1], ALU.mult, ALU.add)
                        give(ins)
            modulate("hx", hT3, 0, 0)
            dve.wait_ge(s["unit_done"], U.at("hx", 3) + 1)
            for t in range(2):
                ins = V.tensor_scalar(xn[:, t], ctxn[:, t], sm[:, 14 + t:15 + t], None, ALU.mult)
            ins.then_inc(s["ctx_norm"], 1)
            modulate("hc", hcT, 8, 1)

            def conv(k, dst, wc, stride, rows, last_unit):
                dve.wait_ge(s["freed_act"], U.count[last_unit])
                src = praw[:, k % 4]
                L = T // rows
                for j in range(2):
                    link(V.tensor_scalar(dst[:, j], src[:, j], colB[:, wc + stride + j:wc + stride + j + 1], None, ALU.mult))
                for j in range(2):
                    y = dst[:, j].rearrange("p (r l) -> p r l", r=rows)
                    v = src[:, j].rearrange("p (r l) -> p r l", r=rows)
                    link(stt(y[:, :, 1:L], v[:, :, 0:L - 1], colB[:, wc + j:wc + j + 1], y[:, :, 1:L], ALU.mult, ALU.add))
                for j in range(2):
                    y = dst[:, j].rearrange("p (r l) -> p r l", r=rows)
                    v = src[:, j].rearrange("p (r l) -> p r l", r=rows)
                    c = wc + 2 * stride + j
                    ins = stt(y[:, :, 0:L - 1], v[:, :, 1:L], colB[:, c:c + 1], y[:, :, 0:L - 1], ALU.mult, ALU.add)
                    if j == 0:
                        link(ins)
                ins.then_inc(s["conv_done"], 1)

            b = take("reltab")
            give(tt(relbuf, b[0:AH, 0:384], distmask, ALU.add))
            dve.wait_ge(s["freed_dve"], U.count[U.at("reltab")])
            dve.sem_inc(s["rel_ready"], 1)
            conv(0, kT[:, 0:2], D_MLC + 4, 8, 4, U.at("kx", 0))
            conv(1, kT[:, 2:4], D_MLC + 6, 8, 4, U.at("kx", 1))
            dve.wait_ge(s["rel_saved"], 16)
            conv(2, kcT[:, 0:2], D_MLC + 4, 8, 1, U.at("kc", 0))
            conv(3, kcT[:, 2:4], D_MLC + 6, 8, 1, U.at("kc", 1))
            ada_rows(1)
            dve.wait_ge(s["vaug_ones"], 1)
            for name, dst in (("vx", vx), ("vc", vc)):
                for t in range(2):
                    b = take(name, t)
                    give(tt(dst[:, t, :, 0:128], b[:].rearrange("p (h c) -> p h c", h=4),
                            b_rows[:, 0:512].rearrange("p (h c) -> p h c", h=4), ALU.add))
            b = take("mgate")
            link(tt(gl[:, 0:64].rearrange("p (s c) -> p s c", s=4), b[:, 0:64].rearrange("p (s c) -> p s c", s=4),
                    b_rows[:, 512:528].unsqueeze(1).broadcast_to([P, 4, 16]), ALU.add))
            for d in range(2):
                link(V.tensor_scalar(nlf[:, :, d], G4[:, :, 2 * d + 1], -1.0, 0.0, ALU.mult, ALU.max))
                link(stt(wk[:, :, d], G4[:, :, 2 * d + 1], -1.0, G4[:, :, 2 * d + 1], ALU.mult, ALU.max))
            dve.sem_inc(s["softplus_arg"], 1)
            dve.sem_inc(s["freed_dve"], 1)
            ada_columns(1)
            dve.sem_inc(s["freed_dve"], 1)
            conv(4, qT[:, 0:2], D_MLC + 0, 8, 4, U.at("q", 0))
            conv(5, qT[:, 2:4], D_MLC + 2, 8, 4, U.at("q", 1))
            dve.wait_ge(s["softplus_l"], 1)
            link(tt(gl[:, 64:96], gl[:, 64:96], gl[:, 96:128], ALU.add))
            dve.sem_inc(s["lf_ready"], 1)
            ada_rows(2)
            give(V.tensor_copy(rw(0), take("crow", 0)[0:4, :]))
            give(V.tensor_copy(rw(1), take("crow", 1)[0:4, :]))
            dve.wait_ge(s["freed_dve"], U.count[U.at("crow", 1)])
            link(V.tensor_reduce(rsm[:, 0:2], rw(1).rearrange("p (d t) -> p d t", d=2), AX.X, ALU.max))
            link(V.tensor_scalar(rsm[:, 0:2], rsm[:, 0:2], 0.0, None, ALU.max))
            link(V.tensor_scalar(rsm[:, 2:4], rsm[:, 0:2], -1.0, None, ALU.mult))
            link(tt(rsm[:, 4:5], rsm[:, 0:1], rw(0)[:, T - 1:T], ALU.subtract))
            link(tt(rsm[:, 5:6], rsm[:, 1:2], rw(0)[:, T:T + 1], ALU.subtract))
            dve.sem_inc(s["w_row_arg"], 1)
            give(V.tensor_copy(rw(2), take("xrow", 0)[0:4, :]))
            give(V.tensor_copy(rw(3), take("xrow", 1)[0:4, :]))
            dve.wait_ge(s["freed_dve"], U.count[U.at("xrow", 1)])
            link(V.tensor_tensor_scan(rw(4)[:, 0:T], rw(3)[:, 0:T], rw(3)[:, 0:T], rsm[:, 4:5], ALU.max, ALU.max))
            link(V.tensor_tensor_scan(rw(4)[:, 2 * T - 1:T - 1:-1], rw(3)[:, 2 * T - 1:T - 1:-1],
                                      rw(3)[:, 2 * T - 1:T - 1:-1], rsm[:, 5:6], ALU.max, ALU.max))
            link(tt(rw(2), rw(2), rw(4), ALU.subtract))
            dve.sem_inc(s["inter_arg"], 1)
            link(V.tensor_scalar(tri, tri, -BIG, BIG, ALU.mult, ALU.add))
            ada_columns(2)
            gains(16, 0, 32, C_NFFN)
            dve.sem_inc(s["freed_dve"], 1)
            conv(6, zhy[:, 0:2], D_HYC + 0, 12, 4, U.at("hy0", 0))
            conv(7, zhy[:, 2:4], D_HYC + 2, 12, 4, U.at("hy0", 1))
            link(V.tensor_copy(mcols[:, 48:64], take("wcol")[:, 0:16]))
            dve.sem_inc(s["freed_dve"], 1)
            conv(8, zhy[:, 4:6], D_HYC + 4, 12, 4, U.at("hy1", 0))
            conv(9, zhy[:, 6:8], D_HYC + 6, 12, 4, U.at("hy1", 1))
            for i in range(2):
                b = take("kcn", i)
                for d in range(2):
                    w0 = 48 + (d * 2 + i) * 4
                    ins = tt(kw[:, d, i].rearrange("p (h c) -> p h c", h=4), b[:].rearrange("p (h c) -> p h c", h=4),
                             mcols[:, w0:w0 + 4].unsqueeze(2).broadcast_to([P, 4, P]))
                give(ins)
            conv(10, zhy[:, 8:10], D_HYC + 8, 12, 4, U.at("hy2", 0))
            conv(11, zhy[:, 10:12], D_HYC + 10, 12, 4, U.at("hy2", 1))
            b = take("cols")
            link(V.tensor_copy(mcols[:, 0:48], b[:, 0:48]))
            link(V.tensor_scalar(mcols[:, 16:32], mcols[:, 16:32], float(DH) ** -0.5, None, ALU.mult))
            dve.sem_inc(s["cols_ready"], 1)
            dve.sem_inc(s["freed_dve"], 1)

            def w_distance(h):
                b = take(f"mb{h}")
                if h >= 2:
                    dve.wait_ge(s["unit_done"], U.at(f"num{h - 2}.1") + 1)
                elif h == 0:
                    dve.wait_ge(s["unit_done"], U.at("hc", 3) + 1)
                for d in range(2):
                    for i in range(2):
                        c = (d * 2 + i) * 4 + h
                        ins = stt(W[:, h % 2, 2 * d + i], b[:, d * T:(d + 1) * T], mcols[:, c:c + 1], tri[:, d, i],
                                  ALU.subtract, ALU.max)
                        if d + i < 2:
                            link(ins)
                link(ins)
                dve.sem_inc(s["w_arg"], 1)
                dve.sem_inc(s["freed_dve"], 1)

            for h in range(HEADS):
                w_distance(h)
                b = take(f"sT{h}")
                dve.wait_ge(s["w_exp"], h + 1)
                for d in range(2):
                    wd = W[:, h % 2, 2 * d:2 * d + 2].rearrange("p i t -> p (i t)")
                    ins = stt(wd, b[:], float(DH) ** -0.5, wd, ALU.mult, ALU.mult)
                give(ins)
                for t in range(2):
                    b = take(f"num{h}.{t}")
                    dve.wait_ge(s["freed_act"], U.count[U.at(f"inter{h}.{t}")])
                    give(tt(NUM[:, t, h], b[:, 0:258].rearrange("p (d c) -> p d c", d=2), tmpB[:, t], ALU.add))
            dve.wait_ge(s["freed_dve"], U.count[U.at("num3.1")])
            den = NUM[:, :, :, :, 128:129].rearrange("p t h d c -> p (t h d) c")[:, :, 0]
            dn = sm[:, 24:40]
            link(stt(dn, den, -1.0, den, ALU.mult, ALU.max))
            for t in range(2):
                fl = mcols[:, 32:48].rearrange("p (d i h) -> p i h d", d=2, i=2)[:, t]
                dt = dn[:, 8 * t:8 * t + 8].rearrange("p (h d) -> p h d", d=2)
                link(tt(dt, dt, fl, ALU.max))
            link(V.reciprocal(dn, dn))
            nv = NUM[:].rearrange("p t h d c -> p (t h d) c")
            link(tt(nv[:, :, 0:128], nv[:, :, 0:128], dn.unsqueeze(2).broadcast_to([P, 16, P])))
            nh = NUM[:].rearrange("p t h d c -> p (t h) d c")
            link(tt(hm, nh[:, :, 0, 0:128], nh[:, :, 1, 0:128], ALU.add))
            link(tt(hsq, hm, hm))
            link(V.tensor_reduce(sm[:, 32:40], hsq, AX.X, ALU.add))
            link(V.tensor_scalar(sm[:, 32:40], sm[:, 32:40], 1.0 / DH, EPS, ALU.mult, ALU.add))
            dve.sem_inc(s["var_ready"], 1)
            inv_root(2, sm[:, 32:40], sm[:, 40:48], sm[:, 48:56])
            link(tt(hm, hm, sm[:, 48:56].unsqueeze(2).broadcast_to([P, 8, P])))
            dve.sem_inc(s["hm_ready"], 1)
            for i in range(2):
                b = take("hT", i)
                for j in range(2):
                    h = 2 * i + j
                    ins = stt(YB[:, h], b[:, j * T:(j + 1) * T], colB[:, D_MLG + h:D_MLG + h + 1], oT[:, h], ALU.mult, ALU.mult)
                give(ins)
            dve.wait_ge(s["unit_done"], U.at("hT", 1) + 1)
            for o in range(2):
                b = take(f"uT{o}", 1)
                if o:
                    dve.wait_ge(s["unit_done"], U.at("uf0", 3) + 1)
                give(V.tensor_copy(unat[:, 1], b[:]))
                if o:
                    dve.wait_ge(s["unit_done"], U.at("yo0", 1) + 1)
                for f in range(2):
                    bc_, bs = take(f"uf{o}", 2 * f), take(f"uf{o}", 2 * f + 1)
                    Kr, Ks = filtK[:, o, 0, f], filtK[:, o, 1, f]
                    link(tt(Utmp[:, 0], bc_[:], Kr))
                    tt(Utmp[:, 1], bc_[:], Ks).then_inc(s["freed_dve"], 1)
                    link(tt(Utmp[:, 2], bs[:], Ks))
                    tt(Utmp[:, 3], bs[:], Kr).then_inc(s["freed_dve"], 1)
                    dve.wait_ge(s["freed_dve"], U.count[U.at(f"uf{o}", 2 * f + 1)])
                    link(tt(Y[:, 0, f], Utmp[:, 0], Utmp[:, 2], ALU.subtract))
                    link(tt(Y[:, 1, f], Utmp[:, 1], Utmp[:, 3], ALU.add))
                dve.sem_inc(s["y_spec"], 1)
                for i in range(2):
                    b = take(f"yo{o}", i)
                    give(tt(zhy[:, 2 * i:2 * i + 2].rearrange("p c t -> p (c t)"), b[:],
                            zhy[:, 4 * (o + 1) + 2 * i:4 * (o + 1) + 2 * i + 2].rearrange("p c t -> p (c t)")))

            def make_diag(chunk, dst, signal):
                for d in range(8):
                    ins = V.tensor_scalar(dst[:, d], ident[:], adaT[:, 8 * chunk + d, 0:1], None, ALU.mult)
                ins.then_inc(signal, 1)
            make_diag(2, diag, s["bc_diag"])
            give(V.tensor_copy(bc2[:, 512:1024], take("bc2", 1)[:]))
            for c in range(4):
                ba, bb = take(f"bra{c}", 0), take(f"bra{c}", 1)
                ga = gates[:, 2 * c:2 * c + 2].rearrange("p c t -> p (c t)")
                gb = gates[:, 8 + 2 * c:8 + 2 * c + 2].rearrange("p c t -> p (c t)")
                if c == 0:
                    wait_emptied(dve, "merge1")
                else:
                    dve.wait_ge(s["merged_ready"], c)
                tt(mtmp[:, 0], ba[:], ga).then_inc(s["freed_dve"], 1)
                tt(mtmp[:, 1], bb[:], gb).then_inc(s["freed_dve"], 1)
                dve.wait_ge(s["freed_dve"], U.count[U.at(f"bra{c}", 1)])
                tt(merged[:, 2 * c:2 * c + 2].rearrange("p c t -> p (c t)"), mtmp[:, 0], mtmp[:, 1], ALU.add).then_inc(s["merged_ready"], 1)
            dve.wait_ge(s["freed_act"], U.count[U.at("bc2", 0)])
            for i in range(4):
                n, t = divmod(i, 2)
                b = take("out1", i)
                dve.wait_ge(s["freed_dve"], U.count[U.at("out1", i)] - 1)
                link(tt(mtmp[:, 2], b[:], bc2[:, 512 * n:512 * n + 512]))
                v = x3[:, t, 512 * n:512 * n + 512]
                give(tt(v, v, mtmp[:, 2], ALU.add))
                dve.wait_ge(s["freed_dve"], U.count[U.at("out1", i)])
                ins = V.bn_stats(bn[:, t, n], v)
            link(ins)

            def rms(kroot):
                for t in range(2):
                    link(V.bn_aggr(sm[:, 16 + 2 * t:18 + 2 * t], bn[:, t].rearrange("p h c -> p (h c)")))
                m2 = sm[:, 16:20].rearrange("p (t c) -> p t c", c=2)
                link(tt(sm[:, 4:6], m2[:, :, 0], m2[:, :, 0]))
                link(tt(sm[:, 4:6], sm[:, 4:6], m2[:, :, 1], ALU.add))
                link(V.tensor_scalar(sm[:, 4:6], sm[:, 4:6], EPS, None, ALU.add))
                dve.sem_inc(s["var_ready"], 1)
                inv_root(kroot, sm[:, 4:6], sm[:, 8:10], sm[:, 12:14])
            dve.wait_ge(s["freed_dve"], U.count[U.at("out1", 3)])
            rms(3)
            for t in range(2):
                ins = V.tensor_scalar(xn2[:, t], x3[:, t], sm[:, 12 + t:13 + t], None, ALU.mult)
            ins.then_inc(s["xn2_ready"], 1)
            modulate("h2T", hT3, 16, 0, 24)
            make_diag(5, diag5, s["bc_diag"])
            dve.wait_ge(s["moe_landed"], 64)
            b = take("route")
            lg = b[:, 0:32].rearrange("p (t e) -> p t e", t=2)
            link(V.tensor_reduce(sm[:, 24:26], lg, AX.X, ALU.max))
            link(tt(affn, lg, sm[:, 24:26].unsqueeze(2).broadcast_to([P, 2, 16]), ALU.subtract))
            dve.sem_inc(s["soft_arg"], 1)
            dve.sem_inc(s["freed_dve"], 1)
            give(V.tensor_copy(bc5[:, 512:1024], take("bc5", 1)[:]))
            dve.wait_ge(s["aff_exp"], 1)
            link(V.tensor_reduce(sm[:, 26:28], affn, AX.X, ALU.add))
            link(V.reciprocal(sm[:, 28:30], sm[:, 26:28]))
            link(tt(affn, affn, sm[:, 28:30].unsqueeze(2).broadcast_to([P, 2, 16])))
            dve.sem_inc(s["aff_ready"], 1)
            give(V.tensor_copy(affT, take("affT")[0:16, 0:T]))
            dve.wait_ge(s["freed_dve"], U.count[U.at("affT")])

            def select(e):
                tt(aff1, affT, ident[0:16, bass.ds(e, 1)].broadcast_to([16, T])).then_inc(s["row_masked"], 1)
                dve.wait_ge(s["row_spread"], e + 1)
                row = bank[3][:, T:2 * T]
                for t in range(2):
                    own = affn[:, t, bass.ds(e, 1)]
                    V.tensor_scalar(rjunk[:, t], row, own, 0.0, ALU.is_gt, ALU.add, accum_out=rank[:, 0, t:t + 1])
                    ins = V.scalar_tensor_tensor(rjunk[:, 2 + t], row, own, ltmask[:, t], ALU.is_equal, ALU.mult,
                                                 accum_out=rank[:, 1, t:t + 1])
                ins.then_inc(s["rank_ready"], 1)
                dve.wait_ge(s["rank_ready"], 2 * e + 1)
                tt(rank[:, 0], rank[:, 0], rank[:, 1], ALU.add).then_inc(s["rank_ready"], 1)
                dve.wait_ge(s["rank_ready"], 2 * e + 2)
                tt(sel, iota.unsqueeze(1).broadcast_to([P, 2, CAP]), rank[:, 0].unsqueeze(2).broadcast_to([P, 2, CAP]),
                   ALU.is_equal).then_inc(s["sel_ready"], 1)

            def gathered_tokens(e):
                dve.wait_ge(s["gathered"], e + 1)
                got = bank[1][:, 0:T].rearrange("p (d c) -> p d c", d=KD)
                tt(xg, got, gcol[:, 16:24].unsqueeze(2).broadcast_to([P, KD, CAP])).then_inc(s["xg_scaled"], 1)
                dve.wait_ge(s["xg_scaled"], e + 1)
                tt(xg, xg, adaT[:, 24:32, 0:1].broadcast_to([P, KD, CAP]), ALU.add).then_inc(s["xg_copied"], 1)

            def gated_selection(e):
                dve.wait_ge(s["sel_ready"], e + 1)
                for t in range(2):
                    ins = V.tensor_scalar(sgs[:, t].rearrange("p (g c) -> p g c", g=4),
                                          sel[:, t].unsqueeze(1).broadcast_to([P, 4, CAP]),
                                          affn[:, t, bass.ds(e, 1)], None, ALU.mult)
                ins.then_inc(s["sg_copied"], 1)
            select(0)
            gated_selection(0)
            gathered_tokens(0)
            V.memset(acc, 0.0).then_inc(s["acc_done"], 1)

            def expert(e, last=False):
                if not last:
                    select(e + 1)
                dve.wait_ge(s["slots_used"], e * PER_EXPERT + 8)
                dve.wait_ge(s["a_read"], e + 1)
                tt(hact, bank[1][:], sact).then_inc(s["hact"], 1)
                dve.wait_ge(s["sg_turned"], e + 1)
                V.tensor_copy(sgT, bank[3][:, 0:T]).then_inc(s["sgT_evac"], 1)
                if not last:
                    gated_selection(e + 1)
                dve.wait_ge(s["hT_turned"], e + 1)
                V.tensor_copy(hTs.rearrange("p c t -> p (c t)"), bank[2][:]).then_inc(s["hT_evac"], 1)
                if not last:
                    gathered_tokens(e + 1)
                if last:
                    dve.wait_ge(s["acc_done"], EXPERTS)
                    wait_emptied(dve, "bc5")
                    for t in range(2):
                        link(tt(acc[:, t], acc[:, t], bc5))
                        link(tt(x3[:, t], x3[:, t], acc[:, t], ALU.add))
                dve.wait_ge(s["scat_done"], e + 1)
                dve.wait_ge(s["acc_done"], e + 1)
                if last:
                    return
                for n in range(4):
                    o = acc[:, :, n * T:(n + 1) * T]
                    ins = tt(o, bank[4 + n][:].rearrange("p (t d) -> p t d", t=2), o, ALU.add)
                ins.then_inc(s["acc_done"], 1)
            with dve.Fori(0, EXPERTS - 1) as e:
                expert(e)
            expert(EXPERTS - 1, True)
            for n in range(4):
                cols = slice(n * T, (n + 1) * T)
                ins = tt(acc[:, :, cols], bank[4 + n][:].rearrange("p (t d) -> p t d", t=2),
                         bc5[:, cols].unsqueeze(1).broadcast_to([P, 2, T]))
            ins.then_inc(s["acc_done"], 1)
            dve.wait_ge(s["acc_done"], EXPERTS + 1)
            for h in range(2):
                cols = slice(h * 512, h * 512 + 512)
                for t in range(2):
                    ins = tt(x3[:, t, cols], x3[:, t, cols], acc[:, t, cols], ALU.add)
                link(ins)
                for t in range(2):
                    ins = V.bn_stats(bn[:, t, h], x3[:, t, cols])
            link(ins)
            rms(4)
            for h in range(2):
                for t in range(2):
                    v = x3[:, t, 512 * h:512 * h + 512]
                    ins = stt(v, v, sm[:, 12 + t:13 + t], fnorm[:, 512 * h:512 * h + 512], ALU.mult, ALU.mult)
                ins.then_inc(s["x1_ready"], 1)

            nroot = [4]

            def next_root(n):
                nroot[0] += 1
                dve.sem_inc(s["var_ready"], 1)
                inv_root(nroot[0], sm[:, 0:n], sm[:, 8:8 + n], sm[:, 16:16 + n])

            def layer_norm(name, w, landed_sem, landed_count, signal):
                for i in range(4):
                    h, t = divmod(i, 2)
                    v = x3[:, t, 512 * h:512 * h + 512]
                    give(stt(v, v, ALPHA, take(name, i)[:], ALU.mult, ALU.add))
                    dve.wait_ge(s["freed_dve"], U.count[U.at(name, i)])
                    ins = V.bn_stats(bn[:, t, h], v)
                link(ins)
                for t in range(2):
                    ins = V.bn_aggr(sm[:, 24 + 2 * t:26 + 2 * t], bn[:, t].rearrange("p h c -> p (h c)"))
                link(ins)
                mv2 = sm[:, 24:28].rearrange("p (t c) -> p t c", c=2)
                link(V.tensor_scalar(sm[:, 0:2], mv2[:, :, 1], LN_EPS, None, ALU.add))
                next_root(2)
                dve.wait_ge(landed_sem, landed_count)
                for h in range(2):
                    cols = slice(512 * h, 512 * h + 512)
                    for t in range(2):
                        ins = V.tensor_scalar(x3[:, t, cols], x3[:, t, cols], sm[:, 24 + 2 * t:25 + 2 * t], sm[:, 16 + t:17 + t],
                                              ALU.subtract, ALU.mult)
                    link(ins)
                    for t in range(2):
                        ins = tt(x3[:, t, cols], x3[:, t, cols], w[:, 0, cols])
                    link(ins)
                    for t in range(2):
                        ins = tt(x3[:, t, cols], x3[:, t, cols], w[:, 1, cols], ALU.add)
                    ins.then_inc(signal, 1)

            def flat(v, i):
                return v[:, 2 * i:2 * i + 2].rearrange("p k t -> p (k t)")

            def low_x(name, n0):
                for i in range(4):
                    b = take(name, i)
                    dve.wait_ge(s["x_hi"], n0 + i + 1)
                    give(tt(flat(hTp[1], i), b[:], flat(hTp[0], i).bitcast(F32), ALU.subtract))

            n_split = [0]

            def split(pair, i, v):
                link(V.tensor_copy(flat(pair[0], i), v))
                tt(flat(pair[1], i), v, flat(pair[0], i).bitcast(F32), ALU.subtract).then_inc(s["prod_split"], 1)
                n_split[0] += 1

            def split_product(pair, i, name, other):
                if n_split[0] >= 2:
                    dve.wait_ge(s["prod_split"], n_split[0] - 1)
                tmp = btmp[:, n_split[0] % 2]
                give(tt(tmp, take(name)[:], other))
                dve.wait_ge(s["freed_dve"], U.count[U.at(name)])
                split(pair, i, tmp)

            for l in range(DEPTH_2):
                low_x(f"xT{l}", 8 * l)
                dve.wait_ge(s["lay_landed"], 64 * (l + 1))
                for i in range(3):
                    wd = 512 if i < 2 else 128
                    for t in range(2):
                        b = take(f"va{l}", 2 * i + t)
                        give(tt(va[:, t, 512 * i:512 * i + wd], b[:, 0:wd], vbias_a[:, 512 * i:512 * i + wd], ALU.add))
                def attention_out(j):
                    b = take(f"attn{l}.{j}")
                    for t in range(2):
                        ins = V.tensor_scalar(ya[:, t, j * AD:(j + 1) * AD], b[:, t * AD:(t + 1) * AD], sm[:, 62 + t:63 + t], None, ALU.mult)
                    give(ins)

                relg = relB.rearrange("p (g j) t -> p g j t", g=NG)
                for j in range(HPG):
                    b0, b1, b2 = (take(f"score{l}.{j}", i) for i in range(3))
                    if j:
                        dve.wait_ge(s["unit_done"], U.at(f"pT{l}.{j - 1}", 2) + 1)
                    else:
                        dve.wait_ge(s["freed_dve"], U.count[U.at(f"va{l}", 5)])
                    scale = AD ** -0.5
                    c1 = sc[:, 3:9].rearrange("p (g k) t -> p g (k t)", g=NG)
                    give(stt(sc[:, 0:3], b0[:, 0:384].rearrange("p (g t) -> p g t", g=3), scale, relg[:, :, j, P:T], ALU.mult, ALU.add))
                    give(stt(c1[:, 0:2], b1[:].rearrange("p (g t) -> p g t", g=2), scale, relg[:, 0:2, j], ALU.mult, ALU.add))
                    give(stt(c1[:, 2], b2[:, 0:T], scale, relg[:, 2, j], ALU.mult, ALU.add))
                    dve.wait_ge(s["freed_dve"], U.count[U.at(f"score{l}.{j}", 2)])
                    V.tensor_reduce(sm[:, 56:57], sc[:, 0:3], AX.XY, ALU.max)
                    link(V.tensor_reduce(sm[:, 57:58], sc[:, 3:9], AX.XY, ALU.max))
                    link(V.tensor_scalar(sm[:, 58:60], sm[:, 56:58], -1.0, None, ALU.mult))
                    dve.sem_inc(s["sc_ready"], 1)
                    if j:
                        attention_out(j - 1)
                    if j == 0:
                        dve.wait_ge(s["vr_landed"], 48 + 16 * l)
                    if QKR_AT[j]:
                        for i in range(QKR_AT[j]):
                            hh = sum(QKR_AT[:j]) + i
                            dve.wait_ge(s["freed_act"], U.count[U.at(f"qkr{l}.{j}", i)])
                            cos2 = rope[:, 0].unsqueeze(1).broadcast_to([P, 2, T])
                            sin2 = rope[:, 1].unsqueeze(1).broadcast_to([P, 2, T])
                            tt(rm1, rraw, cos2)
                            link(tt(rm2, rraw, sin2))
                            tt(qkr[:, 2 * hh], rm1[:, 0], rm2[:, 1], ALU.subtract)
                            link(tt(qkr[:, 2 * hh + 1], rm2[:, 0], rm1[:, 1], ALU.add))
                            dve.sem_inc(s["rot_done"], 1)
                    for i in range(2 * VR_AT[j]):
                        n = sum(VR_AT[:j]) + i // 2
                        v = vr[:, i % 2, 512 * n:512 * n + 512]
                        give(tt(v, take(f"vr{l}.{j}", i)[:], v, ALU.add))
                    dve.wait_ge(s["exp_done"], HPG * l + j + 1)
                    if j:
                        dve.wait_ge(s["freed_dve"], U.count[U.at(f"attn{l}.{j - 1}")])
                    link(V.reciprocal(sm[:, 62:64], sm[:, 60:62]))
                attention_out(HPG - 1)
                for i, (c0, c1) in enumerate(((0, 2), (2, 3))):
                    b = take(f"yaT{l}", i)[:, 0:(c1 - c0) * T]
                    link(V.tensor_copy(yaTp[0][:, c0:c1].rearrange("p k t -> p (k t)"), b))
                    give(tt(yaTp[1][:, c0:c1].rearrange("p k t -> p (k t)"), b,
                            yaTp[0][:, c0:c1].rearrange("p k t -> p (k t)").bitcast(F32), ALU.subtract))
                for h in range(RH):
                    b = take(f"rs{l}.{h}")
                    if h >= 2:
                        dve.wait_ge(s["unit_done"], U.at(f"ro{l}.{h - 2}", 1) + 1)
                    give(tt(pr[:, h % 2], b[:, 0:384], decay[:, h]))
                for h in range(RH):
                    for t in range(2):
                        dve.wait_ge(s["freed_act"], U.count[U.at(f"ro{l}.{h}", t)])
                        c = 2 * (2 * h + t)
                        link(V.bn_stats(bn[:, 0, 0], yr[:, t, h * 512:(h + 1) * 512]))
                        link(V.bn_aggr(sm[:, 24 + c:26 + c], bn[:, 0, 0]))
                mvr = sm[:, 24:40].rearrange("p (n c) -> p n c", c=2)
                link(V.tensor_scalar(sm[:, 0:8], mvr[:, :, 1], LN_EPS, None, ALU.add))
                next_root(8)
                for h in range(RH):
                    for t in range(2):
                        n = 2 * h + t
                        v = yr[:, t, h * 512:(h + 1) * 512]
                        link(V.tensor_scalar(v, v, sm[:, 24 + 2 * n:25 + 2 * n], sm[:, 16 + n:17 + n], ALU.subtract, ALU.mult))
                    dve.sem_inc(s["yr_ready"], 1)
                for c in range(8):
                    dve.wait_ge(s["freed_act"], U.count[U.at(f"gr{l}.{c}")])
                    split_product(ybTp, c, f"yrT{l}.{c}", gtmp[:, c % 2])
                wait_emptied(dve, f"gate{l}")
                for i in range(4):
                    give(tt(merged2[:, 2 * i:2 * i + 2].rearrange("p k t -> p (k t)"), take(f"mixA{l}", i)[:],
                            gates2[:, 2 * i:2 * i + 2].rearrange("p k t -> p (k t)")))
                for i in range(4):
                    m = merged2[:, 2 * i:2 * i + 2].rearrange("p k t -> p (k t)")
                    dve.wait_ge(s["prod_split"], n_split[0])
                    link(tt(btmp[:, i % 2], take(f"mixB{l}", i)[:], gates2[:, 8 + 2 * i:10 + 2 * i].rearrange("p k t -> p (k t)")))
                    dve.wait_ge(s["freed_dve"], U.count[U.at(f"mixA{l}", 3)] + i)
                    give(tt(m, m, btmp[:, i % 2], ALU.add))
                    dve.wait_ge(s["freed_dve"], U.count[U.at(f"mixB{l}", i)])
                    split(mergedp, i, m)
                layer_norm(f"mixo{l}", ln1, s["ln1_landed"], 32 * (l + 1), s["x_done"])
                dve.wait_ge(s["x_done"], 2 * (l + 1) if l == 0 else 6)
                low_x(f"x2T{l}", 8 * l + 4)
                for i in range(NF // 2):
                    dve.wait_ge(s["freed_act"], U.count[U.at(f"ffg{l}.{i}")])
                    split_product(hFp, i, f"ffu{l}.{i}", gtmp[:, i % 2])
                layer_norm(f"down{l}", ln2, s["ln2_landed"], 32 * (l + 1), s["x_done"] if l < DEPTH_2 - 1 else s["y_ready"])
                if l < DEPTH_2 - 1:
                    dve.wait_ge(s["x_done"], 4)

        @block.tensor
        def _(pe):
            M = nc.tensor

            def open_unit(name, i=0):
                u = U.at(name, i)
                if u >= 8:
                    v = u - 8
                    pe.wait_ge(freed[U.engine[v]], U.count[v])
                return bank[u % 8]

            def close(ins):
                ins.then_inc(s["unit_done"], 1)

            def mm(o, l, r, first=True, last=True):
                return M.matmul(o, l, r, start=first, stop=last)

            def tr(o, i):
                return M.transpose(o, i, ident[:])

            def gemm_T(name, i, w, cols, xT, nk=KD):
                b = open_unit(name, i)
                for j, c in enumerate(cols):
                    for q in range(nk):
                        ins = mm(b[:, j * T:(j + 1) * T], w[:, q, c:c + P], xT[:, q], q == 0, q == nk - 1)
                close(ins)

            def gemm_N(name, i, w, width, xT, t, nk=KD):
                b = open_unit(name, i)
                for q in range(nk):
                    ins = mm(b[:, 0:width], xT[:, q, t * P:(t + 1) * P], w[:, q, 0:width], q == 0, q == nk - 1)
                close(ins)

            def turn(name, src3, n=4, ready=None, count=0):
                for i in range(n):
                    if ready and i % 2 == 0:
                        pe.wait_ge(ready, count + i // 2 + 1)
                    b = open_unit(name, i)
                    for j in range(2):
                        for t in range(2):
                            ins = tr(b[:, j * T + t * P:j * T + t * P + P], src3[:, t, (2 * i + j) * P:(2 * i + j + 1) * P])
                    close(ins)

            pe.wait_ge(s["packs_landed"], 16 * len(first_loads))
            b = open_unit("packs", 0)
            M.transpose(b[:, 0:108], colA[0:108, :], ident[0:108, 0:108])
            close(M.transpose(b[:, P:P + 80], colB[0:80, :], ident[0:80, 0:80]))
            b = open_unit("packs", 1)
            M.transpose(b[:, 0:66], colC[0:66, 0:P], ident[0:66, 0:66])
            close(M.transpose(b[:, P:P + 66], colC[0:66, P:2 * P], ident[0:66, 0:66]))
            pe.wait_ge(s["filt_landed"], 16 * len(filter_loads))
            b = open_unit("sin1")
            close(mm(b[0:64, 0:T], w1s[0:33], emb[0:33]))
            b = open_unit("sin2")
            pe.wait_ge(s["sin1_ready"], 1)
            close(mm(b[0:64, 0:T], w2s[0:64], sv[0:64, 1]))
            pe.wait_ge(s["sin2_ready"], 1)
            for i in range(8):
                t, c = divmod(i, 4)
                b = open_unit("filt", i)
                close(mm(b[:], sv[0:64, 3, t * P:(t + 1) * P], w3[0:64, 512 * c:512 * c + 512]))
            pe.wait_ge(s["silu_c"], 1)

            def ada_product(batch):
                for i in range(4):
                    arrived(pe, S_ADA[batch] + i)
                    w = slot(S_ADA[batch] + i, 8, 512)
                    b = open_unit(f"ada{batch}", i)
                    for q in range(2):
                        for g in range(4):
                            ins = mm(b[32 * g:32 * g + 32, :], sTad[:, 2 * g + q], w[:, 2 * g + q], q == 0, q == 1)
                    close(ins)

            def ada_turn(batch):
                wait_emptied(pe, f"ada{batch}")
                b = open_unit(f"adacol{batch}")
                for c in range(16):
                    ins = mm(b[:, 2 * c:2 * c + 2], adarow[:, c // 4, (c % 4) * P:(c % 4 + 1) * P], selsum[:])
                close(ins)
            ada_product(0)
            pe.wait_ge(s["filt_sum"], 1)
            pe.wait_ge(s["tables_landed"], 16 * len(table_loads))
            for i in range(8):
                o, f, q = i // 4, (i // 2) % 2, i % 2
                b = open_unit("filtK", i)
                for t in range(2):
                    ins = mm(b[:], dft[:, q, t, f * P:(f + 1) * P], filt[:, t, o, q], t == 0, t == 1)
                close(ins)
            pe.wait_ge(s["cst_set"], 1)
            pe.wait_ge(s["small_landed"], 16 * len(other_loads))
            ada_turn(0)
            pe.wait_ge(s["x_norm"], 1)
            turn("hx", xn)
            pe.wait_ge(s["ctx_norm"], 1)
            turn("hc", xn)
            wait_emptied(pe, "hx")
            wait_emptied(pe, "hc")

            def gemm_slot_T(n, name, i0, xT, nk=KD, width=512):
                arrived(pe, n)
                w = slot(n, nk, width)
                for i in range(width // 256):
                    gemm_T(name, i0 + i, w, (256 * i, 256 * i + P), xT, nk)

            b = open_unit("reltab")
            close(mm(b[0:AH, 0:384], rel_bias, onehot))
            gemm_slot_T(S_KC, "kx", 0, hT3)
            gemm_slot_T(S_KC, "kc", 0, hcT)
            ada_product(1)
            arrived(pe, S_V)
            for name, act_ in (("vx", hT3), ("vc", hcT)):
                for t in range(2):
                    gemm_N(name, t, slot(S_V, 8, 512), 512, act_, t)
            b = open_unit("mgate")
            wg = w_gate[:].rearrange("p (k c) -> p k c", k=KD)
            for i, act_ in enumerate((hT3, hcT)):
                for t in range(2):
                    for q in range(KD):
                        ins = mm(b[:, (2 * i + t) * 16:(2 * i + t + 1) * 16], act_[:, q, t * P:(t + 1) * P], wg[:, q],
                                 q == 0, q == KD - 1)
            close(ins)
            ada_turn(1)
            gemm_slot_T(S_Q, "q", 0, hT3)
            ada_product(2)
            pe.wait_ge(s["lf_ready"], 1)
            for name, i in (("crow", 1), ("xrow", 0)):
                b = open_unit(name, 0)
                for d in range(2):
                    for t in range(2):
                        ins = mm(b[0:4, d * T:(d + 1) * T], nlf[:, 2 * i + t, d], tri[:, d, t], t == 0, t == 1)
                close(ins)
                b = open_unit(name, 1)
                for d in range(2):
                    for t in range(2):
                        o = b[0:4, d * T + t * P:d * T + (t + 1) * P]
                        mm(o, G4[:, 2 * i + t, 2 * d], ident[:], True, False)
                        for q in range(2):
                            ins = mm(o, nlf[:, 2 * i + q, d], tri[:, d, q, t * P:(t + 1) * P], False, q == 1)
                close(ins)
            gemm_slot_T(S_HY, "hy0", 0, hT3)
            ada_turn(2)
            pe.wait_ge(s["w_row"], 1)
            b = open_unit("wcol")
            for d in range(2):
                for t in range(2):
                    c = (d * 2 + t) * 4
                    ins = mm(b[:, c:c + 4], rw(5)[:, d * T + t * P:d * T + (t + 1) * P], ident[0:4, 0:4])
            close(ins)
            gemm_slot_T(S_HY + 1, "hy1", 0, hT3)
            pe.wait_ge(s["qk_ready"], 4)
            wait_emptied(pe, "wcol")
            for t in range(2):
                b = open_unit("kcn", t)
                for h in range(4):
                    ins = tr(b[:, h * P:(h + 1) * P], kcT[:, h, t * P:(t + 1) * P])
                close(ins)
            gemm_slot_T(S_HY + 2, "hy2", 0, hT3)
            wait_emptied(pe, "kcn")
            wait_emptied(pe, "vc")
            for h in range(4):
                b = open_unit("state", h)
                for d in range(2):
                    for t in range(2):
                        ins = mm(b[:, d * 129:(d + 1) * 129], kw[:, d, t, h * P:(h + 1) * P], vc[:, t, h], t == 0, t == 1)
                close(ins)
            gemm_slot_T(S_O, "o", 0, hT3)
            pe.wait_ge(s["inter_rows"], 1)
            b = open_unit("cols")
            for kind, r in enumerate((3, 0, 2)):
                for d in range(2):
                    for t in range(2):
                        c = kind * 16 + (d * 2 + t) * 4
                        ins = mm(b[:, c:c + 4], rw(r)[:, d * T + t * P:d * T + (t + 1) * P], ident[0:4, 0:4])
            close(ins)
            wait_emptied(pe, "state")
            pe.wait_ge(s["qk_ready"], 6)
            for h in range(HEADS):
                b = open_unit(f"mb{h}")
                close(mm(b[:], sel4[0:4, h * P:(h + 1) * P], rw(4)))
                b = open_unit(f"sT{h}")
                for i in range(2):
                    ins = mm(b[:, i * T:(i + 1) * T], kT[:, h, i * P:(i + 1) * P], qT[:, h])
                close(ins)
                for t in range(2):
                    b = open_unit(f"inter{h}.{t}")
                    close(mm(b[:, 0:258], qT[:, h, t * P:(t + 1) * P], CA[:, h].rearrange("p d c -> p (d c)")))
                    b = open_unit(f"num{h}.{t}")
                    if t == 0:
                        wait_emptied(pe, f"sT{h}")
                    for d in range(2):
                        keys = [i for i in range(2) if (i <= t if d == 0 else i >= t)]
                        for i in keys:
                            ins = mm(b[:, d * 129:(d + 1) * 129], W[:, h % 2, 2 * d + i, t * P:(t + 1) * P], vx[:, i, h],
                                     i == keys[0], i == keys[-1])
                    close(ins)
            gemm_slot_T(S_MERGE, "mergeA", 0, hT3)
            gemm_slot_T(S_MERGE + 1, "mergeA", 2, hT3)
            pe.wait_ge(s["hm_ready"], 1)
            for i in range(2):
                b = open_unit("hT", i)
                for j in range(2):
                    for t in range(2):
                        ins = tr(b[:, j * T + t * P:j * T + t * P + P], hm[:, t * 4 + 2 * i + j])
                close(ins)
            pe.wait_ge(s["conv_done"], 12)
            for o in range(2):
                if o:
                    wait_emptied(pe, "yo0")
                for t in range(2):
                    b = open_unit(f"uT{o}", t)
                    for c in range(4):
                        ins = tr(b[:, c * P:(c + 1) * P], zhy[:, c, t * P:(t + 1) * P])
                    close(ins)
                wait_emptied(pe, f"uT{o}")
                for f in range(2):
                    for q in range(2):
                        b = open_unit(f"uf{o}", 2 * f + q)
                        for t in range(2):
                            ins = mm(b[:], dft[:, q, t, f * P:(f + 1) * P], unat[:, t], t == 0, t == 1)
                        close(ins)
                gemm_slot_T(S_MERGE + 2 + o, f"merge{o}", 0, hT3)
                pe.wait_ge(s["y_spec"], o + 1)
                for i in range(2):
                    b = open_unit(f"yo{o}", i)
                    for j in range(2):
                        n = 0
                        for q in range(2):
                            for f in range(2):
                                ins = mm(b[:, j * T:(j + 1) * T], Y[:, q, f, (2 * i + j) * P:(2 * i + j + 1) * P], dft[:, q, f],
                                         n == 0, n == 3)
                                n += 1
                    close(ins)

            def spread(name, dg):
                for n in range(2):
                    b = open_unit(name, n)
                    for d in range(4):
                        ins = mm(b[:, d * P:(d + 1) * P], ones[:], dg[:, 4 * n + d])
                    close(ins)
            pe.wait_ge(s["bc_diag"], 1)
            spread("bc2", diag)
            arrived(pe, S_BR)
            arrived(pe, S_BR + 1)
            wait_emptied(pe, "yo1")
            wait_emptied(pe, "hT")
            for c in range(4):
                for m, z in ((0, zhy), (1, YB)):
                    gemm_T(f"bra{c}", m, slot(S_BR + m, 4, D), (256 * c, 256 * c + P), z, 4)
            pe.wait_ge(s["merged_ready"], 4)
            for n in range(2):
                arrived(pe, S_OUT + n)
                for t in range(2):
                    gemm_N("out1", 2 * n + t, slot(S_OUT + n, 8, 512), 512, merged, t)

            pe.wait_ge(s["xn2_ready"], 1)
            turn("h2T", xn2)
            pe.wait_ge(s["moe_landed"], 64)
            wait_emptied(pe, "h2T")
            b = open_unit("route")
            for t in range(2):
                for q in range(KD):
                    ins = mm(b[:, t * 16:(t + 1) * 16], hT3[:, q, t * P:(t + 1) * P], w_router[:, q], q == 0, q == KD - 1)
            close(ins)
            pe.wait_ge(s["bc_diag"], 2)
            spread("bc5", diag5)
            pe.wait_ge(s["aff_ready"], 1)
            b = open_unit("affT")
            for t in range(2):
                ins = tr(b[0:16, t * P:(t + 1) * P], affn[:, t])
            close(ins)
            wait_emptied(pe, "bc5")
            wait_emptied(pe, "affT")

            def spread_gates(e):
                pe.wait_ge(s["row_masked"], e + 1)
                mm(bank[3][:, T:2 * T], ones[0:16], aff1).then_inc(s["row_spread"], 1)

            def gather(e):
                pe.wait_ge(s["sel_ready"], e + 1)
                for d in range(KD):
                    for t in range(2):
                        ins = mm(bank[1][:, d * CAP:(d + 1) * CAP], xn2[:, t, d * P:(d + 1) * P], sel[:, t], t == 0, t == 1)
                ins.then_inc(s["gathered"], 1)
            spread_gates(0)
            gather(0)

            def expert(e, last=False):
                pe.wait_ge(s["xg_copied"], e + 1)
                for c in range(8):
                    pe.wait_ge(expert_landed[c % XRING], 32 * (c // XRING + 1) + e * (32 * PER_EXPERT // XRING))
                    w = expert_slot(c, 2)
                    o = bank[c // 4]
                    for q in range(2):
                        kt_ = 2 * (c % 4) + q
                        for g in range(4):
                            ins = mm(o[32 * g:32 * g + 32, :], xg[:, kt_], w[:, q, 512 * g:512 * g + 512], kt_ == 0, kt_ == 7)
                    ins.then_inc(s["slots_used"], 1)
                    if c == 3 and not last:
                        spread_gates(e + 1)
                pe.wait_ge(s["sg_copied"], e + 1)
                if not last:
                    pe.wait_ge(s["sel_ready"], e + 2)
                for t in range(2):
                    ins = tr(bank[3][:, t * P:(t + 1) * P], sgs[:, t])
                ins.then_inc(s["sg_turned"], 1)
                pe.wait_ge(s["hact"], e + 1)
                for c in range(4):
                    ins = tr(bank[2][:, c * P:(c + 1) * P], hact[:, c * P:(c + 1) * P])
                ins.then_inc(s["hT_turned"], 1)
                if not last:
                    gather(e + 1)
                pe.wait_ge(s["hT_evac"], e + 1)
                for r in range(4):
                    m = 8 + r
                    pe.wait_ge(expert_landed[m % XRING], 32 * (m // XRING + 1) + e * (32 * PER_EXPERT // XRING))
                    w = expert_slot(m, 4)
                    for c in range(4):
                        for g in range(4):
                            ins = mm(bank[0][32 * g:32 * g + 32, 0:T], hTs[:, c, 32 * r:32 * r + 32], w[:, c, T * g:T * (g + 1)],
                                     r + c == 0, r + c == 6)
                    ins.then_inc(s["slots_used"], 1)
                pe.wait_ge(s["y_evac"], e + 1)
                pe.wait_ge(s["sgT_evac"], e + 1)
                pe.wait_ge(s["acc_done"], e + 1)
                for t in range(2):
                    for g in range(4):
                        ins = mm(bank[4 + g][:, t * T:(t + 1) * T], sgT[32 * g:32 * g + 32, t * P:(t + 1) * P], ysb[32 * g:32 * g + 32])
                ins.then_inc(s["scat_done"], 1)
            with pe.Fori(0, EXPERTS - 1) as e:
                expert(e)
            expert(EXPERTS - 1, True)

            pe.wait_ge(s["acc_done"], EXPERTS + 1)
            SPLITS = 8 + 4 + NF // 2

            def weights(n):
                pe.wait_ge(s["lo_ready"], n + 1)
                low, high = half(n, ring_r)
                return high, low

            def mm3(o, lhs, rhs, first, last):
                mm(o, lhs[0], rhs[0], first, False)
                mm(o, lhs[0], rhs[1], False, False)
                return mm(o, lhs[1], rhs[0], False, last)

            def both(pair, *at):
                return tuple(v[at] for v in pair)

            def cols_T(o, n, c, xT, nk):
                w = weights(n)
                for q in range(nk):
                    ins = mm3(o, both(w, slice(None), q, slice(c, c + P)), both(xT, slice(None), q), q == 0, q == nk - 1)
                return ins

            def unit_T(name, i, n, xT, nk=KD, c0=0):
                b = open_unit(name, i)
                for j in range(2):
                    ins = cols_T(b[:, j * T:(j + 1) * T], n, c0 + j * P, xT, nk)
                close(ins)

            def chunk_N(name, i0, n, width, xT):
                banks = [open_unit(name, i0 + t) for t in range(2)]
                steps = 2 if width == 512 else 1
                nk = KD // steps
                for h in range(steps):
                    w = weights(n + h)
                    for t in range(2):
                        for q in range(nk):
                            kt_ = h * nk + q
                            ins = mm3(banks[t][:, 0:width], both(xT, slice(None), kt_, slice(t * P, (t + 1) * P)),
                                      both(w, slice(None), q, slice(0, width)), kt_ == 0, kt_ == KD - 1)
                        if h == steps - 1:
                            close(ins)
                    if h < steps - 1:
                        ins.then_inc(s["slots_used"], 1)

            for l in range(DEPTH_2):
                turn(f"xT{l}", x3, 4, s["x1_ready"] if l == 0 else s["x_done"], 0 if l == 0 else 2)
                wait_emptied(pe, f"xT{l}")
                for i in range(9):
                    unit_T(f"qka{l}", i, half_at["qka", l] + i, hTp)
                for i in range(3):
                    chunk_N(f"va{l}", 2 * i, half_at["va", l] + 2 * i, 512 if i < 2 else 128, hTp)
                wait_emptied(pe, f"qka{l}")
                def attention(j):
                    wait_emptied(pe, f"pT{l}.{j}")
                    if j == 0:
                        wait_emptied(pe, f"va{l}")
                    b = open_unit(f"attn{l}.{j}")
                    for t in range(2):
                        terms = [(g, kt_) for g in range(NG) for kt_ in range(t + 1)]
                        for n, (g, kt_) in enumerate(terms):
                            c = (HPG * g + j) * AD
                            blk = g if t == 0 else 3 + 2 * g + kt_
                            ins = mm(b[:, t * AD:(t + 1) * AD], pT[:, blk], va[:, kt_, c:c + AD], n == 0, n == len(terms) - 1)
                    close(ins)

                for j in range(HPG):
                    def qk(h, t):
                        r = AD * (h % 2)
                        return qka[r:r + AD, h // 2, t * P:(t + 1) * P], qka[r:r + AD, 9 + h // 2]
                    b = open_unit(f"score{l}.{j}", 0)
                    for g in range(NG):
                        q_, k_ = qk(HPG * g + j, 0)
                        ins = mm(b[:, g * P:(g + 1) * P], q_, k_[:, 0:P])
                    close(ins)
                    b = open_unit(f"score{l}.{j}", 1)
                    for g in range(2):
                        q_, k_ = qk(HPG * g + j, 1)
                        ins = mm(b[:, g * T:(g + 1) * T], q_, k_)
                    close(ins)
                    b = open_unit(f"score{l}.{j}", 2)
                    q_, k_ = qk(HPG * 2 + j, 1)
                    close(mm(b[:, 0:T], q_, k_))
                    if j:
                        attention(j - 1)
                    for i in range(QKR_AT[j]):
                        unit_T(f"qkr{l}.{j}", i, half_at["qkr", l, j] + i, hTp)
                    for i in range(VR_AT[j]):
                        chunk_N(f"vr{l}.{j}", 2 * i, half_at["vr", l, j] + 2 * i, 512, hTp)
                    pe.wait_ge(s["exp_done"], HPG * l + j + 1)
                    for i in range(3):
                        b = open_unit(f"pT{l}.{j}", i)
                        for q in range(3):
                            ins = tr(b[:, q * P:(q + 1) * P], sc[:, 3 * i + q])
                        close(ins)
                attention(HPG - 1)
                wait_emptied(pe, f"attn{l}.{HPG - 1}")
                for i in range(2):
                    b = open_unit(f"yaT{l}", i)
                    for q in range(2 - i):
                        for t in range(2):
                            ins = tr(b[:, q * T + t * P:q * T + (t + 1) * P], ya[:, t, (2 * i + q) * P:(2 * i + q + 1) * P])
                    close(ins)
                pe.wait_ge(s["rot_done"], 8 * (l + 1))
                wait_emptied(pe, f"vr{l}.{HPG - 1}")

                def scores_r(h):
                    b = open_unit(f"rs{l}.{h}")
                    for kt_ in range(2):
                        o = b[:, 0:T] if kt_ == 0 else b[:, T:T + P]
                        for q in range(2):
                            ins = mm(o, qkr[:, 8 + 2 * h + q, kt_ * P:(kt_ + 1) * P], qkr[:, 2 * h + q, kt_ * P:T], q == 0, q == 1)
                    close(ins)
                scores_r(0)
                for h in range(RH):
                    if h < RH - 1:
                        scores_r(h + 1)
                    wait_emptied(pe, f"rs{l}.{h}")
                    b = open_unit(f"ro{l}.{h}", 0)
                    close(mm(b[:], pr[:, h % 2, 0:P], vr[:, 0, h * 512:(h + 1) * 512]))
                    b = open_unit(f"ro{l}.{h}", 1)
                    mm(b[:], pr[:, h % 2, P:T], vr[:, 0, h * 512:(h + 1) * 512], True, False)
                    close(mm(b[:], pr[:, h % 2, T:T + P], vr[:, 1, h * 512:(h + 1) * 512], False, True))
                for i in range(8):
                    unit_T(f"gate{l}", i, half_at["gate", l] + i, hTp)
                for c in range(8):
                    unit_T(f"gr{l}.{c}", 0, half_at["gr", l] + c, hTp)
                    pe.wait_ge(s["yr_ready"], RH * l + c // 2 + 1)
                    b = open_unit(f"yrT{l}.{c}")
                    for q in range(2):
                        for t in range(2):
                            ins = tr(b[:, q * T + t * P:q * T + (t + 1) * P], yr[:, t, (2 * c + q) * P:(2 * c + q + 1) * P])
                    close(ins)
                wait_emptied(pe, f"yaT{l}")
                for i in range(4):
                    unit_T(f"mixA{l}", i, half_at["mixA", l] + i // 2, yaTp, 3, 256 * (i % 2))
                pe.wait_ge(s["prod_split"], SPLITS * l + 8)
                for i in range(4):
                    b = open_unit(f"mixB{l}", i)
                    for j in range(2):
                        ins = cols_T(b[:, j * T:(j + 1) * T], half_at["mixB", l] + 2 * i + j, 0, ybTp, 16)
                        if j == 0:
                            ins.then_inc(s["slots_used"], 1)
                    close(ins)
                pe.wait_ge(s["prod_split"], SPLITS * l + 12)
                for i in range(2):
                    chunk_N(f"mixo{l}", 2 * i, half_at["mixo", l] + 2 * i, 512, mergedp)
                turn(f"x2T{l}", x3, 4, s["x_done"], 4 * l)
                wait_emptied(pe, f"x2T{l}")
                for i in range(NF // 2):
                    unit_T(f"ffg{l}.{i}", 0, half_at["ff", l] + 2 * i, hTp)
                    unit_T(f"ffu{l}.{i}", 0, half_at["ff", l] + 2 * i + 1, hTp)
                pe.wait_ge(s["prod_split"], SPLITS * (l + 1))
                banks = [open_unit(f"down{l}", i) for i in range(4)]
                for i in range(NF // 2):
                    w = weights(half_at["down", l] + i)
                    last = i == NF // 2 - 1
                    for u in range(4):
                        c, t = divmod(u, 2)
                        for q in range(2):
                            kt_ = 2 * i + q
                            ins = mm3(banks[u][:], both(hFp, slice(None), kt_, slice(t * P, (t + 1) * P)),
                                      both(w, slice(None), q, slice(512 * c, 512 * c + 512)), kt_ == 0, kt_ == NF - 1)
                        if last:
                            close(ins)
                    if not last:
                        ins.then_inc(s["slots_used"], 1)


def constants():
    f = np.float32
    k = {}
    k["ident"] = np.eye(P, dtype=f)
    n = np.arange(T, dtype=np.float64)
    ang = 2 * np.pi * np.outer(n, n) / NFFT
    cs = np.stack([np.cos(ang), np.sin(ang)])
    k["dft"] = cs.reshape(2, 2, P, T).transpose(2, 0, 1, 3).reshape(P, -1).astype(f)
    w = np.full(T, 2.0 / NFFT)
    w[0] = 1.0 / NFFT
    k["dftw"] = w.reshape(2, P).T.astype(f)
    tt = np.linspace(0.0, 1.0, T, dtype=f)[:, None]
    bands = np.linspace(1e-4, 15, 16, dtype=f)[None, :]
    an = f(2.0 * np.pi / T) * np.arange(T, dtype=f)[:, None] * bands
    k["emb"] = np.concatenate([tt, np.cos(an), np.sin(an)], axis=1).T.astype(f)
    lo, hi = np.log(1e-2) / 1.5, np.log(1e-2) / 0.3
    deltas = np.abs(np.linspace(lo, hi, HYC, dtype=f))
    win = np.exp(-tt * deltas).astype(f)
    win = np.stack([win, win])
    win[1, 0] = 0.0
    k["win"] = win.reshape(2, 2, P, HYC).transpose(2, 0, 1, 3).reshape(P, -1).copy()
    sidx, tidx = np.arange(T)[:, None], np.arange(T)[None, :]
    tri = np.stack([sidx <= tidx, sidx >= tidx]).astype(f)
    k["tri"] = tri.reshape(2, 2, P, T).transpose(2, 0, 1, 3).reshape(P, -1).copy()
    sel = np.zeros((4, 4, P), f)
    for h in range(4):
        sel[h, h] = 1.0
    k["sel4"] = sel.reshape(4, -1)
    ss = np.zeros((P, 2), f)
    for g in range(4):
        ss[32 * g, 0] = ss[32 * g + 1, 1] = 1.0
    k["selsum"] = ss
    dist = 255 - np.arange(384)
    big = np.maximum(dist, 16)
    large = 16 + (np.log(big / 16) / np.log(2048 / 16) * 16).astype(np.int32)
    bucket = np.where(dist < 16, np.maximum(dist, 0), np.minimum(large, 31))
    oh = np.zeros((32, 384), f)
    oh[bucket, np.arange(384)] = (dist >= 0)
    k["onehot"] = oh
    dm = np.zeros((AH, 384), f)
    for gi, (window, dil) in enumerate(((128, 1), (512, 4), (2048, 16))):
        ok = (dist >= 0) & (dist <= window) & (dist % dil == 0)
        dm[gi * HPG:(gi + 1) * HPG] = np.where(ok, 0.0, NEG)
    k["distmask"] = dm
    k["ltmask"] = (np.arange(T)[None, :] < np.arange(T)[:, None]).astype(f).reshape(2, P, T).transpose(1, 0, 2).reshape(P, -1).copy()
    k["iota"] = np.tile(np.arange(CAP, dtype=f), (P, 1))
    log_g = np.log(1.0 - 2.0 ** (-5.0 - np.arange(RH)))
    dk = 256
    dec = np.where(tidx >= sidx, np.exp(log_g[:, None, None] * np.maximum(tidx - sidx, 0)), 0.0) * dk ** -0.5
    dec = np.concatenate([dec[:, 0:P, :], dec[:, P:, P:]], axis=2)
    k["decay"] = dec.transpose(1, 0, 2).reshape(P, -1).astype(f)
    inv = f(10000.0) ** (-np.arange(P, dtype=f) / f(P))
    rang = np.arange(T, dtype=f)[None, :] * inv[:, None].astype(f)
    k["rope"] = np.concatenate([np.cos(rang), np.sin(rang)], axis=1).astype(f)
    return k


_INS = """x c ctx c_ctx w_ada b_ada norm_mix_g norm_ffn_g w_in b_in hy_conv hy_f_w1 hy_f_b1 hy_f_w2 hy_f_b2
    hy_f_w3 hy_skip ml_conv ml_norm_g w_branch_hy w_branch_ml w_out w_router w_exp1 w_exp3 w_exp2 final_norm_g
    rel_bias_2 w_in_2 b_in_2 w_attn_proj_2 w_ret_proj_2 w_out_2 ln1_g_2 ln1_b_2 w_ffn_gate_2 w_ffn_up_2
    w_ffn_down_2 ln2_g_2 ln2_b_2""".split()


def kernel(**inputs):
    import concourse.bacc as bacc
    from concourse.bass_utils import run_bass_kernel_spmd

    nc = bacc.Bacc("TRN2", target_bir_lowering=False, num_devices=1)
    arrays, a, k = {}, {}, {}
    for name in _INS:
        v = np.ascontiguousarray(inputs[name])
        arrays[name] = v
        a[name] = nc.dram_tensor(name, v.shape, F32, kind="ExternalInput").ap()
    rows = {n: arrays[n].reshape(-1, P) for n in ("b_ada", "norm_mix_g", "norm_ffn_g", "hy_conv", "ml_conv", "ml_norm_g", "c", "c_ctx")}
    b_in, b_in_2 = arrays["b_in"][0], arrays["b_in_2"]
    packs = {
        "pack_a": np.concatenate([rows["b_ada"], rows["norm_mix_g"], rows["norm_ffn_g"], b_in[0:GATE0].reshape(-1, P),
                                  b_in[MERGE0:].reshape(-1, P)]),
        "pack_b": np.concatenate([rows[n] for n in ("hy_conv", "ml_conv", "ml_norm_g", "c", "c_ctx")]),
        "pack_c": np.stack([np.concatenate([b_in_2[l, c0:c0 + n].reshape(-1, P)
                                            for c0, n in ((QK_A, 2304), (QK_R, 2048), (G_R, 4096))]) for l in range(DEPTH_2)]),
    }
    for name, v in packs.items():
        arrays[name] = v
        a[name] = nc.dram_tensor(name, v.shape, F32, kind="ExternalInput").ap()
    for name, v in constants().items():
        arrays["const_" + name] = np.ascontiguousarray(v)
        k[name] = nc.dram_tensor("const_" + name, v.shape, F32, kind="ExternalInput").ap()
    out = nc.dram_tensor("out", (1, T, D), F32, kind="ExternalOutput").ap()
    kernel_program(nc, a, k, out)
    r = run_bass_kernel_spmd(nc, [arrays], core_ids=[0])
    return r.results[0]["out"]
```
